# Optimizing a Trainium2 kernel written in Bass

```python
import math
import jax, jax.numpy as jnp
from jax import lax
import numpy as np

D_MODEL = 1024
BATCH = 1
SEQ = 512
DEPTH = 2

ATT_HEADS = 8
ATT_KV_HEADS = 2
HEAD_DIM = 64
WINDOW = 128
ROT_DIM = HEAD_DIM // 4
ROPE_THETA = 500000.0
SGU_GROUPS = 8
SGU_GROUP_DIM = 64
CHUNK = 128
CONV_WIDTH = 3
CONV_DIM = D_MODEL
D_FF = 2816
PLE_DIM = 256

N_EVEN = (DEPTH + 1) // 2
N_ODD = DEPTH // 2
ALPHA = (2 * DEPTH) ** 0.25
BETA = (8 * DEPTH) ** -0.25
LN_EPS = 1e-5

Q_W = ATT_HEADS * HEAD_DIM
KV_W = ATT_KV_HEADS * HEAD_DIM
SGU_W = SGU_GROUPS * SGU_GROUP_DIM
AB_IN = Q_W + 2 * KV_W + 2 * SGU_W
AB_OUT = Q_W + SGU_W

kernel_name = "hybrid_gmlp_swa_shortconv_deepnorm"

def layer_norm(x, g, b):
    xf = x.astype(jnp.float32)
    mu = jnp.mean(xf, axis=-1, keepdims=True)
    var = jnp.mean(jnp.square(xf - mu), axis=-1, keepdims=True)
    y = (xf - mu) * lax.rsqrt(var + LN_EPS)
    return (y * g.astype(jnp.float32) + b.astype(jnp.float32)).astype(x.dtype)

def swiglu(x, w_gate, w_up, w_down):
    return (jax.nn.silu(x @ w_gate) * (x @ w_up)) @ w_down

def partial_rotary(x, positions):
    half = ROT_DIM // 2
    inv = jnp.power(ROPE_THETA, -jnp.arange(half, dtype=jnp.float32) * (2.0 / ROT_DIM))
    ang = positions.astype(jnp.float32)[..., None] * inv
    cos = jnp.cos(ang)[:, :, None, :]
    sin = jnp.sin(ang)[:, :, None, :]
    xf = x.astype(jnp.float32)
    x1 = xf[..., :half]
    x2 = xf[..., half:ROT_DIM]
    rot = jnp.concatenate([x1 * cos - x2 * sin, x2 * cos + x1 * sin, xf[..., ROT_DIM:]], axis=-1)
    return rot.astype(x.dtype)

def sliding_window_sink_attention(q, k, v, sinks):
    b, s = q.shape[0], q.shape[1]
    nb = s // WINDOW
    g = ATT_HEADS // ATT_KV_HEADS
    qb = q.reshape(b, nb, WINDOW, ATT_KV_HEADS, g, HEAD_DIM)

    def band(t):
        tb = t.reshape(b, nb, WINDOW, ATT_KV_HEADS, HEAD_DIM)
        prev = jnp.pad(tb, ((0, 0), (1, 0), (0, 0), (0, 0), (0, 0)))[:, :-1]
        return jnp.concatenate([prev, tb], axis=2)

    kb, vb = band(k), band(v)
    scores = jnp.einsum('bnqhgd,bnkhd->bnhgqk', qb, kb).astype(jnp.float32) * (HEAD_DIM ** -0.5)
    qi = jnp.arange(WINDOW)[:, None]
    kj = jnp.arange(2 * WINDOW)[None, :]
    diff = qi + WINDOW - kj
    blk = jnp.arange(nb)[:, None, None]
    valid = (diff >= 0) & (diff < WINDOW) & (blk * WINDOW + kj - WINDOW >= 0)
    scores = jnp.where(valid[None, :, None, None], scores, -1e30)
    sink = jnp.broadcast_to(sinks.astype(jnp.float32).reshape(1, 1, ATT_KV_HEADS, g, 1, 1),
                            scores.shape[:-1] + (1,))
    probs = jax.nn.softmax(jnp.concatenate([scores, sink], axis=-1), axis=-1)[..., :-1]
    out = jnp.einsum('bnhgqk,bnkhd->bnqhgd', probs.astype(vb.dtype), vb)
    return out.reshape(b, s, ATT_HEADS * HEAD_DIM)

def chunked_sgu(u, v, ln_g, ln_b, w_s, b_s):
    b, s = u.shape[0], u.shape[1]
    nc = s // CHUNK
    u = jax.nn.gelu(u)
    v = layer_norm(jax.nn.gelu(v), ln_g, ln_b)
    vc = v.reshape(b, nc, CHUNK, SGU_GROUPS, SGU_GROUP_DIM)
    w = w_s * jnp.tril(jnp.ones((CHUNK, CHUNK), dtype=w_s.dtype))
    mixed = jnp.einsum('gts,bcsgd->bctgd', w, vc) + jnp.transpose(b_s)[None, None, :, :, None]
    return u * mixed.reshape(b, s, SGU_W)

def short_conv_mixer(x, w_in, conv_w, w_out):
    s = x.shape[1]
    gate_b, gate_c, z = jnp.split(x @ w_in, 3, axis=-1)
    zp = jnp.pad(gate_c * z, ((0, 0), (CONV_WIDTH - 1, 0), (0, 0)))
    y = conv_w[0] * zp[:, 0:s]
    for t in range(1, CONV_WIDTH):
        y = y + conv_w[t] * zp[:, t:t + s]
    return (gate_b * y) @ w_out

def setup_inputs(seed: int = 0) -> dict:
    key = jax.random.key(seed)
    ks = jax.random.split(key, 24)
    nrm = jax.random.normal
    f32 = jnp.float32
    x = nrm(ks[0], (BATCH, SEQ, D_MODEL), f32)
    p = nrm(ks[1], (DEPTH, BATCH, SEQ, PLE_DIM), f32)
    offset = jax.random.randint(ks[2], (BATCH, 1), 0, 4096, dtype=jnp.int32)
    positions = offset + jnp.arange(SEQ, dtype=jnp.int32)[None, :]
    ln_g = 1.0 + 0.02 * nrm(ks[3], (DEPTH, 3, D_MODEL), f32)
    ln_b = 0.02 * nrm(ks[4], (DEPTH, 3, D_MODEL), f32)
    ffn_w_gate = nrm(ks[5], (DEPTH, 2, D_MODEL, D_FF), f32) * D_MODEL ** -0.5
    ffn_w_up = nrm(ks[6], (DEPTH, 2, D_MODEL, D_FF), f32) * D_MODEL ** -0.5
    ffn_w_down = nrm(ks[7], (DEPTH, 2, D_FF, D_MODEL), f32) * (D_FF ** -0.5 * BETA)
    ab_w_in = nrm(ks[8], (N_EVEN, D_MODEL, AB_IN), f32) * D_MODEL ** -0.5
    ab_sinks = nrm(ks[9], (N_EVEN, ATT_HEADS), f32)
    sgu_ln_g = 1.0 + 0.02 * nrm(ks[10], (N_EVEN, SGU_W), f32)
    sgu_ln_b = 0.02 * nrm(ks[11], (N_EVEN, SGU_W), f32)
    sgu_w_s = nrm(ks[12], (N_EVEN, SGU_GROUPS, CHUNK, CHUNK), f32) * CHUNK ** -0.5
    sgu_b_s = 1.0 + 0.1 * nrm(ks[13], (N_EVEN, SGU_GROUPS, CHUNK), f32)
    ab_w_out = nrm(ks[14], (N_EVEN, AB_OUT, D_MODEL), f32) * (AB_OUT ** -0.5 * BETA)
    sc_w_in = nrm(ks[15], (N_ODD, D_MODEL, 3 * CONV_DIM), f32) * D_MODEL ** -0.5
    sc_conv_w = nrm(ks[16], (N_ODD, CONV_WIDTH, CONV_DIM), f32) * CONV_WIDTH ** -0.5
    sc_w_out = nrm(ks[17], (N_ODD, CONV_DIM, D_MODEL), f32) * (CONV_DIM ** -0.5 * BETA)
    ple_w_proj = nrm(ks[18], (DEPTH, PLE_DIM, D_MODEL), f32) * PLE_DIM ** -0.5
    ple_w_gate = nrm(ks[19], (DEPTH, D_MODEL, D_MODEL), f32) * D_MODEL ** -0.5
    return {"x": x, "p": p, "positions": positions, "ln_g": ln_g, "ln_b": ln_b,
            "ffn_w_gate": ffn_w_gate, "ffn_w_up": ffn_w_up, "ffn_w_down": ffn_w_down,
            "ab_w_in": ab_w_in, "ab_sinks": ab_sinks, "sgu_ln_g": sgu_ln_g, "sgu_ln_b": sgu_ln_b,
            "sgu_w_s": sgu_w_s, "sgu_b_s": sgu_b_s, "ab_w_out": ab_w_out,
            "sc_w_in": sc_w_in, "sc_conv_w": sc_conv_w, "sc_w_out": sc_w_out,
            "ple_w_proj": ple_w_proj, "ple_w_gate": ple_w_gate}

def reference(x, p, positions, ln_g, ln_b, ffn_w_gate, ffn_w_up, ffn_w_down,
              ab_w_in, ab_sinks, sgu_ln_g, sgu_ln_b, sgu_w_s, sgu_b_s, ab_w_out,
              sc_w_in, sc_conv_w, sc_w_out, ple_w_proj, ple_w_gate):
    b, s = x.shape[0], x.shape[1]
    g = ATT_HEADS // ATT_KV_HEADS
    splits = [Q_W, Q_W + KV_W, Q_W + 2 * KV_W, Q_W + 2 * KV_W + SGU_W]
    for i in range(DEPTH):
        ff1 = swiglu(x, ffn_w_gate[i, 0], ffn_w_up[i, 0], ffn_w_down[i, 0])
        x = layer_norm(ALPHA * x + 0.5 * ff1, ln_g[i, 0], ln_b[i, 0])
        j = i // 2
        if i % 2 == 0:
            h = x @ ab_w_in[j]
            q, k, v, su, sv = jnp.split(h, splits, axis=-1)
            q = partial_rotary(q.reshape(b, s, ATT_HEADS, HEAD_DIM), positions)
            q = q.reshape(b, s, ATT_KV_HEADS, g, HEAD_DIM)
            k = partial_rotary(k.reshape(b, s, ATT_KV_HEADS, HEAD_DIM), positions)
            v = v.reshape(b, s, ATT_KV_HEADS, HEAD_DIM)
            att = sliding_window_sink_attention(q, k, v, ab_sinks[j])
            sgu = chunked_sgu(su, sv, sgu_ln_g[j], sgu_ln_b[j], sgu_w_s[j], sgu_b_s[j])
            mix = jnp.concatenate([att, sgu], axis=-1) @ ab_w_out[j]
        else:
            mix = short_conv_mixer(x, sc_w_in[j], sc_conv_w[j], sc_w_out[j])
        x = layer_norm(ALPHA * x + mix, ln_g[i, 1], ln_b[i, 1])
        ff2 = swiglu(x, ffn_w_gate[i, 1], ffn_w_up[i, 1], ffn_w_down[i, 1])
        x = layer_norm(ALPHA * x + 0.5 * ff2, ln_g[i, 2], ln_b[i, 2])
        x = x + (p[i] @ ple_w_proj[i]) * jax.nn.sigmoid(x @ ple_w_gate[i])
    return x


_drawn_inputs = setup_inputs


def setup_inputs(seed=0):
    import zlib

    import numpy as np

    out = dict(_drawn_inputs(seed))
    spreads = {}
    factors = {'ab_sinks': 8.0, 'sgu_ln_g': 8.0, 'sgu_ln_b': 8.0, 'sgu_b_s': 3.789}
    for name, (base, spread) in spreads.items():
        noise = np.random.default_rng([zlib.crc32(name.encode()), seed]).standard_normal(out[name].shape)
        drawn = base * np.exp(spread * noise) if base else spread * noise
        out[name] = __import__('jax').numpy.asarray(drawn.astype(out[name].dtype))
    for name, factor in factors.items():
        out[name] = (out[name] * factor).astype(out[name].dtype)
    return out
```

```python
from contextlib import ExitStack

import concourse.bass as bass
import numpy as np
from concourse import mybir

F32 = mybir.dt.float32
F32R = mybir.dt.float32r
I32 = mybir.dt.int32
ALU = mybir.AluOpType
ACT = mybir.ActivationFunctionType
AX = mybir.AxisListType

P = 128
T = 512
D = 1024
DT = D // P
DEPTH = 2
D_FF = 2816
FT = D_FF // P
FT_GROUPS = (8, 8, 6)
PLE_T = 256 // P
RING = 4
SLAB = 8 * P
HEADS, KV_HEADS, HEAD_DIM = 8, 2, 64
QT = HEADS * HEAD_DIM // P
BLOCKS = T // P
UNITS = BLOCKS * QT
ROT_HALF = 8
ROPE_THETA = 500000.0
ALPHA = (2 * DEPTH) ** 0.25
LN_EPS = 1e-5
MASKED = 1e30
MAGIC = 1.5 * 2.0 ** 23
TWO_PI = 2 * np.pi


def plan_slabs():
    first, aux_only, n = {}, set(), 0
    for layer in range(DEPTH):
        for half in range(2):
            for g, ft in enumerate(FT_GROUPS):
                first["up", layer, half, g] = n
                n += 2 * ft
                first["down", layer, half, g] = n
                n += DT
            if half == 0:
                first["mix", layer] = n
                n += (2 * QT + 2 + 4 if layer == 0 else 3 * DT)
                first["mix_out", layer] = n
                n += DT
        first["ple_proj", layer] = n
        aux_only |= {n, n + 1}
        n += 2
        first["ple_gate", layer] = n
        n += DT
    return first, aux_only, n


def split_two_pi():
    c1 = float(np.floor(TWO_PI * 2.0 ** 9) / 2.0 ** 9)
    rest = TWO_PI - c1
    scale = 2.0 ** (11 - np.floor(np.log2(rest)))
    c2 = float(np.floor(rest * scale) / scale)
    return c1, c2, float(TWO_PI - c1 - c2)


def build_program(nc, xT, pT, positions, ln_gb, w_up, w_down8, w_down6, w_mix0, w_mix1, w_ple,
                  sinks, sgu_gb, sgu_wT, sgu_b, conv_w, consts, outT):
    FIRST, AUX_ONLY, N_SLABS = plan_slabs()

    def uses(n):
        return sum(1 for m in range(n % RING, n, RING) if m not in AUX_ONLY)

    ctx = ExitStack()
    with ctx:
        def sb(name, shape, dt=F32):
            return ctx.enter_context(nc.sbuf_tensor(name, shape, dt))

        def sem(name):
            return ctx.enter_context(nc.semaphore(name))

        raw = sb("raw", [P, RING, SLAB])
        w_hi = sb("w_hi", [P, RING, SLAB], F32R)
        w_lo = sb("w_lo", [P, RING, SLAB], F32R)
        xf = sb("xf", [P, DT * T])
        a_hi, a_lo = sb("a_hi", [P, DT * T], F32R), sb("a_lo", [P, DT * T], F32R)
        b_hi, b_lo = sb("b_hi", [P, DT * T], F32R), sb("b_lo", [P, DT * T], F32R)
        p_hi, p_lo = sb("p_hi", [P, PLE_T * T], F32R), sb("p_lo", [P, PLE_T * T], F32R)
        gate = sb("gate", [P, 2, T])
        inner = sb("inner", [P, 2, T])
        sum_z, sum_q = sb("sum_z", [P, T]), sb("sum_q", [P, T])
        square = sb("square", [P, 2, T])
        temp = sb("temp", [P, 2, T])
        ident_rot = sb("ident_rot", [P, 2 * P + 2])
        ident, rotT, inv_freq = ident_rot[:, 0:P], ident_rot[:, P:2 * P], ident_rot[:, 2 * P:2 * P + 1]
        ones = sb("ones", [P, P])
        mean_col = sb("mean_col", [P, 2])
        eps = sb("eps", [P, 4])
        gb = sb("gb", [P, 2 * 3 * DEPTH * DT])
        small = sb("small", [P, 32])
        warm_tile = sb("warm_tile", [P, 1])
        nsink = sb("nsink", [P, HEADS])
        conv_taps = sb("conv_taps", [P, 3 * DT])
        taps = sb("taps", [P, 2, 3])
        stats6 = sb("stats6", [P, BLOCKS, 6])
        stats2 = sb("stats2", [P, BLOCKS, 2])
        sgu_std = sb("sgu_std", [P, BLOCKS])
        sgu_rstd = sb("sgu_rstd", [P, BLOCKS])
        sm = sb("sm", [P, 2, 12])

        scratch = sb("scratch", [P, 14080])
        at = 0

        def carve(cols):
            nonlocal at
            at += cols
            return scratch[:, at - cols:at]

        q = carve(QT * T)
        kz = carve(KV_HEADS * T)
        vz = carve(KV_HEADS * BLOCKS * P)
        u_act = carve(4 * T)
        v_act = carve(BLOCKS * T)
        probs = carve(2 * T)
        probsT = carve(2 * T)
        cos, sin = carve(T), carve(T)
        spatial = carve(8 * P)
        mask = carve(2 * P)
        spatial_bias = carve(4 * P)
        sgu_gain, sgu_bias = carve(T), carve(T)
        ple = scratch[:, 0:DT * T]
        p_raw = scratch[:, 0:PLE_T * T]
        conv_y = scratch[:, 0:DT * T]
        zpad = scratch[:, DT * T:DT * T + 2 * (T + 2)]

        bank = [ctx.enter_context(nc.psum_tensor(f"bank{b}", [P, T], F32)) for b in range(8)]

        loaded = [sem(f"loaded{s}") for s in range(RING)]
        const_loaded = sem("const_loaded")
        x_loaded = sem("x_loaded")
        p_loaded = sem("p_loaded")
        hi_ready, lo_ready, slab_done = sem("hi_ready"), sem("lo_ready"), sem("slab_done")
        bank_read = [sem(f"bank_read{b}") for b in range(RING)]
        h_hi_ready, h_lo_ready = sem("h_hi_ready"), sem("h_lo_ready")
        x_hi_ready, x_lo_ready = sem("x_hi_ready"), sem("x_lo_ready")
        p_hi_ready, p_lo_ready = sem("p_hi_ready"), sem("p_lo_ready")
        const_ready = sem("const_ready")
        pool_chain, dve_chain, act_chain = sem("pool_chain"), sem("dve_chain"), sem("act_chain")
        square_ready, sums_ready, stats_ready = sem("square_ready"), sem("sums_ready"), sem("stats_ready")
        var_ready, std_ready, diag_ready = sem("var_ready"), sem("std_ready"), sem("diag_ready")
        spread_ready, normed_ready, xf_ready = sem("spread_ready"), sem("normed_ready"), sem("xf_ready")
        ple_done, ple_read, mixed_in = sem("ple_done"), sem("ple_read"), sem("mixed_in")
        angle_ready, table_ready = sem("angle_ready"), sem("table_ready")
        rot_done, rot_ready = sem("rot_done"), sem("rot_ready")
        v_turned, vz_ready = sem("v_turned"), sem("vz_ready")
        scores_done, scores_read, max_ready, exp_ready = (
            sem("scores_done"), sem("scores_read"), sem("max_ready"), sem("exp_ready"))
        probs_ready, turned, probsT_ready, pv_done = (
            sem("probs_ready"), sem("turned"), sem("probsT_ready"), sem("pv_done"))
        gelu_v, v_var, v_std, v_scaled, v_normed = (
            sem("gelu_v"), sem("v_var"), sem("v_std"), sem("v_scaled"), sem("v_normed"))
        gelu_u, spatial_done, spatial_read, sgu_ready = (
            sem("gelu_u"), sem("spatial_done"), sem("spatial_read"), sem("sgu_ready"))
        conv_m = sem("conv_m")
        out_stored = sem("out_stored")

        def tile(buf, k):
            return buf[:, bass.ds(k * T, T)] if not isinstance(k, int) else buf[:, k * T:(k + 1) * T]

        H_BEFORE, count = {}, 0
        for layer in range(DEPTH):
            for half in range(2):
                for g, ft in enumerate(FT_GROUPS):
                    H_BEFORE[layer, half, g] = count
                    count += ft
                if half == 0:
                    H_BEFORE["mix", layer] = count
                    count += DT
        X_OF = {"load": 0, (0, 0): 1, (0, 1): 2, (0, 2): 3, "ple": 4, (1, 0): 5, (1, 1): 6, (1, 2): 7}

        block = ctx.enter_context(nc.Block())

        @block.sync
        def _(sp):
            def load(n, src, i=0):
                s = n % RING
                if n >= RING:
                    sp.wait_ge(hi_ready, n - RING + 1 + RING * i)
                    sp.wait_ge(lo_ready, n - RING + 1 + RING * i)
                sp.dma_start(raw[:, s, 0:src.shape[-1]], src).then_inc(loaded[s], 16)

            def load_run(n, slabs, src_of):
                start = 0
                if n == 0:
                    for j in range(RING):
                        load(j, src_of(j))
                    start = RING
                steps = (slabs - start) // RING
                with sp.Fori(0, steps) as i:
                    for j in range(RING):
                        load(n + start + j, src_of(i * RING + start + j), i)
                for j in range(start + steps * RING, slabs):
                    load(n + j, src_of(j))

            for layer in range(DEPTH):
                for half in range(2):
                    f = 2 * layer + half
                    for g, ft in enumerate(FT_GROUPS):
                        load_run(FIRST["up", layer, half, g], 2 * ft,
                                 lambda j, b=f * 2 * FT + 16 * g: w_up[b + j])
                        if half == 1 and g == 0:
                            sp.wait_ge(x_lo_ready, DT * (X_OF[layer, 1] + 1))
                            sp.dma_start(p_raw, pT[layer]).then_inc(p_loaded, 16)
                        if g < 2:
                            load_run(FIRST["down", layer, half, g], DT,
                                     lambda j, b=(f * 2 + g) * DT: w_down8[b + j])
                        else:
                            load_run(FIRST["down", layer, half, g], DT,
                                     lambda j, b=f * DT: w_down6[b + j])
                    if half == 0:
                        w_mix = w_mix0 if layer == 0 else w_mix1
                        load_run(FIRST["mix", layer], w_mix.shape[0], lambda j, w=w_mix: w[j])
                load_run(FIRST["ple_proj", layer], 2 + DT, lambda j, b=layer * (2 + DT): w_ple[b + j])
            for d in range(DT):
                sp.wait_ge(mixed_in, DT + d + 1)
                sp.dma_start(outT[:, d, :], tile(xf, d)).then_inc(out_stored, 16)
            sp.wait_ge(out_stored, 16 * DT)

        @block.gpsimd
        def _(pool):
            nc.gpsimd.memset(ones[:, :], 1.0).then_inc(const_ready, 1)
            nc.gpsimd.memset(mean_col[:, :], 1.0 / D).then_inc(const_ready, 1)
            nc.gpsimd.memset(eps[:, 0:1], LN_EPS).then_inc(const_ready, 1)
            nc.gpsimd.memset(eps[:, 1:2], 4 * LN_EPS).then_inc(const_ready, 1)

            def split_x(refresh, d, hi, lo):
                pool.wait_ge(x_hi_ready, DT * refresh + d + 1)
                nc.gpsimd.tensor_tensor(tile(lo, d), tile(xf, d), tile(hi, d).bitcast(F32),
                                        ALU.subtract).then_inc(x_lo_ready, 1)

            for d in range(DT):
                split_x(0, d, a_hi, a_lo)

            nc.gpsimd.memset(kz, 0.0).then_inc(const_ready, 1)
            nc.gpsimd.memset(vz, 0.0).then_inc(const_ready, 1)
            nc.gpsimd.memset(mask, 0.0).then_inc(pool_chain, 1)
            pool.wait_ge(pool_chain, 1)
            nc.gpsimd.affine_select(out=mask[:, 0:P], in_=mask[:, 0:P], compare_op=ALU.is_gt, fill=MASKED,
                                    base=0, pattern=[[1, P]], channel_multiplier=-1).then_inc(const_ready, 1)
            nc.gpsimd.affine_select(out=mask[:, P:2 * P], in_=mask[:, P:2 * P], compare_op=ALU.is_ge,
                                    fill=MASKED, base=0, pattern=[[-1, P]],
                                    channel_multiplier=1).then_inc(const_ready, 1)
            pool.wait_ge(const_loaded, 16 * 8)
            spatial3 = spatial.rearrange("p (g t) -> p g t", g=8)
            nc.gpsimd.affine_select(out=spatial3, in_=spatial3, compare_op=ALU.is_ge, fill=0.0, base=0,
                                    pattern=[[0, 8], [1, P]], channel_multiplier=-1).then_inc(const_ready, 1)

            def norm_part(layer, which, n7, hi, lo):
                norm = 3 * layer + which
                base = 12 * norm
                for d in range(1, DT - 1):
                    n = n7 - (DT - 1) + d
                    if d == 1:
                        pool.wait_ge(bank_read[(n - 1) % RING], uses(n - 1) + 1)
                    pool.wait_ge(bank_read[n % RING], uses(n) + 1)
                    first_z = tile(xf, 0) if d == 1 else sum_z[:, :]
                    first_q = square[:, 0, :] if d == 1 else sum_q[:, :]
                    if d > 1:
                        pool.wait_ge(sums_ready, base + 2 * (d - 1))
                    nc.gpsimd.tensor_tensor(sum_z[:, :], first_z, tile(xf, d), ALU.add).then_inc(sums_ready, 1)
                    pool.wait_ge(square_ready, DT * norm + d + 1)
                    nc.gpsimd.tensor_tensor(sum_q[:, :], first_q, square[:, d % 2, :],
                                            ALU.add).then_inc(sums_ready, 1)
                for d in range(DT):
                    split_x(X_OF[layer, which], d, hi, lo)

            def mixer_part():
                for tb in range(BLOCKS):
                    v = tile(v_act, tb)
                    pool.wait_ge(v_scaled, tb + 1)
                    nc.gpsimd.tensor_tensor(v, v, sgu_gain, ALU.mult).then_inc(pool_chain, 1)
                    pool.wait_ge(pool_chain, 2 + tb)
                    nc.gpsimd.tensor_tensor(v, v, sgu_bias, ALU.add).then_inc(v_normed, 1)

            for layer in range(DEPTH):
                x_hi, x_lo, o_hi, o_lo = (a_hi, a_lo, b_hi, b_lo) if layer == 0 else (b_hi, b_lo, a_hi, a_lo)
                norm_part(layer, 0, FIRST["down", layer, 0, 2] + DT - 1, x_hi, x_lo)
                if layer == 0:
                    mixer_part()
                norm_part(layer, 1, FIRST["mix_out", layer] + DT - 1, x_hi, x_lo)
                norm_part(layer, 2, FIRST["down", layer, 1, 2] + DT - 1, x_hi, x_lo)
                if layer == 0:
                    for d in range(DT):
                        split_x(X_OF["ple"], d, o_hi, o_lo)

        @block.scalar
        def _(act):
            for d in range(DT):
                act.dma_start(tile(xf, d), xT[:, d, :]).then_inc(x_loaded, 16)
                act.wait_ge(x_loaded, 16 * (d + 1))
            act.dma_start(ident_rot[:, :], consts).then_inc(const_loaded, 16)
            act.dma_start(gb[:, :], ln_gb).then_inc(const_loaded, 16)
            act.dma_start(spatial, sgu_wT).then_inc(const_loaded, 16)
            act.dma_start(spatial_bias, sgu_b).then_inc(const_loaded, 16)
            act.dma_start(scratch[:, 14080 - 2 * T:14080], sgu_gb.broadcast_to([P, 2 * T])).then_inc(const_loaded, 16)
            act.dma_start(nsink[:, :], sinks.broadcast_to([P, HEADS])).then_inc(const_loaded, 16)
            act.dma_start(conv_taps[:, :], conv_w).then_inc(const_loaded, 16)
            act.dma_start(q[:, 0:T].bitcast(I32), positions.broadcast_to([P, T])).then_inc(const_loaded, 16)

            def warm(func):
                nc.scalar.activation(warm_tile[:, :], mean_col[:, 0:1], func)

            def refill(n, i=0):
                m = n + RING
                if m < N_SLABS:
                    act.wait_ge(loaded[m % RING], 16 * (m // RING + 1) + 16 * i)
                    nc.scalar.activation(w_hi[:, m % RING, :], raw[:, m % RING, :], ACT.Copy).then_inc(hi_ready, 1)

            for d in range(DT):
                act.wait_ge(x_loaded, 16 * (d + 1))
                nc.scalar.activation(tile(a_hi, d), tile(xf, d), ACT.Copy).then_inc(x_hi_ready, 1)
            for s in range(RING):
                act.wait_ge(loaded[s], 16)
                nc.scalar.activation(w_hi[:, s, :], raw[:, s, :], ACT.Copy).then_inc(hi_ready, 1)
            act.wait_ge(const_ready, 4)
            warm(ACT.Silu)

            def up_pair(n, jj, hc, h_tile, i=0):
                b = n % RING
                act.wait_ge(slab_done, n + 1 + RING * i)
                nc.scalar.activation(gate[:, jj, :], bank[b][:, :], ACT.Silu).then_inc(bank_read[b], 1)
                refill(n, i)
                act.wait_ge(slab_done, n + 2 + RING * i)
                refill(n + 1, i)
                act.wait_ge(bank_read[(n + 1) % RING], uses(n + 1) + 1 + i)
                nc.scalar.activation(h_tile, inner[:, jj, :], ACT.Copy).then_inc(h_hi_ready, 1)

            def ffn(layer, half, o_hi):
                for g, ft in enumerate(FT_GROUPS):
                    n = FIRST["up", layer, half, g]
                    with act.Fori(0, ft // 2) as i:
                        for jj in range(2):
                            up_pair(n + 2 * jj, jj, 0, tile(o_hi, 2 * i + jj), i)
                    if g < 2:
                        n = FIRST["down", layer, half, g]
                        with act.Fori(0, DT // RING) as i:
                            for j in range(RING):
                                act.wait_ge(slab_done, n + j + 1 + RING * i)
                                refill(n + j, i)
                    if layer == 0 and half == 0 and g == 0:
                        act.wait_ge(angle_ready, 1)
                        nc.scalar.activation(sin, temp[:, 0, :], ACT.Sin).then_inc(table_ready, 1)
                        nc.scalar.activation(cos, temp[:, 1, :], ACT.Sin).then_inc(table_ready, 1)
                        warm(ACT.Silu)
                    if half == 1 and g == 0:
                        act.wait_ge(p_loaded, 16 * (layer + 1))
                        nc.scalar.activation(p_hi[:, :], p_raw, ACT.Copy).then_inc(p_hi_ready, 1)

            def final_products(norm, n0, after_last):
                warm(ACT.Sqrt)
                for d in range(DT):
                    n = n0 + d
                    act.wait_ge(slab_done, n + 1)
                    if d < DT - 1:
                        refill(n)
                    act.wait_ge(bank_read[n % RING], uses(n) + 1)
                    if d >= 2:
                        act.wait_ge(sums_ready, 12 * norm + 2 * max(1, d - 2))
                    nc.scalar.activation(square[:, d % 2, :], tile(xf, d), ACT.Square).then_inc(square_ready, 1)
                refill(n0 + DT - 1)
                after_last()

            def normalise(layer, which, scale, hi, next_func, extra):
                norm = 3 * layer + which
                act.wait_ge(var_ready, norm + 1)
                nc.scalar.activation(small[:, 8:12], small[:, 4:8], ACT.Sqrt,
                                     bias=eps[:, scale:scale + 1]).then_inc(std_ready, 1)
                warm(next_func)
                extra(-1)
                for d in range(DT):
                    c = norm * DT + d
                    g0 = 3 * DEPTH * DT
                    act.wait_ge(normed_ready, c + 1)
                    nc.scalar.activation(tile(xf, d), temp[:, d % 2, :], ACT.Identity, scale=gb[:, c:c + 1],
                                         bias=gb[:, g0 + c:g0 + c + 1]).then_inc(xf_ready, 1)
                    act.wait_ge(xf_ready, c + 1)
                    nc.scalar.activation(tile(hi, d), tile(xf, d), ACT.Copy).then_inc(x_hi_ready, 1)
                    extra(d)

            def nothing(*_):
                pass

            def attention_mixer(o_hi):
                m0, h0 = FIRST["mix", 0], H_BEFORE["mix", 0]

                def take(n, dst, func=ACT.Copy):
                    act.wait_ge(slab_done, n + 1)
                    nc.scalar.activation(dst, bank[n % RING][:, :], func).then_inc(bank_read[n % RING], 1)

                def exps(u):
                    lo = P if u < QT else 0
                    par = u % 2
                    act.wait_ge(max_ready, u + 1)
                    for g in range(2):
                        c = slice(g * 2 * P + lo, (g + 1) * 2 * P)
                        nc.scalar.activation(tile(probs, par)[:, c], inner[:, par, c], ACT.Exp, scale=-1.0,
                                             bias=sm[:, par, 2 + g:3 + g],
                                             accum_out=sm[:, par, 6 + g:7 + g]).then_inc(act_chain, 1)
                    nc.scalar.activation(sm[:, par, 8:10], sm[:, par, 4:6], ACT.Exp).then_inc(act_chain, 1)
                    act.wait_ge(act_chain, 3 * u + 3)
                    nc.scalar.activation(warm_tile[:, :], mean_col[:, 0:1], ACT.Copy).then_inc(exp_ready, 1)

                def turned_out(u):
                    act.wait_ge(turned, u + 1)
                    if u >= 2:
                        act.wait_ge(pv_done, u - 1)
                    lo = P if u < QT else 0
                    src = bank[6][:, :].rearrange("p (g k) -> p g k", g=2)[:, :, lo:]
                    dst = tile(probsT, u % 2).rearrange("p (g k) -> p g k", g=2)[:, :, lo:]
                    nc.scalar.activation(dst, src, ACT.Copy).then_inc(probsT_ready, 1)

                def att_out(n):
                    act.wait_ge(pv_done, QT * (n + 1))
                    dst = o_hi[:, 0:QT * T].rearrange("p (j t) -> p j t", j=QT)[:, :, n * P:(n + 1) * P]
                    src = bank[7][:, :].rearrange("p (j t) -> p j t", j=QT)
                    nc.scalar.activation(dst, src, ACT.Copy).then_inc(h_hi_ready, 1)

                for j in range(QT):
                    take(m0 + j, tile(q, j))
                    refill(m0 + j)
                take(m0 + 4, square[:, 0, :])
                refill(m0 + 4)
                take(m0 + 5, gate[:, 0, :])
                refill(m0 + 5)
                act.wait_ge(v_turned, 1)
                act.wait_ge(const_ready, 6)
                vz4 = vz.rearrange("p (g n c) -> p g n c", g=2, n=BLOCKS)
                src = bank[6][:, :].rearrange("p (n c) -> p n c", n=BLOCKS)
                for g in range(2):
                    c = slice(g * HEAD_DIM, (g + 1) * HEAD_DIM)
                    nc.scalar.activation(vz4[:, g, :, c], src[:, :, c], ACT.Copy).then_inc(vz_ready, 1)
                for w in range(UNITS // 2 + 2):
                    if w < 8:
                        n = m0 + 6 + w
                        act.wait_ge(slab_done, n + 1)
                        if w == 3:
                            for tb in range(BLOCKS):
                                b = (m0 + 6 + tb) % RING
                                nc.scalar.activation(tile(v_act, tb), bank[b][:, :],
                                                     ACT.Gelu_apprx_tanh).then_inc(bank_read[b], 1)
                        if w >= 4:
                            take(n, tile(u_act, w - 4))
                        refill(n)
                        if w == 5:
                            act.wait_ge(v_var, 1)
                            nc.scalar.activation(sgu_std[:, :], stats2[:, :, 1], ACT.Sqrt,
                                                 bias=eps[:, 0:1]).then_inc(v_std, 1)
                    for u in (2 * w, 2 * w + 1):
                        if 2 <= u < UNITS + 2:
                            turned_out(u - 2)
                        if u < UNITS:
                            exps(u)
                    if w >= 3 and w % 2 == 1:
                        att_out((w - 3) // 2)
                for j in range(4):
                    act.wait_ge(bank_read[(m0 + 10 + j) % RING], uses(m0 + 10 + j) + 1)
                    nc.scalar.activation(tile(u_act, j), tile(u_act, j), ACT.Gelu_apprx_tanh).then_inc(gelu_u, 1)
                for j in range(4):
                    act.wait_ge(sgu_ready, j + 1)
                    nc.scalar.activation(tile(o_hi, QT + j), inner[:, j % 2, :], ACT.Copy).then_inc(h_hi_ready, 1)

            def conv_mixer(o_hi):
                m0 = FIRST["mix", 1]

                def gate_and_z(n, i=0):
                    for jj in range(2):
                        g = n + 2 * jj
                        act.wait_ge(slab_done, g + 1 + RING * i)
                        act.wait_ge(bank_read[(g + 1) % RING], uses(g + 1) + i)
                        nc.scalar.activation(gate[:, jj, :], bank[g % RING][:, :],
                                             ACT.Copy).then_inc(bank_read[g % RING], 1)
                        refill(g, i)
                        act.wait_ge(slab_done, g + 2 + RING * i)
                        refill(g + 1, i)

                with act.Fori(0, DT // 2) as i:
                    gate_and_z(m0, i)
                n = m0 + 2 * DT
                with act.Fori(0, DT // RING) as i:
                    for j in range(RING):
                        act.wait_ge(slab_done, n + j + 1 + RING * i)
                        refill(n + j, i)
                        act.wait_ge(bank_read[(n + j) % RING], uses(n + j) + 1 + i)
                        nc.scalar.activation(tile(o_hi, RING * i + j), inner[:, j % 2, :],
                                             ACT.Copy).then_inc(h_hi_ready, 1)

            def ple_step(layer):
                pp0 = FIRST["ple_proj", layer]

                def take(p):
                    if p % 4 == 3:
                        act.wait_ge(slab_done, pp0 + p // 4 + 1)
                    else:
                        act.wait_ge(ple_done, 6 * layer + 3 * (p // 4) + p % 4 + 1)
                    nc.scalar.activation(tile(ple, p), bank[4 + p % 2][:, :], ACT.Copy).then_inc(ple_read, 1)

                def after_last():
                    for p in range(4):
                        take(p)
                    refill(pp0)

                def extra(d):
                    if d == -1:
                        take(4)
                        take(5)
                    if d == 0:
                        take(6)
                    if d == 1:
                        take(7)
                    if d == 2:
                        refill(pp0 + 1)
                return after_last, extra

            def ple_gates(layer, o_hi):
                n0 = FIRST["ple_gate", layer]
                for d in range(DT):
                    n = n0 + d
                    act.wait_ge(slab_done, n + 1)
                    if d >= 2:
                        act.wait_ge(mixed_in, DT * layer + d - 1)
                    nc.scalar.activation(gate[:, d % 2, :], bank[n % RING][:, :],
                                         ACT.Sigmoid).then_inc(bank_read[n % RING], 1)
                    if d == DT - 1:
                        warm(ACT.Silu)
                    refill(n)
                    if layer == 0:
                        act.wait_ge(mixed_in, DT * layer + d + 1)
                        nc.scalar.activation(tile(o_hi, d), tile(xf, d), ACT.Copy).then_inc(x_hi_ready, 1)

            for layer in range(DEPTH):
                x_hi, o_hi = (a_hi, b_hi) if layer == 0 else (b_hi, a_hi)
                ffn(layer, 0, o_hi)
                final_products(3 * layer, FIRST["down", layer, 0, 2], nothing)
                normalise(layer, 0, 1, x_hi, ACT.Exp if layer == 0 else ACT.Copy, nothing)
                if layer == 0:
                    attention_mixer(o_hi)
                else:
                    conv_mixer(o_hi)
                final_products(3 * layer + 1, FIRST["mix_out", layer], nothing)
                normalise(layer, 1, 0, x_hi, ACT.Silu, nothing)
                ffn(layer, 1, o_hi)
                after_last, extra = ple_step(layer)
                final_products(3 * layer + 2, FIRST["down", layer, 1, 2], after_last)
                normalise(layer, 2, 1, x_hi, ACT.Sigmoid, extra)
                ple_gates(layer, o_hi)

        @block.vector
        def _(dve):
            chain = [0]

            def link(ins):
                chain[0] += 1
                ins.then_inc(dve_chain, 1)
                dve.wait_ge(dve_chain, chain[0])

            def refill(n, i=0):
                m = n + RING
                if m < N_SLABS:
                    dve.wait_ge(hi_ready, m + 1 + RING * i)
                    nc.vector.tensor_tensor(w_lo[:, m % RING, :], raw[:, m % RING, :],
                                            w_hi[:, m % RING, :].bitcast(F32), ALU.subtract).then_inc(lo_ready, 1)

            for s in range(RING):
                refill(s - RING)

            def up_pair(n, jj, hc, o_hi, o_lo, k, i=0):
                refill(n, i)
                dve.wait_ge(bank_read[n % RING], uses(n) + 1 + i)
                dve.wait_ge(slab_done, n + 2 + RING * i)
                b = (n + 1) % RING
                nc.vector.tensor_tensor(inner[:, jj, :], gate[:, jj, :], bank[b][:, :],
                                        ALU.mult).then_inc(bank_read[b], 1)
                refill(n + 1, i)
                dve.wait_ge(h_hi_ready, hc + 1 + 2 * i)
                nc.vector.tensor_tensor(tile(o_lo, k), inner[:, jj, :], tile(o_hi, k).bitcast(F32),
                                        ALU.subtract).then_inc(h_lo_ready, 1)

            def add_product(n, z, first, scale, i=0):
                b = n % RING
                dve.wait_ge(slab_done, n + 1 + RING * i)
                if first:
                    nc.vector.scalar_tensor_tensor(out=z, in0=z, scalar=scale, in1=bank[b][:, :],
                                                   op0=ALU.mult, op1=ALU.add).then_inc(bank_read[b], 1)
                else:
                    nc.vector.tensor_tensor(z, z, bank[b][:, :], ALU.add).then_inc(bank_read[b], 1)

            def angles():
                c1, c2, c3 = split_two_pi()
                dve.wait_ge(const_loaded, 16 * 8)
                ang, turns, high, low = temp[:, 0, :], temp[:, 1, :], square[:, 0, :], square[:, 1, :]
                link(nc.vector.tensor_copy(ang, q[:, 0:T].bitcast(I32)))
                link(nc.vector.tensor_scalar(ang, ang, inv_freq, None, ALU.mult))
                link(nc.vector.tensor_scalar(turns, ang, 1 / TWO_PI, None, ALU.mult))
                link(nc.vector.tensor_scalar(turns, turns, MAGIC, None, ALU.add))
                link(nc.vector.tensor_scalar(turns, turns, MAGIC, None, ALU.subtract))
                link(nc.vector.tensor_scalar(high, turns, MAGIC * 4096, None, ALU.add))
                link(nc.vector.tensor_scalar(high, high, MAGIC * 4096, None, ALU.subtract))
                link(nc.vector.tensor_tensor(low, turns, high, ALU.subtract))
                for part, c in ((high, c1), (low, c1), (high, c2), (low, c2), (turns, c3)):
                    link(nc.vector.scalar_tensor_tensor(out=ang, in0=part, scalar=-c, in1=ang,
                                                        op0=ALU.mult, op1=ALU.add))
                link(nc.vector.tensor_scalar(ang, ang, float(np.float32(3.1415925)), -float(np.float32(3.1415925)),
                                             ALU.min, ALU.max))
                link(nc.vector.scalar_tensor_tensor(out=turns, in0=ang, scalar=-1.0, in1=ang,
                                                    op0=ALU.mult, op1=ALU.max))
                nc.vector.tensor_scalar(turns, turns, -1.0, float(np.pi / 2), ALU.mult, ALU.add).then_inc(angle_ready, 1)

            def ffn(layer, half, o_hi, o_lo):
                for g, ft in enumerate(FT_GROUPS):
                    n, h = FIRST["up", layer, half, g], H_BEFORE[layer, half, g]
                    with dve.Fori(0, ft // 2) as i:
                        for jj in range(2):
                            up_pair(n + 2 * jj, jj, h + jj, o_hi, o_lo, 2 * i + jj, i)
                    if g < 2:
                        n = FIRST["down", layer, half, g]
                        with dve.Fori(0, DT // RING) as i:
                            for j in range(RING):
                                add_product(n + j, tile(xf, RING * i + j), g == 0, 2 * ALPHA, i)
                                refill(n + j, i)
                    if layer == 0 and half == 0 and g == 0:
                        angles()
                    if half == 1 and g == 0:
                        dve.wait_ge(p_hi_ready, layer + 1)
                        nc.vector.tensor_tensor(p_lo[:, :], p_raw, p_hi[:, :].bitcast(F32),
                                                ALU.subtract).then_inc(p_lo_ready, 1)

            def final_products(n0, first, scale):
                for d in range(DT):
                    add_product(n0 + d, tile(xf, d), first, scale)
                    if d < DT - 1:
                        refill(n0 + d)

            def normalise(layer, which, n7):
                norm = 3 * layer + which
                mean, meansq = bank[7][:, 0:4], bank[7][:, 4:8]
                dve.wait_ge(stats_ready, norm + 1)
                link(nc.vector.tensor_copy(small[:, 0:8], bank[7][:, 0:8]))
                link(nc.vector.tensor_tensor(small[:, 12:16], small[:, 0:4], small[:, 0:4], ALU.mult))
                nc.vector.tensor_tensor(small[:, 4:8], small[:, 4:8], small[:, 12:16],
                                        ALU.subtract).then_inc(var_ready, 1)
                dve.wait_ge(std_ready, norm + 1)
                link(nc.vector.reciprocal(small[:, 16:20], small[:, 8:12]))

                def spread(dst, col):
                    nc.vector.tensor_tensor(
                        dst.rearrange("p (b t) -> p b t", b=BLOCKS),
                        ident.unsqueeze(1).broadcast_to([P, BLOCKS, P]),
                        small[:, col:col + 4].unsqueeze(2).broadcast_to([P, BLOCKS, P]),
                        ALU.mult).then_inc(diag_ready, 1)

                spread(square[:, 0, :], 16)
                link(nc.vector.scalar_tensor_tensor(out=small[:, 20:24], in0=small[:, 0:4], scalar=-1.0,
                                                    in1=small[:, 16:20], op0=ALU.mult, op1=ALU.mult))
                spread(square[:, 1, :], 20)
                for d in range(DT):
                    t = temp[:, d % 2, :]
                    if d == 0:
                        dve.wait_ge(spread_ready, 2 * norm + 1)
                    if d >= 2:
                        dve.wait_ge(xf_ready, norm * DT + d - 1)
                    link(nc.vector.tensor_tensor(t, tile(xf, d), bank[6][:, :], ALU.mult))
                    if d == 0:
                        dve.wait_ge(spread_ready, 2 * norm + 2)
                    nc.vector.tensor_tensor(t, t, bank[7][:, :], ALU.add).then_inc(normed_ready, 1)
                    if d == 1:
                        refill(n7)
                        if which == 2:
                            refill(n7 + 1)
                    if d == 4 and which == 2:
                        refill(n7 + 2)

            def attention_mixer(o_hi, o_lo):
                m0, h0 = FIRST["mix", 0], H_BEFORE["mix", 0]

                def rotate(r, src):
                    b = bank[4 + r % 2]
                    if r < QT:
                        dve.wait_ge(bank_read[(m0 + r) % RING], uses(m0 + r) + 1)
                    link(nc.vector.tensor_tensor(temp[:, 0, :], src, cos, ALU.mult))
                    dve.wait_ge(rot_done, r + 1)
                    link(nc.vector.tensor_tensor(temp[:, 1, :], b[:, :], sin, ALU.mult))
                    if r < QT:
                        nc.vector.tensor_tensor(src, temp[:, 0, :], temp[:, 1, :], ALU.add).then_inc(rot_ready, 1)
                        dve.wait_ge(rot_ready, r + 1)
                    else:
                        for g in range(2):
                            rows = slice(g * HEAD_DIM, (g + 1) * HEAD_DIM)
                            nc.vector.tensor_tensor(kz[rows, g * T:(g + 1) * T], temp[rows, 0, :],
                                                    temp[rows, 1, :], ALU.add).then_inc(rot_ready, 1)

                def mask_and_max(u):
                    par, j = u % 2, u % QT
                    lo = P if u < QT else 0
                    view = inner[:, par, :].rearrange("p (g k) -> p g k", g=2)[:, :, lo:]
                    src = bank[4 + par][:, :].rearrange("p (g k) -> p g k", g=2)[:, :, lo:]
                    dve.wait_ge(scores_done, u + 1)
                    nc.vector.scalar_tensor_tensor(
                        out=view, in0=src, scalar=-HEAD_DIM ** -0.5,
                        in1=mask[:, lo:2 * P].unsqueeze(1).broadcast_to([P, 2, 2 * P - lo]),
                        op0=ALU.mult, op1=ALU.add).then_inc(scores_read, 1)
                    dve.wait_ge(scores_read, u + 1)
                    link(nc.vector.tensor_reduce(sm[:, par, 0:2], view, AX.X, ALU.min))
                    ns = nsink[:, 2 * j:2 * j + 2]
                    link(nc.vector.tensor_tensor(sm[:, par, 2:4], sm[:, par, 0:2], ns, ALU.min))
                    nc.vector.tensor_tensor(sm[:, par, 4:6], sm[:, par, 2:4], ns, ALU.subtract).then_inc(max_ready, 1)

                def normalise_probs(u):
                    par = u % 2
                    lo = P if u < QT else 0
                    dve.wait_ge(exp_ready, u + 1)
                    link(nc.vector.tensor_tensor(sm[:, par, 10:12], sm[:, par, 6:8], sm[:, par, 8:10], ALU.add))
                    link(nc.vector.reciprocal(sm[:, par, 10:12], sm[:, par, 10:12]))
                    for g in range(2):
                        c = slice(g * 2 * P + lo, (g + 1) * 2 * P)
                        e = tile(probs, par)[:, c]
                        ins = nc.vector.tensor_scalar(e, e, sm[:, par, 10 + g:11 + g], None, ALU.mult)
                        if g == 0:
                            link(ins)
                    ins.then_inc(probs_ready, 1)

                def att_out(n):
                    dve.wait_ge(h_hi_ready, h0 + n + 1)
                    c = slice(n * P, (n + 1) * P)
                    hi = o_hi[:, 0:QT * T].rearrange("p (j t) -> p j t", j=QT)[:, :, c]
                    lo = o_lo[:, 0:QT * T].rearrange("p (j t) -> p j t", j=QT)[:, :, c]
                    nc.vector.tensor_tensor(lo, bank[7][:, :].rearrange("p (j t) -> p j t", j=QT),
                                            hi.bitcast(F32), ALU.subtract).then_inc(h_lo_ready, 1)

                link(nc.vector.tensor_scalar(nsink[:, :], nsink[:, :], -1.0, None, ALU.mult))
                dve.wait_ge(const_ready, 9)
                dve.wait_ge(table_ready, 2)
                for j in range(3):
                    refill(m0 + j)
                rotate(0, tile(q, 0))
                refill(m0 + 3)
                rotate(1, tile(q, 1))
                rotate(2, tile(q, 2))
                refill(m0 + 4)
                rotate(3, tile(q, 3))
                refill(m0 + 5)
                rotate(4, square[:, 0, :])
                for w in range(UNITS // 2 + 2):
                    if w < 8:
                        refill(m0 + 6 + w)
                    if w == 4:
                        for tb in range(BLOCKS):
                            b = (m0 + 6 + tb) % RING
                            dve.wait_ge(bank_read[b], uses(m0 + 6 + tb) + 1)
                            link(nc.vector.bn_stats(stats6[:, tb, :], tile(v_act, tb)))
                            ins = nc.vector.bn_aggr(stats2[:, tb, :], stats6[:, tb, :])
                            if tb < BLOCKS - 1:
                                link(ins)
                        ins.then_inc(v_var, 1)
                    if w == 5:
                        dve.wait_ge(v_std, 1)
                        link(nc.vector.reciprocal(sgu_rstd[:, :], sgu_std[:, :]))
                        for tb in range(BLOCKS):
                            v = tile(v_act, tb)
                            nc.vector.tensor_scalar(v, v, stats2[:, tb, 0:1], sgu_rstd[:, tb:tb + 1],
                                                    ALU.subtract, ALU.mult).then_inc(v_scaled, 1)
                    if w < UNITS // 2:
                        mask_and_max(2 * w)
                        mask_and_max(2 * w + 1)
                        normalise_probs(2 * w)
                        normalise_probs(2 * w + 1)
                    if w >= 3 and w % 2 == 1:
                        att_out((w - 3) // 2)
                for j in range(4):
                    for cp in range(2):
                        dve.wait_ge(spatial_done, 2 * j + cp + 1)
                        for g in range(2):
                            rows = slice(g * HEAD_DIM, (g + 1) * HEAD_DIM)
                            src = bank[4 + cp][rows, :].rearrange("p (c k) -> p c k", c=2)[:, :, g * P:(g + 1) * P]
                            dst = temp[rows, j % 2, cp * 2 * P:(cp + 1) * 2 * P].rearrange("p (c k) -> p c k", c=2)
                            bias = spatial_bias[rows, j * P:(j + 1) * P].unsqueeze(1).broadcast_to([HEAD_DIM, 2, P])
                            nc.vector.tensor_tensor(dst, src, bias, ALU.add).then_inc(spatial_read, 1)
                    dve.wait_ge(spatial_read, 4 * j + 4)
                    dve.wait_ge(gelu_u, j + 1)
                    nc.vector.tensor_tensor(inner[:, j % 2, :], temp[:, j % 2, :], tile(u_act, j),
                                            ALU.mult).then_inc(sgu_ready, 1)
                    dve.wait_ge(h_hi_ready, h0 + BLOCKS + j + 1)
                    nc.vector.tensor_tensor(tile(o_lo, QT + j), inner[:, j % 2, :], tile(o_hi, QT + j).bitcast(F32),
                                            ALU.subtract).then_inc(h_lo_ready, 1)

            def conv_mixer(o_hi, o_lo):
                m0, h0 = FIRST["mix", 1], H_BEFORE["mix", 1]
                for s in range(2):
                    link(nc.vector.memset(zpad[:, s * (T + 2):s * (T + 2) + 2], 0.0))
                base = chain[0]
                with dve.Fori(0, DT // 2) as i:
                    for jj in range(2):
                        n = m0 + 2 * jj
                        b = (n + 1) % RING
                        refill(n, i)
                        dve.wait_ge(bank_read[n % RING], uses(n) + 1 + i)
                        dve.wait_ge(slab_done, n + 2 + RING * i)
                        z0 = jj * (T + 2)
                        nc.vector.tensor_tensor(zpad[:, z0 + 2:z0 + 2 + T], gate[:, jj, :], bank[b][:, :],
                                                ALU.mult).then_inc(bank_read[b], 1)
                        refill(n + 1, i)
                        dve.wait_ge(bank_read[b], uses(n + 1) + 1 + i)
                        k = 2 * i + jj
                        y = tile(conv_y, k)
                        done = base + 4 * jj + 1 + 8 * i
                        nc.vector.tensor_copy(taps[:, jj, :], conv_taps[:, bass.ds(k * 3, 3)]).then_inc(dve_chain, 1)
                        dve.wait_ge(dve_chain, done)
                        for tap in range(3):
                            z = zpad[:, z0 + tap:z0 + tap + T]
                            wt = taps[:, jj, tap:tap + 1]
                            if tap == 0:
                                ins = nc.vector.tensor_scalar(y, z, wt, None, ALU.mult)
                            else:
                                ins = nc.vector.scalar_tensor_tensor(out=y, in0=z, scalar=wt, in1=y,
                                                                     op0=ALU.mult, op1=ALU.add)
                            ins.then_inc(dve_chain, 1)
                            dve.wait_ge(dve_chain, done + tap + 1)
                chain[0] += 4 * DT
                n = m0 + 2 * DT
                with dve.Fori(0, DT // RING) as i:
                    for j in range(RING):
                        b = (n + j) % RING
                        k = RING * i + j
                        dve.wait_ge(slab_done, n + j + 1 + RING * i)
                        nc.vector.tensor_tensor(inner[:, j % 2, :], tile(conv_y, k), bank[b][:, :],
                                                ALU.mult).then_inc(bank_read[b], 1)
                        refill(n + j, i)
                        dve.wait_ge(h_hi_ready, h0 + j + 1 + RING * i)
                        nc.vector.tensor_tensor(tile(o_lo, k), inner[:, j % 2, :], tile(o_hi, k).bitcast(F32),
                                                ALU.subtract).then_inc(h_lo_ready, 1)

            def ple_gates(layer):
                n0 = FIRST["ple_gate", layer]
                for d in range(DT):
                    n = n0 + d
                    dve.wait_ge(bank_read[n % RING], uses(n) + 1)
                    if d == 0:
                        dve.wait_ge(ple_read, DT * (layer + 1))
                    link(nc.vector.tensor_tensor(temp[:, d % 2, :], tile(ple, d), gate[:, d % 2, :], ALU.mult))
                    nc.vector.tensor_tensor(tile(xf, d), tile(xf, d), temp[:, d % 2, :],
                                            ALU.add).then_inc(mixed_in, 1)
                    refill(n)

            for layer in range(DEPTH):
                o_hi, o_lo = (b_hi, b_lo) if layer == 0 else (a_hi, a_lo)
                ffn(layer, 0, o_hi, o_lo)
                final_products(FIRST["down", layer, 0, 2], False, None)
                normalise(layer, 0, FIRST["mix", layer] - 1)
                if layer == 0:
                    attention_mixer(o_hi, o_lo)
                else:
                    conv_mixer(o_hi, o_lo)
                final_products(FIRST["mix_out", layer], True, ALPHA)
                normalise(layer, 1, FIRST["up", layer, 1, 0] - 1)
                ffn(layer, 1, o_hi, o_lo)
                final_products(FIRST["down", layer, 1, 2], False, None)
                normalise(layer, 2, FIRST["ple_proj", layer] - 1)
                ple_gates(layer)

        @block.tensor
        def _(pe):
            def three_passes(out, w0, hi0, lo0, x_hi, x_lo, start, stop):
                s, c = w0
                nc.tensor.matmul(out, w_hi[:, s, c], x_hi, start=start, stop=False)
                nc.tensor.matmul(out, w_hi[:, s, c], x_lo, start=False, stop=False)
                return nc.tensor.matmul(out, w_lo[:, s, c], x_hi, start=False, stop=stop)

            def wait_slab(n, i=0):
                pe.wait_ge(lo_ready, n + 1 + RING * i)
                if uses(n) > 0:
                    pe.wait_ge(bank_read[n % RING], uses(n) + i)

            def tile_product(n, k, tiles, hi, lo):
                return three_passes(bank[n % RING][:, :], (n % RING, slice(k * P, (k + 1) * P)), None, None,
                                    tile(hi, k), tile(lo, k), k == 0, k == tiles - 1)

            def slab(n, hi, lo, tiles=DT, i=0, ready=None):
                wait_slab(n, i)
                for k in range(tiles):
                    if ready is not None:
                        pe.wait_ge(h_lo_ready, ready(k))
                    last = tile_product(n, k, tiles, hi, lo)
                last.then_inc(slab_done, 1)

            def slabs_by_tile(n, sem_, ready, hi, lo, count=3):
                for m in range(n, n + count):
                    wait_slab(m)
                for k in range(DT):
                    pe.wait_ge(sem_, ready(k))
                    for m in range(n, n + count):
                        last = tile_product(m, k, DT, hi, lo)
                        if k == DT - 1:
                            last.then_inc(slab_done, 1)

            def ffn(layer, half, refresh, x, o):
                for g, ft in enumerate(FT_GROUPS):
                    n, h = FIRST["up", layer, half, g], H_BEFORE[layer, half, g]
                    steps = ft // 2
                    if g == 0:
                        slabs_by_tile(n, x_lo_ready, lambda k: DT * refresh + k + 1, *x)
                        slab(n + 3, *x)
                        n += RING
                        steps -= 1
                    with pe.Fori(0, steps) as i:
                        for j in range(RING):
                            slab(n + j, *x, i=i)
                    n = FIRST["down", layer, half, g]
                    with pe.Fori(0, DT // RING) as i:
                        for j in range(RING):
                            slab(n + j, *o, tiles=ft, i=i, ready=(lambda k: h + k + 1) if j == 0 else None)

            def statistics(norm, n7):
                stat = bank[7]

                def add(src, col, start, stop):
                    for tb in range(BLOCKS):
                        last = nc.tensor.matmul(stat[:, col + tb:col + tb + 1], src[:, tb * P:(tb + 1) * P],
                                                mean_col[:, 0:1], start=start and tb == 0, stop=stop,
                                                skip_group_check=True)
                    return last

                pe.wait_ge(const_ready, 4)
                pe.wait_ge(sums_ready, 12 * norm + 12)
                add(sum_z[:, :], 0, True, False)
                add(sum_q[:, :], 4, False, False)
                pe.wait_ge(bank_read[n7 % RING], uses(n7) + 1)
                add(tile(xf, DT - 1), 0, False, True)
                pe.wait_ge(square_ready, DT * (norm + 1))
                add(square[:, 1, :], 4, False, True).then_inc(stats_ready, 1)

            def spread(norm, which):
                pe.wait_ge(diag_ready, 2 * norm + which + 1)
                nc.tensor.matmul(bank[6 + which][:, :], ones[:, :], square[:, which, :], start=True,
                                 stop=True).then_inc(spread_ready, 1)

            def attention_mixer(refresh, x, o):
                m0, h0 = FIRST["mix", 0], H_BEFORE["mix", 0]
                vz4 = vz.rearrange("p (g n c) -> p g n c", g=2, n=BLOCKS)

                def rotate(r):
                    n = m0 + r
                    pe.wait_ge(bank_read[n % RING], uses(n) + 1)
                    if r >= 2:
                        pe.wait_ge(rot_ready, r - 1)
                    src = tile(q, r) if r < QT else square[:, 0, :]
                    nc.tensor.matmul(bank[4 + r % 2][:, :], rotT, src, start=True, stop=True).then_inc(rot_done, 1)

                def turn_v():
                    pe.wait_ge(bank_read[(m0 + 5) % RING], uses(m0 + 5) + 1)
                    for n in range(BLOCKS):
                        last = nc.tensor.transpose(bank[6][:, n * P:(n + 1) * P], gate[:, 0, n * P:(n + 1) * P], ident)
                    last.then_inc(v_turned, 1)

                def sgu_v_slab(r):
                    n = m0 + 6 + r
                    if r == 0:
                        for tb in range(BLOCKS):
                            pe.wait_ge(bank_read[(n + tb) % RING], uses(n + tb))
                    pe.wait_ge(lo_ready, n + 1)
                    for kk in range(2):
                        k = 2 * r + kk
                        whi = w_hi[:, n % RING, kk * T:(kk + 1) * T]
                        wlo = w_lo[:, n % RING, kk * T:(kk + 1) * T]
                        for tb in range(BLOCKS):
                            out = bank[(m0 + 6 + tb) % RING][:, :]
                            c = slice(k * T + tb * P, k * T + (tb + 1) * P)
                            nc.tensor.matmul(out, x[0][:, c], whi, start=(k == 0), stop=False)
                            nc.tensor.matmul(out, x[0][:, c], wlo, start=False, stop=False)
                            last = nc.tensor.matmul(out, x[1][:, c], whi, start=False, stop=(k == DT - 1))
                    last.then_inc(slab_done, 1)

                def scores(u):
                    n, j = u // QT, u % QT
                    if u == 0:
                        pe.wait_ge(rot_ready, QT + 2)
                    if u >= 2:
                        pe.wait_ge(scores_read, u - 1)
                    for g in range(2):
                        k0, k1 = max(n - 1, 0) * P, (n + 1) * P
                        out = bank[4 + u % 2][:, (g + 1) * 2 * P - (k1 - k0):(g + 1) * 2 * P]
                        last = nc.tensor.matmul(out, q[:, j * T + n * P:j * T + (n + 1) * P],
                                                kz[:, g * T + k0:g * T + k1], start=True, stop=True)
                    last.then_inc(scores_done, 1)

                def turn_probs(u):
                    pe.wait_ge(probs_ready, u + 1)
                    if u > 0:
                        pe.wait_ge(probsT_ready, u)
                    else:
                        pe.wait_ge(vz_ready, 2)
                    e = tile(probs, u % 2)
                    for g in range(2):
                        for kb in range(1 if u < QT else 0, 2):
                            c = slice((2 * g + kb) * P, (2 * g + kb + 1) * P)
                            last = nc.tensor.transpose(bank[6][:, c], e[:, c], ident)
                    last.then_inc(turned, 1)

                def weighted_values(u):
                    n, j = u // QT, u % QT
                    pe.wait_ge(probsT_ready, u + 1)
                    if j == 0 and n > 0:
                        pe.wait_ge(h_lo_ready, h0 + n)
                    parts = [(g, kb) for g in range(2) for kb in range(1 if n == 0 else 0, 2)]
                    for g, kb in parts:
                        c = slice((2 * g + kb) * P, (2 * g + kb + 1) * P)
                        last = nc.tensor.matmul(bank[7][:, j * P:(j + 1) * P], vz4[:, g, n - 1 + kb, :],
                                                tile(probsT, u % 2)[:, c], start=(g, kb) == parts[0],
                                                stop=(g, kb) == parts[-1])
                    last.then_inc(pv_done, 1)

                slabs_by_tile(m0, x_lo_ready, lambda k: DT * refresh + k + 1, *x)
                slab(m0 + 3, *x)
                rotate(0)
                rotate(1)
                slab(m0 + 4, *x)
                rotate(2)
                rotate(3)
                slab(m0 + 5, *x)
                rotate(4)
                turn_v()
                for w in range(UNITS // 2 + 2):
                    if w < 4:
                        sgu_v_slab(w)
                    elif w < 8:
                        slab(m0 + 6 + w, *x)
                    for u in (2 * w, 2 * w + 1):
                        if u < UNITS:
                            scores(u)
                        if 2 <= u < UNITS + 2:
                            turn_probs(u - 2)
                        if u >= 4:
                            weighted_values(u - 4)
                pe.wait_ge(v_normed, BLOCKS)
                for j in range(4):
                    for cp in range(2):
                        if j > 0:
                            pe.wait_ge(spatial_read, 4 * (j - 1) + 2 * cp + 2)
                        for cc in range(2):
                            c = 2 * cp + cc
                            last = nc.tensor.matmul(bank[4 + cp][:, cc * 2 * P:(cc + 1) * 2 * P],
                                                    v_act[:, c * T + j * P:c * T + (j + 1) * P],
                                                    spatial[:, 2 * j * P:(2 * j + 2) * P], start=True, stop=True)
                        last.then_inc(spatial_done, 1)
                n = FIRST["mix_out", 0]
                slabs_by_tile(n, h_lo_ready, lambda k: h0 + BLOCKS + max(0, k - QT + 1), *o)
                for d in range(3, DT):
                    slab(n + d, *o)

            def conv_mixer(refresh, x, o):
                n, h0 = FIRST["mix", 1], H_BEFORE["mix", 1]
                slabs_by_tile(n, x_lo_ready, lambda k: DT * refresh + k + 1, *x)
                slab(n + 3, *x)
                with pe.Fori(0, (3 * DT - RING) // RING) as i:
                    for j in range(RING):
                        slab(n + RING + j, *x, i=i)
                n = FIRST["mix_out", 1]
                with pe.Fori(0, DT // RING) as i:
                    for j in range(RING):
                        slab(n + j, *o, i=i, ready=(lambda k: h0 + k + 1) if j == 0 else None)

            def ple_products(layer, half_slab, p):
                n = FIRST["ple_proj", layer] + half_slab
                c = 4 * half_slab + p
                if p == 0:
                    pe.wait_ge(lo_ready, n + 1)
                    pe.wait_ge(p_lo_ready, layer + 1)
                done = DT * layer + c
                if done >= 2:
                    pe.wait_ge(ple_read, done - 1)
                for k in range(PLE_T):
                    last = three_passes(bank[4 + c % 2][:, :],
                                        (n % RING, slice((2 * p + k) * P, (2 * p + k + 1) * P)), None, None,
                                        tile(p_hi, k), tile(p_lo, k), k == 0, k == PLE_T - 1)
                last.then_inc(slab_done if p == 3 else ple_done, 1)

            for layer in range(DEPTH):
                a, b = ((a_hi, a_lo), (b_hi, b_lo)) if layer == 0 else ((b_hi, b_lo), (a_hi, a_lo))
                ffn(layer, 0, 0 if layer == 0 else X_OF["ple"], a, b)
                statistics(3 * layer, FIRST["mix", layer] - 1)
                spread(3 * layer, 0)
                spread(3 * layer, 1)
                (attention_mixer if layer == 0 else conv_mixer)(X_OF[layer, 0], a, b)
                statistics(3 * layer + 1, FIRST["up", layer, 1, 0] - 1)
                spread(3 * layer + 1, 0)
                spread(3 * layer + 1, 1)
                ffn(layer, 1, X_OF[layer, 1], a, b)
                for p in range(4):
                    ple_products(layer, 0, p)
                pe_done = FIRST["ple_proj", layer]
                statistics(3 * layer + 2, pe_done - 1)
                ple_products(layer, 1, 0)
                spread(3 * layer + 2, 0)
                ple_products(layer, 1, 1)
                spread(3 * layer + 2, 1)
                ple_products(layer, 1, 2)
                ple_products(layer, 1, 3)
                n = FIRST["ple_gate", layer]
                slabs_by_tile(n, x_lo_ready, lambda k: DT * X_OF[layer, 2] + k + 1, *a)
                for d in range(3, DT):
                    slab(n + d, *a)


def constants():
    c = np.zeros((P, 2 * P + 2), np.float32)
    c[:, 0:P] = np.eye(P)
    inv = np.power(np.float32(ROPE_THETA), -np.arange(ROT_HALF, dtype=np.float32) * np.float32(2.0 / (2 * ROT_HALF)))
    for base in (0, HEAD_DIM):
        for d in range(ROT_HALF):
            c[base + d + ROT_HALF, P + base + d] = -1.0
            c[base + d, P + base + d + ROT_HALF] = 1.0
            c[base + d, 2 * P] = c[base + d + ROT_HALF, 2 * P] = inv[d]
    return c


def kernel(x, p, positions, ln_g, ln_b, ffn_w_gate, ffn_w_up, ffn_w_down, ab_w_in, ab_sinks, sgu_ln_g,
           sgu_ln_b, sgu_w_s, sgu_b_s, ab_w_out, sc_w_in, sc_conv_w, sc_w_out, ple_w_proj, ple_w_gate):
    import concourse.bacc as bacc
    from concourse.bass_utils import run_bass_kernel_spmd

    def slabs(w):
        w = np.asarray(w)
        k, m = w.shape
        return w.reshape(k // P, P, m // P, P).transpose(2, 1, 0, 3).reshape(m // P, P, k)

    def feature_major(a):
        a = np.asarray(a)
        return np.ascontiguousarray(a.T.reshape(-1, P, a.shape[0]).transpose(1, 0, 2))

    wg, wu, wd = np.asarray(ffn_w_gate), np.asarray(ffn_w_up), np.asarray(ffn_w_down)
    w_up, w_down8, w_down6 = [], [], []
    for layer in range(DEPTH):
        for half in range(2):
            w_up.append(np.stack([slabs(wg[layer, half]), slabs(wu[layer, half])], 1).reshape(2 * FT, P, D))
            rows = wd[layer, half]
            w_down8 += [slabs(rows[0:8 * P]), slabs(rows[8 * P:16 * P])]
            w_down6.append(slabs(rows[16 * P:]))

    w_in = np.asarray(ab_w_in)[0]
    q_cols = w_in[:, 0:512].reshape(D, 2, QT, HEAD_DIM).transpose(0, 2, 1, 3).reshape(D, 512)
    k_cols, v_cols, su, sv = w_in[:, 512:640], w_in[:, 640:768], w_in[:, 768:1280], w_in[:, 1280:1792]
    sv_slabs = sv.reshape(4, 2, P, 512).transpose(0, 2, 1, 3).reshape(4, P, D)
    w_out = np.asarray(ab_w_out)[0]
    att_rows = w_out[0:512].reshape(2, QT, HEAD_DIM, D).transpose(1, 0, 2, 3).reshape(512, D)
    w_mix0 = np.concatenate([slabs(q_cols), slabs(k_cols), slabs(v_cols), sv_slabs, slabs(su),
                             slabs(np.concatenate([att_rows, w_out[512:]], 0))], 0)
    sc = np.asarray(sc_w_in)[0]
    w_mix1 = np.concatenate([
        np.stack([slabs(sc[:, D:2 * D]), slabs(sc[:, 2 * D:])], 1).reshape(2 * DT, P, D),
        slabs(sc[:, 0:D]), slabs(np.asarray(sc_w_out)[0])], 0)
    w_ple = np.concatenate([np.concatenate([
        slabs(np.asarray(ple_w_proj)[i]).reshape(2, 4, P, 256).transpose(0, 2, 1, 3).reshape(2, P, D),
        slabs(np.asarray(ple_w_gate)[i])], 0) for i in range(DEPTH)], 0)

    def columns(a):
        return np.asarray(a).reshape(3 * DEPTH, DT, P).transpose(2, 0, 1).reshape(P, 3 * DEPTH * DT)

    arrays = {
        "xT": feature_major(np.asarray(x)[0]),
        "pT": np.stack([feature_major(np.asarray(p)[i, 0]).reshape(P, PLE_T * T) for i in range(DEPTH)]),
        "positions": np.asarray(positions).reshape(1, T),
        "ln_gb": np.concatenate([columns(ln_g), columns(ln_b)], 1),
        "w_up": np.concatenate(w_up, 0),
        "w_down8": np.concatenate(w_down8, 0),
        "w_down6": np.concatenate(w_down6, 0),
        "w_mix0": w_mix0,
        "w_mix1": w_mix1,
        "w_ple": w_ple,
        "sinks": np.asarray(ab_sinks)[0].reshape(2, QT).T.reshape(1, HEADS),
        "sgu_gb": np.concatenate([np.asarray(sgu_ln_g)[0], np.asarray(sgu_ln_b)[0]]).reshape(1, 2 * T),
        "sgu_wT": np.asarray(sgu_w_s)[0].transpose(2, 0, 1).reshape(P, 8 * P),
        "sgu_b": np.repeat(np.asarray(sgu_b_s)[0].reshape(4, 2, 1, P), HEAD_DIM, 2).reshape(4, P, P)
                   .transpose(1, 0, 2).reshape(P, 4 * P),
        "conv_w": np.asarray(sc_conv_w)[0].reshape(3, DT, P).transpose(2, 1, 0).reshape(P, 3 * DT),
        "consts": constants(),
    }
    nc = bacc.Bacc("TRN2", target_bir_lowering=False, num_devices=1, dynamic_dma_scratch_size=1024)
    args, feed = [], {}
    for name, a in arrays.items():
        a = np.ascontiguousarray(a)
        feed[name] = a
        args.append(nc.dram_tensor(name, a.shape, mybir.dt.from_np(a.dtype), kind="ExternalInput").ap())
    args.append(nc.dram_tensor("outT", (P, DT, T), F32, kind="ExternalOutput").ap())
    build_program(nc, *args)
    got = run_bass_kernel_spmd(nc, [feed], core_ids=[0]).results[0]["outT"]
    return got.transpose(1, 0, 2).reshape(D, T).T.reshape(1, T, D)
```

```python
from contextlib import ExitStack

import concourse.bass as bass
import numpy as np
from concourse import mybir

F32 = mybir.dt.float32
F32R = mybir.dt.float32r
I32 = mybir.dt.int32
ALU = mybir.AluOpType
ACT = mybir.ActivationFunctionType
AX = mybir.AxisListType

P = 128
T = 512
D = 1024
DT = D // P
DEPTH = 2
D_FF = 2816
FT = D_FF // P
FT_GROUPS = (8, 8, 6)
PLE_T = 256 // P
RING = 4
SLAB = 8 * P
HEADS, KV_HEADS, HEAD_DIM = 8, 2, 64
QT = HEADS * HEAD_DIM // P
BLOCKS = T // P
UNITS = BLOCKS * QT
ROT_HALF = 8
ROPE_THETA = 500000.0
ALPHA = (2 * DEPTH) ** 0.25
LN_EPS = 1e-5
MASKED = 1e30
MAGIC = 1.5 * 2.0 ** 23
TWO_PI = 2 * np.pi
HEAD = 3
X_CHUNKS = ((0, 1), (1, 4), (4, 8))


def plan_slabs():
    first, aux_only, n = {}, set(), 0
    for layer in range(DEPTH):
        for half in range(2):
            for g, ft in enumerate(FT_GROUPS):
                first["up", layer, half, g] = n
                n += 2 * ft
                first["down", layer, half, g] = n
                n += DT
            if half == 0:
                first["mix", layer] = n
                n += (2 * QT + 2 + 4 if layer == 0 else 3 * DT)
                first["mix_out", layer] = n
                n += DT
        first["ple_proj", layer] = n
        aux_only |= {n, n + 1}
        n += 2
        first["ple_gate", layer] = n
        n += DT
    return first, aux_only, n


def split_two_pi():
    c1 = float(np.floor(TWO_PI * 2.0 ** 9) / 2.0 ** 9)
    rest = TWO_PI - c1
    scale = 2.0 ** (11 - np.floor(np.log2(rest)))
    c2 = float(np.floor(rest * scale) / scale)
    return c1, c2, float(TWO_PI - c1 - c2)


def build_program(nc, xT, pT, positions, ln_gb, w_up, w_down8, w_down6, w_mix0, w_mix1, w_ple,
                  sinks, sgu_gb, sgu_wT, sgu_b, conv_w, consts, outT):
    FIRST, AUX_ONLY, N_SLABS = plan_slabs()

    def uses(n):
        return sum(1 for m in range(n % RING, n, RING) if m not in AUX_ONLY)

    ctx = ExitStack()
    with ctx:
        def sb(name, shape, dt=F32):
            return ctx.enter_context(nc.sbuf_tensor(name, shape, dt))

        def sem(name):
            return ctx.enter_context(nc.semaphore(name))

        raw = sb("raw", [P, RING, SLAB])
        w_hi = sb("w_hi", [P, RING, SLAB], F32R)
        w_lo = sb("w_lo", [P, RING, SLAB], F32R)
        xf = sb("xf", [P, DT * T])
        a_hi, a_lo = sb("a_hi", [P, DT * T], F32R), sb("a_lo", [P, DT * T], F32R)
        b_hi, b_lo = sb("b_hi", [P, DT * T], F32R), sb("b_lo", [P, DT * T], F32R)
        p_hi, p_lo = sb("p_hi", [P, PLE_T * T], F32R), sb("p_lo", [P, PLE_T * T], F32R)
        gate = sb("gate", [P, 2, T])
        inner = sb("inner", [P, 2, T])
        sum_z, sum_q = sb("sum_z", [P, T]), sb("sum_q", [P, T])
        square = sb("square", [P, 2, T])
        temp = sb("temp", [P, 2, T])
        ident_rot = sb("ident_rot", [P, 2 * P + 2])
        ident, rotT, inv_freq = ident_rot[:, 0:P], ident_rot[:, P:2 * P], ident_rot[:, 2 * P:2 * P + 1]
        ones = sb("ones", [P, P])
        mean_col = sb("mean_col", [P, 2])
        eps = sb("eps", [P, 4])
        gb = sb("gb", [P, 2 * 3 * DEPTH * DT])
        small = sb("small", [P, 32])
        warm_rhs = sb("warm_rhs", [P, T], mybir.dt.bfloat16)
        warm_tile = sb("warm_tile", [P, 1])
        nsink = sb("nsink", [P, HEADS])
        conv_taps = sb("conv_taps", [P, 3 * DT])
        taps = sb("taps", [P, 2, 3])
        stats6 = sb("stats6", [P, BLOCKS, 6])
        stats2 = sb("stats2", [P, BLOCKS, 2])
        sgu_std = sb("sgu_std", [P, BLOCKS])
        sgu_rstd = sb("sgu_rstd", [P, BLOCKS])
        sm = sb("sm", [P, 2, 12])

        scratch = sb("scratch", [P, 14080])
        at = 0

        def carve(cols):
            nonlocal at
            at += cols
            return scratch[:, at - cols:at]

        q = carve(QT * T)
        kz = carve(KV_HEADS * T)
        vz = carve(KV_HEADS * BLOCKS * P)
        u_act = carve(4 * T)
        v_act = carve(BLOCKS * T)
        probs = carve(2 * T)
        probsT = carve(2 * T)
        cos, sin = carve(T), carve(T)
        spatial = carve(8 * P)
        mask = carve(2 * P)
        spatial_bias = carve(4 * P)
        sgu_gain, sgu_bias = carve(T), carve(T)
        ple = scratch[:, 0:DT * T]
        p_raw = scratch[:, 0:PLE_T * T]
        conv_y = scratch[:, 0:DT * T]
        zpad = scratch[:, DT * T:DT * T + 2 * (T + 2)]

        bank = [ctx.enter_context(nc.psum_tensor(f"bank{b}", [P, T], F32)) for b in range(8)]

        loaded = [sem(f"loaded{s}") for s in range(RING)]
        const_loaded = sem("const_loaded")
        x_loaded = [sem(f"x_loaded{c}") for c in range(len(X_CHUNKS))]
        head_loaded = [sem(f"head_loaded{s}") for s in range(HEAD)]
        head_hi, head_lo = sem("head_hi"), sem("head_lo")
        p_loaded = sem("p_loaded")
        hi_ready, lo_ready, slab_done = sem("hi_ready"), sem("lo_ready"), sem("slab_done")
        bank_read = [sem(f"bank_read{b}") for b in range(RING)]
        h_hi_ready, h_lo_ready = sem("h_hi_ready"), sem("h_lo_ready")
        x_hi_ready, x_lo_ready = sem("x_hi_ready"), sem("x_lo_ready")
        p_hi_ready, p_lo_ready = sem("p_hi_ready"), sem("p_lo_ready")
        const_ready = sem("const_ready")
        pool_chain, dve_chain, act_chain = sem("pool_chain"), sem("dve_chain"), sem("act_chain")
        square_ready, sums_ready = sem("square_ready"), sem("sums_ready")
        mean_ready, meansq_ready = sem("mean_ready"), sem("meansq_ready")
        mean2_ready = sem("mean2_ready")
        var_ready, std_ready, diag_ready = sem("var_ready"), sem("std_ready"), sem("diag_ready")
        spread_ready, normed_ready, xf_ready = sem("spread_ready"), sem("normed_ready"), sem("xf_ready")
        ple_done, ple_read, mixed_in = sem("ple_done"), sem("ple_read"), sem("mixed_in")
        angle_ready, table_ready = sem("angle_ready"), sem("table_ready")
        rot_done, rot_ready = sem("rot_done"), sem("rot_ready")
        v_turned, vz_ready = sem("v_turned"), sem("vz_ready")
        scores_done, scores_read, max_ready, exp_ready = (
            sem("scores_done"), sem("scores_read"), sem("max_ready"), sem("exp_ready"))
        probs_ready, turned, probsT_ready, pv_done = (
            sem("probs_ready"), sem("turned"), sem("probsT_ready"), sem("pv_done"))
        gelu_v, v_var, v_std, v_scaled, v_normed = (
            sem("gelu_v"), sem("v_var"), sem("v_std"), sem("v_scaled"), sem("v_normed"))
        gelu_u, spatial_done, spatial_read, sgu_ready = (
            sem("gelu_u"), sem("spatial_done"), sem("spatial_read"), sem("sgu_ready"))
        conv_m = sem("conv_m")
        out_stored = sem("out_stored")

        def tile(buf, k):
            return buf[:, bass.ds(k * T, T)] if not isinstance(k, int) else buf[:, k * T:(k + 1) * T]

        H_BEFORE, count = {}, 0
        for layer in range(DEPTH):
            for half in range(2):
                for g, ft in enumerate(FT_GROUPS):
                    H_BEFORE[layer, half, g] = count
                    count += ft
                if half == 0:
                    H_BEFORE["mix", layer] = count
                    count += DT
        X_OF = {"load": 0, (0, 0): 1, (0, 1): 2, (0, 2): 3, "ple": 4, (1, 0): 5, (1, 1): 6, (1, 2): 7}
        NORM_OF = {X_OF[layer, which]: 3 * layer + which for layer in range(DEPTH) for which in range(3)}

        block = ctx.enter_context(nc.Block())

        @block.sync
        def _(sp):
            def load(n, src, i=0):
                s = n % RING
                if n >= RING:
                    sp.wait_ge(hi_ready, n - RING + 1 + RING * i)
                    sp.wait_ge(lo_ready, n - RING + 1 + RING * i)
                sp.dma_start(raw[:, s, 0:src.shape[-1]], src).then_inc(loaded[s], 16)

            def load_run(n, slabs, src_of):
                start = 0
                if n == 0:
                    for j in range(HEAD):
                        sp.dma_start(raw[:, j, 0:T], src_of(j)[:, 0:T]).then_inc(head_loaded[j], 16)
                    for j in range(HEAD):
                        sp.dma_start(raw[:, j, T:SLAB], src_of(j)[:, T:SLAB]).then_inc(loaded[j], 16)
                    load(HEAD, src_of(HEAD))
                    start = RING
                steps = (slabs - start) // RING
                with sp.Fori(0, steps) as i:
                    for j in range(RING):
                        load(n + start + j, src_of(i * RING + start + j), i)
                for j in range(start + steps * RING, slabs):
                    load(n + j, src_of(j))

            for layer in range(DEPTH):
                for half in range(2):
                    f = 2 * layer + half
                    for g, ft in enumerate(FT_GROUPS):
                        load_run(FIRST["up", layer, half, g], 2 * ft,
                                 lambda j, b=f * 2 * FT + 16 * g: w_up[b + j])
                        if half == 1 and g == 0:
                            sp.wait_ge(x_lo_ready, DT * (X_OF[layer, 1] + 1))
                            sp.dma_start(p_raw, pT[layer]).then_inc(p_loaded, 16)
                        if g < 2:
                            load_run(FIRST["down", layer, half, g], DT,
                                     lambda j, b=(f * 2 + g) * DT: w_down8[b + j])
                        else:
                            load_run(FIRST["down", layer, half, g], DT,
                                     lambda j, b=f * DT: w_down6[b + j])
                    if half == 0:
                        w_mix = w_mix0 if layer == 0 else w_mix1
                        load_run(FIRST["mix", layer], w_mix.shape[0], lambda j, w=w_mix: w[j])
                load_run(FIRST["ple_proj", layer], 2 + DT, lambda j, b=layer * (2 + DT): w_ple[b + j])
            for d in range(DT):
                sp.wait_ge(mixed_in, DT + d + 1)
                sp.dma_start(outT[:, d, :], tile(xf, d)).then_inc(out_stored, 16)
            sp.wait_ge(out_stored, 16 * DT)

        @block.gpsimd
        def _(pool):
            nc.gpsimd.memset(warm_rhs[:, :], 1.0).then_inc(const_ready, 1)
            nc.gpsimd.memset(ones[:, :], 1.0).then_inc(const_ready, 1)
            nc.gpsimd.memset(mean_col[:, :], 1.0 / D).then_inc(const_ready, 1)
            nc.gpsimd.memset(eps[:, 0:1], LN_EPS).then_inc(const_ready, 1)
            nc.gpsimd.memset(eps[:, 1:2], 4 * LN_EPS).then_inc(const_ready, 1)

            def split_x(refresh, d, hi, lo):
                pool.wait_ge(x_hi_ready, DT * refresh + d + 1)
                if refresh == 0:
                    for c, (d0, _) in enumerate(X_CHUNKS):
                        if d == d0:
                            pool.wait_ge(x_loaded[c], 16)
                elif refresh != X_OF["ple"]:
                    pool.wait_ge(xf_ready, DT * NORM_OF[refresh] + d + 1)
                nc.gpsimd.tensor_tensor(tile(lo, d), tile(xf, d), tile(hi, d).bitcast(F32),
                                        ALU.subtract).then_inc(x_lo_ready, 1)

            for d in range(DT):
                split_x(0, d, a_hi, a_lo)

            nc.gpsimd.memset(kz, 0.0).then_inc(const_ready, 1)
            nc.gpsimd.memset(vz, 0.0).then_inc(const_ready, 1)
            nc.gpsimd.memset(mask, 0.0).then_inc(pool_chain, 1)
            pool.wait_ge(pool_chain, 1)
            nc.gpsimd.affine_select(out=mask[:, 0:P], in_=mask[:, 0:P], compare_op=ALU.is_gt, fill=MASKED,
                                    base=0, pattern=[[1, P]], channel_multiplier=-1).then_inc(const_ready, 1)
            nc.gpsimd.affine_select(out=mask[:, P:2 * P], in_=mask[:, P:2 * P], compare_op=ALU.is_ge,
                                    fill=MASKED, base=0, pattern=[[-1, P]],
                                    channel_multiplier=1).then_inc(const_ready, 1)
            pool.wait_ge(const_loaded, 16 * 8)
            spatial3 = spatial.rearrange("p (g t) -> p g t", g=8)
            nc.gpsimd.affine_select(out=spatial3, in_=spatial3, compare_op=ALU.is_ge, fill=0.0, base=0,
                                    pattern=[[0, 8], [1, P]], channel_multiplier=-1).then_inc(const_ready, 1)

            def norm_part(layer, which, hi, lo):
                for d in range(DT):
                    split_x(X_OF[layer, which], d, hi, lo)

            def mixer_part():
                for tb in range(BLOCKS):
                    v = tile(v_act, tb)
                    pool.wait_ge(v_scaled, tb + 1)
                    nc.gpsimd.tensor_tensor(v, v, sgu_gain, ALU.mult).then_inc(pool_chain, 1)
                    pool.wait_ge(pool_chain, 2 + tb)
                    nc.gpsimd.tensor_tensor(v, v, sgu_bias, ALU.add).then_inc(v_normed, 1)

            for layer in range(DEPTH):
                x_hi, x_lo, o_hi, o_lo = (a_hi, a_lo, b_hi, b_lo) if layer == 0 else (b_hi, b_lo, a_hi, a_lo)
                norm_part(layer, 0, x_hi, x_lo)
                if layer == 0:
                    mixer_part()
                norm_part(layer, 1, x_hi, x_lo)
                norm_part(layer, 2, x_hi, x_lo)
                if layer == 0:
                    for d in range(DT):
                        split_x(X_OF["ple"], d, o_hi, o_lo)

        @block.scalar
        def _(act):
            for c, (d0, d1) in enumerate(X_CHUNKS):
                act.dma_start(xf[:, d0 * T:d1 * T], xT[:, d0:d1, :].rearrange("p d t -> p (d t)")).then_inc(x_loaded[c], 16)

            def split_chunk(c):
                act.wait_ge(x_loaded[c], 16)
                for d in range(*X_CHUNKS[c]):
                    nc.scalar.activation(tile(a_hi, d), tile(xf, d), ACT.Copy).then_inc(x_hi_ready, 1)

            split_chunk(0)
            for j in range(HEAD):
                act.wait_ge(head_loaded[j], 16)
                nc.scalar.activation(w_hi[:, j, 0:T], raw[:, j, 0:T], ACT.Copy).then_inc(head_hi, 1)
            split_chunk(1)
            for j in range(HEAD):
                act.wait_ge(loaded[j], 16)
                nc.scalar.activation(w_hi[:, j, T:SLAB], raw[:, j, T:SLAB], ACT.Copy).then_inc(hi_ready, 1)
            split_chunk(2)
            act.wait_ge(loaded[HEAD], 16)
            nc.scalar.activation(w_hi[:, HEAD, :], raw[:, HEAD, :], ACT.Copy).then_inc(hi_ready, 1)
            act.dma_start(ident_rot[:, :], consts).then_inc(const_loaded, 16)
            act.dma_start(gb[:, :], ln_gb).then_inc(const_loaded, 16)
            act.dma_start(spatial, sgu_wT).then_inc(const_loaded, 16)
            act.dma_start(spatial_bias, sgu_b).then_inc(const_loaded, 16)
            act.dma_start(scratch[:, 14080 - 2 * T:14080], sgu_gb.broadcast_to([P, 2 * T])).then_inc(const_loaded, 16)
            act.dma_start(nsink[:, :], sinks.broadcast_to([P, HEADS])).then_inc(const_loaded, 16)
            act.dma_start(conv_taps[:, :], conv_w).then_inc(const_loaded, 16)
            act.dma_start(q[:, 0:T].bitcast(I32), positions.broadcast_to([P, T])).then_inc(const_loaded, 16)

            def warm(func):
                nc.scalar.activation(warm_tile[:, :], mean_col[:, 0:1], func)

            def refill(n, i=0):
                m = n + RING
                if m < N_SLABS:
                    act.wait_ge(loaded[m % RING], 16 * (m // RING + 1) + 16 * i)
                    nc.scalar.activation(w_hi[:, m % RING, :], raw[:, m % RING, :], ACT.Copy).then_inc(hi_ready, 1)

            act.wait_ge(const_ready, 5)
            warm(ACT.Silu)

            def up_pair(n, jj, hc, h_tile, i=0):
                b = n % RING
                act.wait_ge(slab_done, n + 1 + RING * i)
                nc.scalar.activation(gate[:, jj, :], bank[b][:, :], ACT.Silu).then_inc(bank_read[b], 1)
                refill(n, i)
                act.wait_ge(slab_done, n + 2 + RING * i)
                refill(n + 1, i)
                act.wait_ge(bank_read[(n + 1) % RING], uses(n + 1) + 1 + i)
                nc.scalar.activation(h_tile, inner[:, jj, :], ACT.Copy).then_inc(h_hi_ready, 1)

            def ffn(layer, half, o_hi):
                for g, ft in enumerate(FT_GROUPS):
                    n = FIRST["up", layer, half, g]
                    with act.Fori(0, ft // 2) as i:
                        for jj in range(2):
                            up_pair(n + 2 * jj, jj, 0, tile(o_hi, 2 * i + jj), i)
                    if g < 2:
                        n = FIRST["down", layer, half, g]
                        with act.Fori(0, DT // RING) as i:
                            for j in range(RING):
                                act.wait_ge(slab_done, n + j + 1 + RING * i)
                                refill(n + j, i)
                    if layer == 0 and half == 0 and g == 0:
                        act.wait_ge(angle_ready, 1)
                        nc.scalar.activation(sin, temp[:, 0, :], ACT.Sin).then_inc(table_ready, 1)
                        nc.scalar.activation(cos, temp[:, 1, :], ACT.Sin).then_inc(table_ready, 1)
                        warm(ACT.Silu)
                    if half == 1 and g == 0:
                        act.wait_ge(p_loaded, 16 * (layer + 1))
                        nc.scalar.activation(p_hi[:, :], p_raw, ACT.Copy).then_inc(p_hi_ready, 1)

            def final_products(norm, n0, after_last):
                warm(ACT.Sqrt)
                for d in range(DT):
                    n = n0 + d
                    if d >= 2:
                        act.wait_ge(sums_ready, 12 * norm + 2 * max(1, d - 2))
                    act.wait_ge(bank_read[n % RING], uses(n) + 1)
                    nc.scalar.activation(square[:, d % 2, :], tile(xf, d), ACT.Square).then_inc(square_ready, 1)
                    if d < DT - 1:
                        refill(n)
                refill(n0 + DT - 1)
                after_last()

            def normalise(layer, which, scale, hi, next_func, extra):
                norm = 3 * layer + which
                act.wait_ge(var_ready, norm + 1)
                nc.scalar.activation(small[:, 8:12], small[:, 4:8], ACT.Sqrt,
                                     bias=eps[:, scale:scale + 1]).then_inc(std_ready, 1)
                warm(next_func)
                extra(-1)
                for d in range(DT):
                    c = norm * DT + d
                    g0 = 3 * DEPTH * DT
                    act.wait_ge(normed_ready, c + 1)
                    for dst, signal in ((tile(hi, d), x_hi_ready), (tile(xf, d), xf_ready)):
                        nc.scalar.activation(dst, temp[:, d % 2, :], ACT.Identity, scale=gb[:, c:c + 1],
                                             bias=gb[:, g0 + c:g0 + c + 1]).then_inc(signal, 1)
                    extra(d)

            def nothing(*_):
                pass

            def attention_mixer(o_hi):
                m0, h0 = FIRST["mix", 0], H_BEFORE["mix", 0]

                def take(n, dst, func=ACT.Copy):
                    act.wait_ge(slab_done, n + 1)
                    nc.scalar.activation(dst, bank[n % RING][:, :], func).then_inc(bank_read[n % RING], 1)

                def exps(u):
                    lo = P if u < QT else 0
                    par = u % 2
                    act.wait_ge(max_ready, u + 1)
                    for g in range(2):
                        c = slice(g * 2 * P + lo, (g + 1) * 2 * P)
                        nc.scalar.activation(tile(probs, par)[:, c], inner[:, par, c], ACT.Exp, scale=-1.0,
                                             bias=sm[:, par, 2 + g:3 + g],
                                             accum_out=sm[:, par, 6 + g:7 + g]).then_inc(act_chain, 1)
                    nc.scalar.activation(sm[:, par, 8:10], sm[:, par, 4:6], ACT.Exp).then_inc(act_chain, 1)
                    act.wait_ge(act_chain, 3 * u + 3)
                    nc.scalar.activation(warm_tile[:, :], mean_col[:, 0:1], ACT.Copy).then_inc(exp_ready, 1)

                def turned_out(u):
                    act.wait_ge(turned, u + 1)
                    if u >= 2:
                        act.wait_ge(pv_done, u - 1)
                    lo = P if u < QT else 0
                    src = bank[6][:, :].rearrange("p (g k) -> p g k", g=2)[:, :, lo:]
                    dst = tile(probsT, u % 2).rearrange("p (g k) -> p g k", g=2)[:, :, lo:]
                    nc.scalar.activation(dst, src, ACT.Copy).then_inc(probsT_ready, 1)

                def att_out(n):
                    act.wait_ge(pv_done, QT * (n + 1))
                    dst = o_hi[:, 0:QT * T].rearrange("p (j t) -> p j t", j=QT)[:, :, n * P:(n + 1) * P]
                    src = bank[7][:, :].rearrange("p (j t) -> p j t", j=QT)
                    nc.scalar.activation(dst, src, ACT.Copy).then_inc(h_hi_ready, 1)

                for j in range(QT):
                    take(m0 + j, tile(q, j))
                    refill(m0 + j)
                take(m0 + 4, square[:, 0, :])
                refill(m0 + 4)
                take(m0 + 5, gate[:, 0, :])
                refill(m0 + 5)
                act.wait_ge(v_turned, 1)
                act.wait_ge(const_ready, 7)
                vz4 = vz.rearrange("p (g n c) -> p g n c", g=2, n=BLOCKS)
                src = bank[6][:, :].rearrange("p (n c) -> p n c", n=BLOCKS)
                for g in range(2):
                    c = slice(g * HEAD_DIM, (g + 1) * HEAD_DIM)
                    nc.scalar.activation(vz4[:, g, :, c], src[:, :, c], ACT.Copy).then_inc(vz_ready, 1)
                for w in range(UNITS // 2 + 2):
                    if w < 8:
                        n = m0 + 6 + w
                        act.wait_ge(slab_done, n + 1)
                        if w == 3:
                            for tb in range(BLOCKS):
                                b = (m0 + 6 + tb) % RING
                                nc.scalar.activation(tile(v_act, tb), bank[b][:, :],
                                                     ACT.Gelu_apprx_tanh).then_inc(bank_read[b], 1)
                        if w >= 4:
                            take(n, tile(u_act, w - 4))
                        refill(n)
                        if w == 5:
                            act.wait_ge(v_var, 1)
                            nc.scalar.activation(sgu_std[:, :], stats2[:, :, 1], ACT.Sqrt,
                                                 bias=eps[:, 0:1]).then_inc(v_std, 1)
                    for u in (2 * w, 2 * w + 1):
                        if 2 <= u < UNITS + 2:
                            turned_out(u - 2)
                        if u < UNITS:
                            exps(u)
                    if w >= 3 and w % 2 == 1:
                        att_out((w - 3) // 2)
                for j in range(4):
                    act.wait_ge(bank_read[(m0 + 10 + j) % RING], uses(m0 + 10 + j) + 1)
                    nc.scalar.activation(tile(u_act, j), tile(u_act, j), ACT.Gelu_apprx_tanh).then_inc(gelu_u, 1)
                for j in range(4):
                    act.wait_ge(sgu_ready, j + 1)
                    nc.scalar.activation(tile(o_hi, QT + j), inner[:, j % 2, :], ACT.Copy).then_inc(h_hi_ready, 1)

            def conv_mixer(o_hi):
                m0 = FIRST["mix", 1]

                def gate_and_z(n, i=0):
                    for jj in range(2):
                        g = n + 2 * jj
                        act.wait_ge(slab_done, g + 1 + RING * i)
                        act.wait_ge(bank_read[(g + 1) % RING], uses(g + 1) + i)
                        nc.scalar.activation(gate[:, jj, :], bank[g % RING][:, :],
                                             ACT.Copy).then_inc(bank_read[g % RING], 1)
                        refill(g, i)
                        act.wait_ge(slab_done, g + 2 + RING * i)
                        refill(g + 1, i)

                with act.Fori(0, DT // 2) as i:
                    gate_and_z(m0, i)
                n = m0 + 2 * DT
                with act.Fori(0, DT // RING) as i:
                    for j in range(RING):
                        act.wait_ge(slab_done, n + j + 1 + RING * i)
                        refill(n + j, i)
                        act.wait_ge(bank_read[(n + j) % RING], uses(n + j) + 1 + i)
                        nc.scalar.activation(tile(o_hi, RING * i + j), inner[:, j % 2, :],
                                             ACT.Copy).then_inc(h_hi_ready, 1)

            def ple_step(layer):
                pp0 = FIRST["ple_proj", layer]

                def take(p):
                    if p % 4 == 3:
                        act.wait_ge(slab_done, pp0 + p // 4 + 1)
                    else:
                        act.wait_ge(ple_done, 6 * layer + 3 * (p // 4) + p % 4 + 1)
                    nc.scalar.activation(tile(ple, p), bank[4 + p % 2][:, :], ACT.Copy).then_inc(ple_read, 1)

                def after_last():
                    take(0)
                    take(1)

                def extra(d):
                    if d == -1:
                        take(2)
                        take(3)
                    if 0 <= d < 4:
                        take(4 + d)
                    if d == 1:
                        refill(pp0)
                    if d == 4:
                        refill(pp0 + 1)
                return after_last, extra

            def ple_gates(layer, o_hi):
                n0 = FIRST["ple_gate", layer]
                for d in range(DT):
                    n = n0 + d
                    act.wait_ge(slab_done, n + 1)
                    if d >= 2:
                        act.wait_ge(mixed_in, DT * layer + d - 1)
                    nc.scalar.activation(gate[:, d % 2, :], bank[n % RING][:, :],
                                         ACT.Sigmoid).then_inc(bank_read[n % RING], 1)
                    if d == DT - 1:
                        warm(ACT.Silu)
                    refill(n)
                    if layer == 0:
                        act.wait_ge(mixed_in, DT * layer + d + 1)
                        nc.scalar.activation(tile(o_hi, d), tile(xf, d), ACT.Copy).then_inc(x_hi_ready, 1)

            for layer in range(DEPTH):
                x_hi, o_hi = (a_hi, b_hi) if layer == 0 else (b_hi, a_hi)
                ffn(layer, 0, o_hi)
                final_products(3 * layer, FIRST["down", layer, 0, 2], nothing)
                normalise(layer, 0, 1, x_hi, ACT.Exp if layer == 0 else ACT.Copy, nothing)
                if layer == 0:
                    attention_mixer(o_hi)
                else:
                    conv_mixer(o_hi)
                final_products(3 * layer + 1, FIRST["mix_out", layer], nothing)
                normalise(layer, 1, 0, x_hi, ACT.Silu, nothing)
                ffn(layer, 1, o_hi)
                after_last, extra = ple_step(layer)
                final_products(3 * layer + 2, FIRST["down", layer, 1, 2], after_last)
                normalise(layer, 2, 1, x_hi, ACT.Sigmoid, extra)
                ple_gates(layer, o_hi)

        @block.vector
        def _(dve):
            chain = [0]

            def link(ins):
                chain[0] += 1
                ins.then_inc(dve_chain, 1)
                dve.wait_ge(dve_chain, chain[0])

            def refill(n, i=0):
                m = n + RING
                if m < N_SLABS:
                    dve.wait_ge(hi_ready, m + 1 + RING * i)
                    nc.vector.tensor_tensor(w_lo[:, m % RING, :], raw[:, m % RING, :],
                                            w_hi[:, m % RING, :].bitcast(F32), ALU.subtract).then_inc(lo_ready, 1)

            for j in range(HEAD):
                dve.wait_ge(head_hi, j + 1)
                nc.vector.tensor_tensor(w_lo[:, j, 0:T], raw[:, j, 0:T], w_hi[:, j, 0:T].bitcast(F32),
                                        ALU.subtract).then_inc(head_lo, 1)
            for j in range(HEAD):
                dve.wait_ge(hi_ready, j + 1)
                nc.vector.tensor_tensor(w_lo[:, j, T:SLAB], raw[:, j, T:SLAB], w_hi[:, j, T:SLAB].bitcast(F32),
                                        ALU.subtract).then_inc(lo_ready, 1)
            refill(HEAD - RING)

            def up_pair(n, jj, hc, o_hi, o_lo, k, i=0):
                refill(n, i)
                dve.wait_ge(bank_read[n % RING], uses(n) + 1 + i)
                dve.wait_ge(slab_done, n + 2 + RING * i)
                b = (n + 1) % RING
                nc.vector.tensor_tensor(inner[:, jj, :], gate[:, jj, :], bank[b][:, :],
                                        ALU.mult).then_inc(bank_read[b], 1)
                refill(n + 1, i)
                dve.wait_ge(h_hi_ready, hc + 1 + 2 * i)
                nc.vector.tensor_tensor(tile(o_lo, k), inner[:, jj, :], tile(o_hi, k).bitcast(F32),
                                        ALU.subtract).then_inc(h_lo_ready, 1)

            def add_product(n, z, first, scale, i=0):
                b = n % RING
                dve.wait_ge(slab_done, n + 1 + RING * i)
                if first:
                    nc.vector.scalar_tensor_tensor(out=z, in0=z, scalar=scale, in1=bank[b][:, :],
                                                   op0=ALU.mult, op1=ALU.add).then_inc(bank_read[b], 1)
                else:
                    nc.vector.tensor_tensor(z, z, bank[b][:, :], ALU.add).then_inc(bank_read[b], 1)

            def angles():
                c1, c2, c3 = split_two_pi()
                dve.wait_ge(const_loaded, 16 * 8)
                ang, turns, high, low = temp[:, 0, :], temp[:, 1, :], square[:, 0, :], square[:, 1, :]
                link(nc.vector.tensor_copy(ang, q[:, 0:T].bitcast(I32)))
                link(nc.vector.tensor_scalar(ang, ang, inv_freq, None, ALU.mult))
                link(nc.vector.tensor_scalar(turns, ang, 1 / TWO_PI, None, ALU.mult))
                link(nc.vector.tensor_scalar(turns, turns, MAGIC, None, ALU.add))
                link(nc.vector.tensor_scalar(turns, turns, MAGIC, None, ALU.subtract))
                link(nc.vector.tensor_scalar(high, turns, MAGIC * 4096, None, ALU.add))
                link(nc.vector.tensor_scalar(high, high, MAGIC * 4096, None, ALU.subtract))
                link(nc.vector.tensor_tensor(low, turns, high, ALU.subtract))
                for part, c in ((high, c1), (low, c1), (high, c2), (low, c2), (turns, c3)):
                    link(nc.vector.scalar_tensor_tensor(out=ang, in0=part, scalar=-c, in1=ang,
                                                        op0=ALU.mult, op1=ALU.add))
                link(nc.vector.tensor_scalar(ang, ang, float(np.float32(3.1415925)), -float(np.float32(3.1415925)),
                                             ALU.min, ALU.max))
                link(nc.vector.scalar_tensor_tensor(out=turns, in0=ang, scalar=-1.0, in1=ang,
                                                    op0=ALU.mult, op1=ALU.max))
                nc.vector.tensor_scalar(turns, turns, -1.0, float(np.pi / 2), ALU.mult, ALU.add).then_inc(angle_ready, 1)

            def ffn(layer, half, o_hi, o_lo):
                for g, ft in enumerate(FT_GROUPS):
                    n, h = FIRST["up", layer, half, g], H_BEFORE[layer, half, g]
                    with dve.Fori(0, ft // 2) as i:
                        for jj in range(2):
                            up_pair(n + 2 * jj, jj, h + jj, o_hi, o_lo, 2 * i + jj, i)
                    if g < 2:
                        n = FIRST["down", layer, half, g]
                        with dve.Fori(0, DT // RING) as i:
                            for j in range(RING):
                                add_product(n + j, tile(xf, RING * i + j), g == 0, 2 * ALPHA, i)
                                refill(n + j, i)
                    if layer == 0 and half == 0 and g == 0:
                        angles()
                    if half == 1 and g == 0:
                        dve.wait_ge(p_hi_ready, layer + 1)
                        nc.vector.tensor_tensor(p_lo[:, :], p_raw, p_hi[:, :].bitcast(F32),
                                                ALU.subtract).then_inc(p_lo_ready, 1)

            def final_products(norm, n0, first, scale):
                for d in range(DT):
                    z = tile(xf, d)
                    add_product(n0 + d, z, first, scale)
                    if 1 <= d < DT - 1:
                        dve.wait_ge(bank_read[(n0 + d) % RING], uses(n0 + d) + 1)
                        nc.vector.tensor_tensor(sum_z[:, :], tile(xf, 0) if d == 1 else sum_z[:, :], z,
                                                ALU.add).then_inc(sums_ready, 1)
                        dve.wait_ge(square_ready, DT * norm + d + 1)
                        nc.vector.tensor_tensor(sum_q[:, :], square[:, 0, :] if d == 1 else sum_q[:, :],
                                                square[:, d % 2, :], ALU.add).then_inc(sums_ready, 1)
                    if d < DT - 1:
                        refill(n0 + d)

            def normalise(layer, which, n7):
                norm = 3 * layer + which
                mean, meansq = bank[6][:, 0:4], bank[7][:, 0:4]
                mean2, var, std, rstd = small[:, 0:4], small[:, 4:8], small[:, 8:12], small[:, 12:16]

                def diagonal(dst, col):
                    nc.vector.tensor_tensor(
                        dst.rearrange("p (b t) -> p b t", b=BLOCKS),
                        ident.unsqueeze(1).broadcast_to([P, BLOCKS, P]),
                        col.unsqueeze(2).broadcast_to([P, BLOCKS, P]),
                        ALU.mult).then_inc(diag_ready, 1)

                dve.wait_ge(mean_ready, norm + 1)
                mean_sb = small[:, 16:20]
                link(nc.vector.tensor_copy(mean_sb, mean))
                nc.vector.tensor_tensor(mean2, mean_sb, mean_sb, ALU.mult).then_inc(mean2_ready, 1)
                diagonal(square[:, 0, :], mean_sb)
                dve.wait_ge(mean2_ready, norm + 1)
                dve.wait_ge(meansq_ready, norm + 1)
                nc.vector.tensor_tensor(var, meansq, mean2, ALU.subtract).then_inc(var_ready, 1)
                dve.wait_ge(std_ready, norm + 1)
                link(nc.vector.reciprocal(rstd, std))
                diagonal(square[:, 1, :], rstd)
                for d in range(DT):
                    t = temp[:, d % 2, :]
                    if d == 0:
                        dve.wait_ge(spread_ready, 2 * norm + 1)
                    if d >= 2:
                        dve.wait_ge(xf_ready, norm * DT + d - 1)
                    link(nc.vector.tensor_tensor(t, tile(xf, d), bank[6][:, :], ALU.subtract))
                    if d == 0:
                        dve.wait_ge(spread_ready, 2 * norm + 2)
                    nc.vector.tensor_tensor(t, t, bank[7][:, :], ALU.mult).then_inc(normed_ready, 1)
                    if d == 2:
                        refill(n7)
                        if which == 2:
                            refill(n7 + 1)
                    if d == 4 and which == 2:
                        refill(n7 + 2)

            def attention_mixer(o_hi, o_lo):
                m0, h0 = FIRST["mix", 0], H_BEFORE["mix", 0]

                def rotate(r, src):
                    b = bank[4 + r % 2]
                    if r < QT:
                        dve.wait_ge(bank_read[(m0 + r) % RING], uses(m0 + r) + 1)
                    link(nc.vector.tensor_tensor(temp[:, 0, :], src, cos, ALU.mult))
                    dve.wait_ge(rot_done, r + 1)
                    link(nc.vector.tensor_tensor(temp[:, 1, :], b[:, :], sin, ALU.mult))
                    if r < QT:
                        nc.vector.tensor_tensor(src, temp[:, 0, :], temp[:, 1, :], ALU.add).then_inc(rot_ready, 1)
                        dve.wait_ge(rot_ready, r + 1)
                    else:
                        for g in range(2):
                            rows = slice(g * HEAD_DIM, (g + 1) * HEAD_DIM)
                            nc.vector.tensor_tensor(kz[rows, g * T:(g + 1) * T], temp[rows, 0, :],
                                                    temp[rows, 1, :], ALU.add).then_inc(rot_ready, 1)

                def mask_and_max(u):
                    par, j = u % 2, u % QT
                    lo = P if u < QT else 0
                    view = inner[:, par, :].rearrange("p (g k) -> p g k", g=2)[:, :, lo:]
                    src = bank[4 + par][:, :].rearrange("p (g k) -> p g k", g=2)[:, :, lo:]
                    dve.wait_ge(scores_done, u + 1)
                    nc.vector.scalar_tensor_tensor(
                        out=view, in0=src, scalar=-HEAD_DIM ** -0.5,
                        in1=mask[:, lo:2 * P].unsqueeze(1).broadcast_to([P, 2, 2 * P - lo]),
                        op0=ALU.mult, op1=ALU.add).then_inc(scores_read, 1)
                    dve.wait_ge(scores_read, u + 1)
                    link(nc.vector.tensor_reduce(sm[:, par, 0:2], view, AX.X, ALU.min))
                    ns = nsink[:, 2 * j:2 * j + 2]
                    link(nc.vector.tensor_tensor(sm[:, par, 2:4], sm[:, par, 0:2], ns, ALU.min))
                    nc.vector.tensor_tensor(sm[:, par, 4:6], sm[:, par, 2:4], ns, ALU.subtract).then_inc(max_ready, 1)

                def normalise_probs(u):
                    par = u % 2
                    lo = P if u < QT else 0
                    dve.wait_ge(exp_ready, u + 1)
                    link(nc.vector.tensor_tensor(sm[:, par, 10:12], sm[:, par, 6:8], sm[:, par, 8:10], ALU.add))
                    link(nc.vector.reciprocal(sm[:, par, 10:12], sm[:, par, 10:12]))
                    for g in range(2):
                        c = slice(g * 2 * P + lo, (g + 1) * 2 * P)
                        e = tile(probs, par)[:, c]
                        ins = nc.vector.tensor_scalar(e, e, sm[:, par, 10 + g:11 + g], None, ALU.mult)
                        if g == 0:
                            link(ins)
                    ins.then_inc(probs_ready, 1)

                def att_out(n):
                    dve.wait_ge(h_hi_ready, h0 + n + 1)
                    c = slice(n * P, (n + 1) * P)
                    hi = o_hi[:, 0:QT * T].rearrange("p (j t) -> p j t", j=QT)[:, :, c]
                    lo = o_lo[:, 0:QT * T].rearrange("p (j t) -> p j t", j=QT)[:, :, c]
                    nc.vector.tensor_tensor(lo, bank[7][:, :].rearrange("p (j t) -> p j t", j=QT),
                                            hi.bitcast(F32), ALU.subtract).then_inc(h_lo_ready, 1)

                link(nc.vector.tensor_scalar(nsink[:, :], nsink[:, :], -1.0, None, ALU.mult))
                dve.wait_ge(const_ready, 10)
                dve.wait_ge(table_ready, 2)
                for j in range(3):
                    refill(m0 + j)
                rotate(0, tile(q, 0))
                refill(m0 + 3)
                rotate(1, tile(q, 1))
                rotate(2, tile(q, 2))
                refill(m0 + 4)
                rotate(3, tile(q, 3))
                refill(m0 + 5)
                rotate(4, square[:, 0, :])
                for w in range(UNITS // 2 + 2):
                    if w < 8:
                        refill(m0 + 6 + w)
                    if w == 4:
                        for tb in range(BLOCKS):
                            b = (m0 + 6 + tb) % RING
                            dve.wait_ge(bank_read[b], uses(m0 + 6 + tb) + 1)
                            link(nc.vector.bn_stats(stats6[:, tb, :], tile(v_act, tb)))
                            ins = nc.vector.bn_aggr(stats2[:, tb, :], stats6[:, tb, :])
                            if tb < BLOCKS - 1:
                                link(ins)
                        ins.then_inc(v_var, 1)
                    if w == 5:
                        dve.wait_ge(v_std, 1)
                        link(nc.vector.reciprocal(sgu_rstd[:, :], sgu_std[:, :]))
                        for tb in range(BLOCKS):
                            v = tile(v_act, tb)
                            nc.vector.tensor_scalar(v, v, stats2[:, tb, 0:1], sgu_rstd[:, tb:tb + 1],
                                                    ALU.subtract, ALU.mult).then_inc(v_scaled, 1)
                    if w < UNITS // 2:
                        mask_and_max(2 * w)
                        mask_and_max(2 * w + 1)
                        normalise_probs(2 * w)
                        normalise_probs(2 * w + 1)
                    if w >= 3 and w % 2 == 1:
                        att_out((w - 3) // 2)
                for j in range(4):
                    for cp in range(2):
                        dve.wait_ge(spatial_done, 2 * j + cp + 1)
                        for g in range(2):
                            rows = slice(g * HEAD_DIM, (g + 1) * HEAD_DIM)
                            src = bank[4 + cp][rows, :].rearrange("p (c k) -> p c k", c=2)[:, :, g * P:(g + 1) * P]
                            dst = temp[rows, j % 2, cp * 2 * P:(cp + 1) * 2 * P].rearrange("p (c k) -> p c k", c=2)
                            bias = spatial_bias[rows, j * P:(j + 1) * P].unsqueeze(1).broadcast_to([HEAD_DIM, 2, P])
                            nc.vector.tensor_tensor(dst, src, bias, ALU.add).then_inc(spatial_read, 1)
                    dve.wait_ge(spatial_read, 4 * j + 4)
                    dve.wait_ge(gelu_u, j + 1)
                    nc.vector.tensor_tensor(inner[:, j % 2, :], temp[:, j % 2, :], tile(u_act, j),
                                            ALU.mult).then_inc(sgu_ready, 1)
                    dve.wait_ge(h_hi_ready, h0 + BLOCKS + j + 1)
                    nc.vector.tensor_tensor(tile(o_lo, QT + j), inner[:, j % 2, :], tile(o_hi, QT + j).bitcast(F32),
                                            ALU.subtract).then_inc(h_lo_ready, 1)

            def conv_mixer(o_hi, o_lo):
                m0, h0 = FIRST["mix", 1], H_BEFORE["mix", 1]
                for s in range(2):
                    link(nc.vector.memset(zpad[:, s * (T + 2):s * (T + 2) + 2], 0.0))
                base = chain[0]
                with dve.Fori(0, DT // 2) as i:
                    for jj in range(2):
                        n = m0 + 2 * jj
                        b = (n + 1) % RING
                        refill(n, i)
                        dve.wait_ge(bank_read[n % RING], uses(n) + 1 + i)
                        dve.wait_ge(slab_done, n + 2 + RING * i)
                        z0 = jj * (T + 2)
                        nc.vector.tensor_tensor(zpad[:, z0 + 2:z0 + 2 + T], gate[:, jj, :], bank[b][:, :],
                                                ALU.mult).then_inc(bank_read[b], 1)
                        refill(n + 1, i)
                        dve.wait_ge(bank_read[b], uses(n + 1) + 1 + i)
                        k = 2 * i + jj
                        y = tile(conv_y, k)
                        done = base + 4 * jj + 1 + 8 * i
                        nc.vector.tensor_copy(taps[:, jj, :], conv_taps[:, bass.ds(k * 3, 3)]).then_inc(dve_chain, 1)
                        dve.wait_ge(dve_chain, done)
                        for tap in range(3):
                            z = zpad[:, z0 + tap:z0 + tap + T]
                            wt = taps[:, jj, tap:tap + 1]
                            if tap == 0:
                                ins = nc.vector.tensor_scalar(y, z, wt, None, ALU.mult)
                            else:
                                ins = nc.vector.scalar_tensor_tensor(out=y, in0=z, scalar=wt, in1=y,
                                                                     op0=ALU.mult, op1=ALU.add)
                            ins.then_inc(dve_chain, 1)
                            dve.wait_ge(dve_chain, done + tap + 1)
                chain[0] += 4 * DT
                n = m0 + 2 * DT
                with dve.Fori(0, DT // RING) as i:
                    for j in range(RING):
                        b = (n + j) % RING
                        k = RING * i + j
                        dve.wait_ge(slab_done, n + j + 1 + RING * i)
                        nc.vector.tensor_tensor(inner[:, j % 2, :], tile(conv_y, k), bank[b][:, :],
                                                ALU.mult).then_inc(bank_read[b], 1)
                        refill(n + j, i)
                        dve.wait_ge(h_hi_ready, h0 + j + 1 + RING * i)
                        nc.vector.tensor_tensor(tile(o_lo, k), inner[:, j % 2, :], tile(o_hi, k).bitcast(F32),
                                                ALU.subtract).then_inc(h_lo_ready, 1)

            def ple_gates(layer):
                n0 = FIRST["ple_gate", layer]
                for d in range(DT):
                    n = n0 + d
                    dve.wait_ge(bank_read[n % RING], uses(n) + 1)
                    if d == 0:
                        dve.wait_ge(ple_read, DT * (layer + 1))
                    link(nc.vector.tensor_tensor(temp[:, d % 2, :], tile(ple, d), gate[:, d % 2, :], ALU.mult))
                    nc.vector.tensor_tensor(tile(xf, d), tile(xf, d), temp[:, d % 2, :],
                                            ALU.add).then_inc(mixed_in, 1)
                    refill(n)

            for layer in range(DEPTH):
                o_hi, o_lo = (b_hi, b_lo) if layer == 0 else (a_hi, a_lo)
                ffn(layer, 0, o_hi, o_lo)
                final_products(3 * layer, FIRST["down", layer, 0, 2], False, None)
                normalise(layer, 0, FIRST["mix", layer] - 1)
                if layer == 0:
                    attention_mixer(o_hi, o_lo)
                else:
                    conv_mixer(o_hi, o_lo)
                final_products(3 * layer + 1, FIRST["mix_out", layer], True, ALPHA)
                normalise(layer, 1, FIRST["up", layer, 1, 0] - 1)
                ffn(layer, 1, o_hi, o_lo)
                final_products(3 * layer + 2, FIRST["down", layer, 1, 2], False, None)
                normalise(layer, 2, FIRST["ple_proj", layer] - 1)
                ple_gates(layer)

        @block.tensor
        def _(pe):
            X_SPLIT, H_SPLIT = (x_hi_ready, x_lo_ready), (h_hi_ready, h_lo_ready)

            def keep_warm(count):
                for _ in range(count):
                    nc.tensor.matmul(bank[5][:, :], warm_rhs[:, 0:P], warm_rhs[:, :], start=True, stop=True)

            def three_passes(out, w0, hi0, lo0, x_hi, x_lo, start, stop):
                s, c = w0
                nc.tensor.matmul(out, w_hi[:, s, c], x_hi, start=start, stop=False)
                nc.tensor.matmul(out, w_hi[:, s, c], x_lo, start=False, stop=False)
                return nc.tensor.matmul(out, w_lo[:, s, c], x_hi, start=False, stop=stop)

            def wait_slab(n, i=0):
                pe.wait_ge(lo_ready, n + 1 + RING * i)
                if uses(n) > 0:
                    pe.wait_ge(bank_read[n % RING], uses(n) + i)

            def tile_product(n, k, tiles, hi, lo):
                return three_passes(bank[n % RING][:, :], (n % RING, slice(k * P, (k + 1) * P)), None, None,
                                    tile(hi, k), tile(lo, k), k == 0, k == tiles - 1)

            def slab(n, hi, lo, tiles=DT, i=0, ready=None, midway=None):
                wait_slab(n, i)
                for k in range(tiles):
                    if midway is not None and k == tiles - 2:
                        midway()
                    if ready is not None:
                        pe.wait_ge(h_lo_ready, ready(k))
                    last = tile_product(n, k, tiles, hi, lo)
                last.then_inc(slab_done, 1)

            def slabs_by_tile(n, signals, ready, hi, lo):
                for m in range(n, n + HEAD):
                    if n > 0:
                        wait_slab(m)
                for k in range(DT + 1):
                    if n == 0 and k == 0:
                        pe.wait_ge(head_lo, HEAD)
                    if n == 0 and k == DT // 2:
                        pe.wait_ge(lo_ready, HEAD)
                    if k < DT:
                        pe.wait_ge(signals[0], ready(k))
                        for m in range(n, n + HEAD):
                            s, c = m % RING, slice(k * P, (k + 1) * P)
                            nc.tensor.matmul(bank[s][:, :], w_hi[:, s, c], tile(hi, k), start=(k == 0), stop=False)
                            nc.tensor.matmul(bank[s][:, :], w_lo[:, s, c], tile(hi, k), start=False, stop=False)
                    if k > 0:
                        pe.wait_ge(signals[1], ready(k - 1))
                        for m in range(n, n + HEAD):
                            s, c = m % RING, slice((k - 1) * P, k * P)
                            last = nc.tensor.matmul(bank[s][:, :], w_hi[:, s, c], tile(lo, k - 1), start=False,
                                                    stop=(k == DT))
                            if k == DT:
                                last.then_inc(slab_done, 1)

            def ffn(layer, half, refresh, x, o):
                for g, ft in enumerate(FT_GROUPS):
                    n, h = FIRST["up", layer, half, g], H_BEFORE[layer, half, g]
                    steps = ft // 2
                    if g == 0:
                        slabs_by_tile(n, X_SPLIT, lambda k: DT * refresh + k + 1, *x)
                        slab(n + 3, *x)
                        n += RING
                        steps -= 1
                    with pe.Fori(0, steps) as i:
                        for j in range(RING):
                            slab(n + j, *x, i=i)
                    n = FIRST["down", layer, half, g]
                    if g == len(FT_GROUPS) - 1:
                        final_slabs(3 * layer + 2 * half, n, *o, ft, lambda k: h + k + 1)
                        continue
                    with pe.Fori(0, DT // RING) as i:
                        for j in range(RING):
                            slab(n + j, *o, tiles=ft, i=i, ready=(lambda k: h + k + 1) if j == 0 else None)

            def add_statistics(norm, src, which, start, stop):
                for tb in range(BLOCKS):
                    last = nc.tensor.matmul(bank[6 + which][:, tb:tb + 1], src[:, tb * P:(tb + 1) * P],
                                            mean_col[:, 0:1], start=start and tb == 0, stop=stop,
                                            skip_group_check=True)
                return last

            def last_slab(norm, n7, hi, lo, tiles=DT):
                def midway():
                    pe.wait_ge(const_ready, 5)
                    pe.wait_ge(sums_ready, 12 * norm + 12)
                    add_statistics(norm, sum_z[:, :], 0, True, False)
                    add_statistics(norm, sum_q[:, :], 1, True, False)
                slab(n7, hi, lo, tiles=tiles, midway=midway)

            def finish_statistics(norm, n7, warm):
                pe.wait_ge(bank_read[n7 % RING], uses(n7) + 1)
                add_statistics(norm, tile(xf, DT - 1), 0, False, True).then_inc(mean_ready, 1)
                pe.wait_ge(square_ready, DT * (norm + 1))
                add_statistics(norm, square[:, 1, :], 1, False, True).then_inc(meansq_ready, 1)

            def spread(norm, which):
                pe.wait_ge(diag_ready, 2 * norm + which + 1)
                nc.tensor.matmul(bank[6 + which][:, :], ones[:, :], square[:, which, :], start=True,
                                 stop=True).then_inc(spread_ready, 1)

            def norm_alone(norm, n7):
                keep_warm(3)
                finish_statistics(norm, n7, True)
                keep_warm(3)
                spread(norm, 0)
                keep_warm(3)
                spread(norm, 1)
                keep_warm(7)

            def final_slabs(norm, n, hi, lo, tiles, ready=None):
                for j in range(DT - 1):
                    slab(n + j, hi, lo, tiles=tiles, ready=ready if j == 0 else None)
                last_slab(norm, n + DT - 1, hi, lo, tiles)

            def attention_mixer(refresh, x, o):
                m0, h0 = FIRST["mix", 0], H_BEFORE["mix", 0]
                vz4 = vz.rearrange("p (g n c) -> p g n c", g=2, n=BLOCKS)

                def rotate(r):
                    n = m0 + r
                    pe.wait_ge(bank_read[n % RING], uses(n) + 1)
                    if r >= 2:
                        pe.wait_ge(rot_ready, r - 1)
                    src = tile(q, r) if r < QT else square[:, 0, :]
                    nc.tensor.matmul(bank[4 + r % 2][:, :], rotT, src, start=True, stop=True).then_inc(rot_done, 1)

                def turn_v():
                    pe.wait_ge(bank_read[(m0 + 5) % RING], uses(m0 + 5) + 1)
                    for n in range(BLOCKS):
                        last = nc.tensor.transpose(bank[6][:, n * P:(n + 1) * P], gate[:, 0, n * P:(n + 1) * P], ident)
                    last.then_inc(v_turned, 1)

                def sgu_v_slab(r):
                    n = m0 + 6 + r
                    if r == 0:
                        for tb in range(BLOCKS):
                            pe.wait_ge(bank_read[(n + tb) % RING], uses(n + tb))
                    pe.wait_ge(lo_ready, n + 1)
                    for kk in range(2):
                        k = 2 * r + kk
                        whi = w_hi[:, n % RING, kk * T:(kk + 1) * T]
                        wlo = w_lo[:, n % RING, kk * T:(kk + 1) * T]
                        for tb in range(BLOCKS):
                            out = bank[(m0 + 6 + tb) % RING][:, :]
                            c = slice(k * T + tb * P, k * T + (tb + 1) * P)
                            nc.tensor.matmul(out, x[0][:, c], whi, start=(k == 0), stop=False)
                            nc.tensor.matmul(out, x[0][:, c], wlo, start=False, stop=False)
                            last = nc.tensor.matmul(out, x[1][:, c], whi, start=False, stop=(k == DT - 1))
                    last.then_inc(slab_done, 1)

                def scores(u):
                    n, j = u // QT, u % QT
                    if u == 0:
                        pe.wait_ge(rot_ready, QT + 2)
                    if u >= 2:
                        pe.wait_ge(scores_read, u - 1)
                    for g in range(2):
                        k0, k1 = max(n - 1, 0) * P, (n + 1) * P
                        out = bank[4 + u % 2][:, (g + 1) * 2 * P - (k1 - k0):(g + 1) * 2 * P]
                        last = nc.tensor.matmul(out, q[:, j * T + n * P:j * T + (n + 1) * P],
                                                kz[:, g * T + k0:g * T + k1], start=True, stop=True)
                    last.then_inc(scores_done, 1)

                def turn_probs(u):
                    pe.wait_ge(probs_ready, u + 1)
                    if u > 0:
                        pe.wait_ge(probsT_ready, u)
                    else:
                        pe.wait_ge(vz_ready, 2)
                    e = tile(probs, u % 2)
                    for g in range(2):
                        for kb in range(1 if u < QT else 0, 2):
                            c = slice((2 * g + kb) * P, (2 * g + kb + 1) * P)
                            last = nc.tensor.transpose(bank[6][:, c], e[:, c], ident)
                    last.then_inc(turned, 1)

                def weighted_values(u):
                    n, j = u // QT, u % QT
                    pe.wait_ge(probsT_ready, u + 1)
                    if j == 0 and n > 0:
                        pe.wait_ge(h_lo_ready, h0 + n)
                    parts = [(g, kb) for g in range(2) for kb in range(1 if n == 0 else 0, 2)]
                    for g, kb in parts:
                        c = slice((2 * g + kb) * P, (2 * g + kb + 1) * P)
                        last = nc.tensor.matmul(bank[7][:, j * P:(j + 1) * P], vz4[:, g, n - 1 + kb, :],
                                                tile(probsT, u % 2)[:, c], start=(g, kb) == parts[0],
                                                stop=(g, kb) == parts[-1])
                    last.then_inc(pv_done, 1)

                slabs_by_tile(m0, X_SPLIT, lambda k: DT * refresh + k + 1, *x)
                slab(m0 + 3, *x)
                rotate(0)
                rotate(1)
                slab(m0 + 4, *x)
                rotate(2)
                rotate(3)
                slab(m0 + 5, *x)
                rotate(4)
                turn_v()
                for w in range(UNITS // 2 + 2):
                    if w < 4:
                        sgu_v_slab(w)
                    elif w < 8:
                        slab(m0 + 6 + w, *x)
                    for u in (2 * w, 2 * w + 1):
                        if u < UNITS:
                            scores(u)
                        if 2 <= u < UNITS + 2:
                            turn_probs(u - 2)
                        if u >= 4:
                            weighted_values(u - 4)
                pe.wait_ge(v_normed, BLOCKS)
                for j in range(4):
                    for cp in range(2):
                        if j > 0:
                            pe.wait_ge(spatial_read, 4 * (j - 1) + 2 * cp + 2)
                        for cc in range(2):
                            c = 2 * cp + cc
                            last = nc.tensor.matmul(bank[4 + cp][:, cc * 2 * P:(cc + 1) * 2 * P],
                                                    v_act[:, c * T + j * P:c * T + (j + 1) * P],
                                                    spatial[:, 2 * j * P:(2 * j + 2) * P], start=True, stop=True)
                        last.then_inc(spatial_done, 1)
                n = FIRST["mix_out", 0]
                slabs_by_tile(n, H_SPLIT, lambda k: h0 + BLOCKS + max(0, k - QT + 1), *o)
                for d in range(3, DT - 1):
                    slab(n + d, *o)
                last_slab(1, n + DT - 1, *o)

            def conv_mixer(refresh, x, o):
                n, h0 = FIRST["mix", 1], H_BEFORE["mix", 1]
                slabs_by_tile(n, X_SPLIT, lambda k: DT * refresh + k + 1, *x)
                slab(n + 3, *x)
                with pe.Fori(0, (3 * DT - RING) // RING) as i:
                    for j in range(RING):
                        slab(n + RING + j, *x, i=i)
                n = FIRST["mix_out", 1]
                final_slabs(4, n, *o, DT, lambda k: h0 + k + 1)

            def ple_products(layer, half_slab, p):
                n = FIRST["ple_proj", layer] + half_slab
                c = 4 * half_slab + p
                if p == 0:
                    pe.wait_ge(lo_ready, n + 1)
                    pe.wait_ge(p_lo_ready, layer + 1)
                done = DT * layer + c
                if done >= 2:
                    pe.wait_ge(ple_read, done - 1)
                for k in range(PLE_T):
                    last = three_passes(bank[4 + c % 2][:, :],
                                        (n % RING, slice((2 * p + k) * P, (2 * p + k + 1) * P)), None, None,
                                        tile(p_hi, k), tile(p_lo, k), k == 0, k == PLE_T - 1)
                last.then_inc(slab_done if p == 3 else ple_done, 1)

            for layer in range(DEPTH):
                a, b = ((a_hi, a_lo), (b_hi, b_lo)) if layer == 0 else ((b_hi, b_lo), (a_hi, a_lo))
                ffn(layer, 0, 0 if layer == 0 else X_OF["ple"], a, b)
                norm_alone(3 * layer, FIRST["mix", layer] - 1)
                (attention_mixer if layer == 0 else conv_mixer)(X_OF[layer, 0], a, b)
                norm_alone(3 * layer + 1, FIRST["up", layer, 1, 0] - 1)
                ffn(layer, 1, X_OF[layer, 1], a, b)
                norm = 3 * layer + 2
                ple_products(layer, 0, 0)
                finish_statistics(norm, FIRST["ple_proj", layer] - 1, False)
                ple_products(layer, 0, 1)
                spread(norm, 0)
                ple_products(layer, 0, 2)
                spread(norm, 1)
                ple_products(layer, 0, 3)
                for p in range(4):
                    ple_products(layer, 1, p)
                n = FIRST["ple_gate", layer]
                slabs_by_tile(n, X_SPLIT, lambda k: DT * X_OF[layer, 2] + k + 1, *a)
                for d in range(3, DT):
                    slab(n + d, *a)


def constants():
    c = np.zeros((P, 2 * P + 2), np.float32)
    c[:, 0:P] = np.eye(P)
    inv = np.power(np.float32(ROPE_THETA), -np.arange(ROT_HALF, dtype=np.float32) * np.float32(2.0 / (2 * ROT_HALF)))
    for base in (0, HEAD_DIM):
        for d in range(ROT_HALF):
            c[base + d + ROT_HALF, P + base + d] = -1.0
            c[base + d, P + base + d + ROT_HALF] = 1.0
            c[base + d, 2 * P] = c[base + d + ROT_HALF, 2 * P] = inv[d]
    return c


def kernel(x, p, positions, ln_g, ln_b, ffn_w_gate, ffn_w_up, ffn_w_down, ab_w_in, ab_sinks, sgu_ln_g,
           sgu_ln_b, sgu_w_s, sgu_b_s, ab_w_out, sc_w_in, sc_conv_w, sc_w_out, ple_w_proj, ple_w_gate):
    import concourse.bacc as bacc
    from concourse.bass_utils import run_bass_kernel_spmd

    def slabs(w):
        w = np.asarray(w)
        k, m = w.shape
        return w.reshape(k // P, P, m // P, P).transpose(2, 1, 0, 3).reshape(m // P, P, k)

    def feature_major(a):
        a = np.asarray(a)
        return np.ascontiguousarray(a.T.reshape(-1, P, a.shape[0]).transpose(1, 0, 2))

    wg, wu, wd = np.asarray(ffn_w_gate), np.asarray(ffn_w_up), np.asarray(ffn_w_down)
    w_up, w_down8, w_down6 = [], [], []
    for layer in range(DEPTH):
        for half in range(2):
            w_up.append(np.stack([slabs(wg[layer, half]), slabs(wu[layer, half])], 1).reshape(2 * FT, P, D))
            rows = wd[layer, half]
            w_down8 += [slabs(rows[0:8 * P]), slabs(rows[8 * P:16 * P])]
            w_down6.append(slabs(rows[16 * P:]))

    w_in = np.asarray(ab_w_in)[0]
    q_cols = w_in[:, 0:512].reshape(D, 2, QT, HEAD_DIM).transpose(0, 2, 1, 3).reshape(D, 512)
    k_cols, v_cols, su, sv = w_in[:, 512:640], w_in[:, 640:768], w_in[:, 768:1280], w_in[:, 1280:1792]
    sv_slabs = sv.reshape(4, 2, P, 512).transpose(0, 2, 1, 3).reshape(4, P, D)
    w_out = np.asarray(ab_w_out)[0]
    att_rows = w_out[0:512].reshape(2, QT, HEAD_DIM, D).transpose(1, 0, 2, 3).reshape(512, D)
    w_mix0 = np.concatenate([slabs(q_cols), slabs(k_cols), slabs(v_cols), sv_slabs, slabs(su),
                             slabs(np.concatenate([att_rows, w_out[512:]], 0))], 0)
    sc = np.asarray(sc_w_in)[0]
    w_mix1 = np.concatenate([
        np.stack([slabs(sc[:, D:2 * D]), slabs(sc[:, 2 * D:])], 1).reshape(2 * DT, P, D),
        slabs(sc[:, 0:D]), slabs(np.asarray(sc_w_out)[0])], 0)
    w_ple = np.concatenate([np.concatenate([
        slabs(np.asarray(ple_w_proj)[i]).reshape(2, 4, P, 256).transpose(0, 2, 1, 3).reshape(2, P, D),
        slabs(np.asarray(ple_w_gate)[i])], 0) for i in range(DEPTH)], 0)

    def columns(a):
        return np.asarray(a).reshape(3 * DEPTH, DT, P).transpose(2, 0, 1).reshape(P, 3 * DEPTH * DT)

    arrays = {
        "xT": feature_major(np.asarray(x)[0]),
        "pT": np.stack([feature_major(np.asarray(p)[i, 0]).reshape(P, PLE_T * T) for i in range(DEPTH)]),
        "positions": np.asarray(positions).reshape(1, T),
        "ln_gb": np.concatenate([columns(ln_g), columns(ln_b)], 1),
        "w_up": np.concatenate(w_up, 0),
        "w_down8": np.concatenate(w_down8, 0),
        "w_down6": np.concatenate(w_down6, 0),
        "w_mix0": w_mix0,
        "w_mix1": w_mix1,
        "w_ple": w_ple,
        "sinks": np.asarray(ab_sinks)[0].reshape(2, QT).T.reshape(1, HEADS),
        "sgu_gb": np.concatenate([np.asarray(sgu_ln_g)[0], np.asarray(sgu_ln_b)[0]]).reshape(1, 2 * T),
        "sgu_wT": np.asarray(sgu_w_s)[0].transpose(2, 0, 1).reshape(P, 8 * P),
        "sgu_b": np.repeat(np.asarray(sgu_b_s)[0].reshape(4, 2, 1, P), HEAD_DIM, 2).reshape(4, P, P)
                   .transpose(1, 0, 2).reshape(P, 4 * P),
        "conv_w": np.asarray(sc_conv_w)[0].reshape(3, DT, P).transpose(2, 1, 0).reshape(P, 3 * DT),
        "consts": constants(),
    }
    nc = bacc.Bacc("TRN2", target_bir_lowering=False, num_devices=1, dynamic_dma_scratch_size=1024)
    args, feed = [], {}
    for name, a in arrays.items():
        a = np.ascontiguousarray(a)
        feed[name] = a
        args.append(nc.dram_tensor(name, a.shape, mybir.dt.from_np(a.dtype), kind="ExternalInput").ap())
    args.append(nc.dram_tensor("outT", (P, DT, T), F32, kind="ExternalOutput").ap())
    build_program(nc, *args)
    got = run_bass_kernel_spmd(nc, [feed], core_ids=[0]).results[0]["outT"]
    return got.transpose(1, 0, 2).reshape(D, T).T.reshape(1, T, D)
```

```python
from contextlib import ExitStack

import concourse.bass as bass
import numpy as np
from concourse import mybir

F32 = mybir.dt.float32
F32R = mybir.dt.float32r
I32 = mybir.dt.int32
ALU = mybir.AluOpType
ACT = mybir.ActivationFunctionType
AX = mybir.AxisListType

P = 128
T = 512
TH = T // 2
D = 1024
DT = D // P
DEPTH = 2
D_FF = 2816
FT = D_FF // P
FT_GROUPS = (8, 8, 6)
PLE_T = 256 // P
RING = 4
SLAB = 8 * P
HEADS, KV_HEADS, HEAD_DIM = 8, 2, 64
QT = HEADS * HEAD_DIM // P
BLOCKS = T // P
UNITS = BLOCKS * QT
STEPS = UNITS // 2 + 2
ROT_HALF = 8
ROPE_THETA = 500000.0
ALPHA = (2 * DEPTH) ** 0.25
LN_EPS = 1e-5
MASKED = 1e30
MAGIC = 1.5 * 2.0 ** 23
TWO_PI = 2 * np.pi
HEAD = 3
X_CHUNKS = ((0, 1), (1, 2), (2, 4), (4, 8))
PIECES = ((0, 2), (2, 4), (4, 8))


def plan_slabs():
    first, aux_only, n = {}, set(), 0
    for layer in range(DEPTH):
        for half in range(2):
            for g, ft in enumerate(FT_GROUPS):
                first["up", layer, half, g] = n
                n += 2 * ft
                first["down", layer, half, g] = n
                n += DT
            if half == 0:
                first["mix", layer] = n
                n += (2 * QT + 2 + 4 if layer == 0 else 3 * DT)
                first["mix_out", layer] = n
                n += DT
        first["ple_proj", layer] = n
        aux_only |= {n, n + 1}
        n += 2
        first["ple_gate", layer] = n
        n += DT
    return first, aux_only, n


def split_two_pi():
    c1 = float(np.floor(TWO_PI * 2.0 ** 9) / 2.0 ** 9)
    rest = TWO_PI - c1
    scale = 2.0 ** (11 - np.floor(np.log2(rest)))
    c2 = float(np.floor(rest * scale) / scale)
    return c1, c2, float(TWO_PI - c1 - c2)


def build_program(nc, xT, pT, positions, ln_gb, w_up, w_down8, w_down6, w_mix0, w_mix1, w_ple,
                  sinks, sgu_gb, sgu_wT, sgu_b, conv_w, consts, outT):
    FIRST, AUX_ONLY, N_SLABS = plan_slabs()

    def uses(n):
        return sum(1 for m in range(n % RING, n, RING) if m not in AUX_ONLY)

    ctx = ExitStack()
    with ctx:
        def sb(name, shape, dt=F32):
            return ctx.enter_context(nc.sbuf_tensor(name, shape, dt))

        def sem(name):
            return ctx.enter_context(nc.semaphore(name))

        raw = sb("raw", [P, RING, SLAB])
        w_hi = sb("w_hi", [P, RING, SLAB], F32R)
        w_lo = sb("w_lo", [P, RING, SLAB], F32R)
        xf = sb("xf", [P, DT * T])
        a_hi, a_lo = sb("a_hi", [P, DT * T], F32R), sb("a_lo", [P, DT * T], F32R)
        b_hi, b_lo = sb("b_hi", [P, DT * T], F32R), sb("b_lo", [P, DT * T], F32R)
        p_hi, p_lo = sb("p_hi", [P, PLE_T * T], F32R), sb("p_lo", [P, PLE_T * T], F32R)
        gate = sb("gate", [P, 2, T])
        inner = sb("inner", [P, 2, T])
        sum_z, sum_q = sb("sum_z", [P, T]), sb("sum_q", [P, T])
        square = sb("square", [P, 2, T])
        temp = sb("temp", [P, 2, T])
        ident_rot = sb("ident_rot", [P, 2 * P + 2])
        ident, rotT, inv_freq = ident_rot[:, 0:P], ident_rot[:, P:2 * P], ident_rot[:, 2 * P:2 * P + 1]
        ones = sb("ones", [P, P])
        mean_col = sb("mean_col", [P, 2])
        eps = sb("eps", [P, 4])
        gb = sb("gb", [P, 2 * 3 * DEPTH * DT])
        small = sb("small", [P, 32])
        warm_rhs = sb("warm_rhs", [P, T], mybir.dt.bfloat16)
        warm_tile = sb("warm_tile", [P, 3])
        nsink = sb("nsink", [P, HEADS])
        conv_taps = sb("conv_taps", [P, 3 * DT])
        taps = sb("taps", [P, 2, 3])
        stats6 = sb("stats6", [P, BLOCKS, 6])
        stats2 = sb("stats2", [P, BLOCKS, 2])
        sgu_std = sb("sgu_std", [P, BLOCKS])
        sgu_rstd = sb("sgu_rstd", [P, BLOCKS])
        sm = sb("sm", [P, 2, 12])

        scratch = sb("scratch", [P, 14080])
        at = 0

        def carve(cols):
            nonlocal at
            at += cols
            return scratch[:, at - cols:at]

        q = carve(QT * T)
        kz = carve(KV_HEADS * T)
        vz = carve(KV_HEADS * BLOCKS * P)
        u_act = carve(4 * T)
        v_act = carve(BLOCKS * T)
        probs = carve(2 * T)
        probsT = carve(2 * T)
        cos, sin = carve(T), carve(T)
        spatial = carve(8 * P)
        mask = carve(2 * P)
        spatial_bias = carve(4 * P)
        sgu_gain, sgu_bias = carve(T), carve(T)
        ple = scratch[:, 0:DT * T]
        p_raw = scratch[:, 0:PLE_T * T]
        conv_y = scratch[:, 0:DT * T]
        zpad = scratch[:, DT * T:DT * T + 2 * (T + 2)]

        bank = [ctx.enter_context(nc.psum_tensor(f"bank{b}", [P, T], F32)) for b in range(8)]

        loaded = [sem(f"loaded{s}") for s in range(RING)]
        const_loaded = sem("const_loaded")
        x_loaded = [sem(f"x_loaded{c}") for c in range(len(X_CHUNKS))]
        head_loaded = [[sem(f"head_loaded{c}_{s}") for s in range(HEAD)] for c in range(2)]
        head_hi, head_lo = sem("head_hi"), sem("head_lo")
        p_loaded = sem("p_loaded")
        hi_ready, lo_ready, slab_done = sem("hi_ready"), sem("lo_ready"), sem("slab_done")
        bank_read = [sem(f"bank_read{b}") for b in range(RING)]
        h_hi_ready, h_lo_ready = sem("h_hi_ready"), sem("h_lo_ready")
        x_hi_ready, x_lo_ready = sem("x_hi_ready"), sem("x_lo_ready")
        p_hi_ready, p_lo_ready = sem("p_hi_ready"), sem("p_lo_ready")
        const_ready = sem("const_ready")
        pool_chain, dve_chain, act_chain = sem("pool_chain"), sem("dve_chain"), sem("act_chain")
        square_ready, sums_ready = sem("square_ready"), sem("sums_ready")
        mean_ready, meansq_ready = sem("mean_ready"), sem("meansq_ready")
        mean2_ready = sem("mean2_ready")
        first_product, second_read, second_square = (
            sem("first_product"), sem("second_read"), sem("second_square"))
        first_sums, second_sums = sem("first_sums"), sem("second_sums")
        first_normed, first_xf, first_hi, first_lo = (
            sem("first_normed"), sem("first_xf"), sem("first_hi"), sem("first_lo"))
        var_ready, std_ready, diag_ready = sem("var_ready"), sem("std_ready"), sem("diag_ready")
        spread_ready, normed_ready, xf_ready = sem("spread_ready"), sem("normed_ready"), sem("xf_ready")
        ple_done, ple_read, mixed_in = sem("ple_done"), sem("ple_read"), sem("mixed_in")
        angle_ready, table_ready = sem("angle_ready"), sem("table_ready")
        rot_done, rot_ready, in_phase_ready = sem("rot_done"), sem("rot_ready"), sem("in_phase_ready")
        v_turned, vz_ready = sem("v_turned"), sem("vz_ready")
        scores_done, scores_read, max_ready, exp_ready = (
            sem("scores_done"), sem("scores_read"), sem("max_ready"), sem("exp_ready"))
        probs_ready, turned, probsT_ready, pv_done = (
            sem("probs_ready"), sem("turned"), sem("probsT_ready"), sem("pv_done"))
        gelu_v, v_var, v_std, v_scaled, v_normed = (
            sem("gelu_v"), sem("v_var"), sem("v_std"), sem("v_scaled"), sem("v_normed"))
        gelu_u, spatial_done, spatial_read, sgu_ready = (
            sem("gelu_u"), sem("spatial_done"), sem("spatial_read"), sem("sgu_ready"))
        out_stored = sem("out_stored")

        def tile(buf, k):
            return buf[:, bass.ds(k * T, T)] if not isinstance(k, int) else buf[:, k * T:(k + 1) * T]

        H_BEFORE, count = {}, 0
        for layer in range(DEPTH):
            for half in range(2):
                for g, ft in enumerate(FT_GROUPS):
                    H_BEFORE[layer, half, g] = count
                    count += ft
                if half == 0:
                    H_BEFORE["mix", layer] = count
                    count += DT
        X_OF = {"load": 0, (0, 0): 1, (0, 1): 2, (0, 2): 3, "ple": 4, (1, 0): 5, (1, 1): 6, (1, 2): 7}
        NORM_OF = {X_OF[layer, which]: 3 * layer + which for layer in range(DEPTH) for which in range(3)}

        WHOLE, FIRST_HALF, SECOND_HALF = None, 0, 1
        CHAIN = [5 * (norm // 3) + 2 * (norm % 3) for norm in range(3 * DEPTH)]

        def halved(layer, which):
            return 2 * layer + which

        def part_of(part, width=T):
            return slice(0, width) if part is WHOLE else slice(part * width // 2, (part + 1) * width // 2)

        def tile_part(buf, k, part):
            c = part_of(part)
            return buf[:, k * T + c.start:k * T + c.stop]

        def statistics_bank(which, part):
            if part is SECOND_HALF:
                return bank[5][:, 8 * which:8 * which + BLOCKS // 2]
            return bank[6 + which][:, part_of(part, BLOCKS)]

        def spread_bank(which, part):
            return bank[(4 if part is SECOND_HALF else 6) + which][:, part_of(part)]

        block = ctx.enter_context(nc.Block())

        @block.sync
        def _(sp):
            def load(n, src, i=0):
                s = n % RING
                if n >= RING:
                    sp.wait_ge(hi_ready, n - RING + 1 + RING * i)
                    sp.wait_ge(lo_ready, n - RING + 1 + RING * i)
                sp.dma_start(raw[:, s, 0:src.shape[-1]], src).then_inc(loaded[s], 16)

            def load_x(c):
                d0, d1 = X_CHUNKS[c]
                sp.dma_start(xf[:, d0 * T:d1 * T], xT[:, d0:d1, :].rearrange("p d t -> p (d t)")).then_inc(x_loaded[c], 16)

            def load_run(n, slabs, src_of):
                start = 0
                if n == 0:
                    load_x(0)
                    for c, (k0, k1) in enumerate(PIECES):
                        for j in range(HEAD):
                            signal = head_loaded[c][j] if c < 2 else loaded[j]
                            sp.dma_start(raw[:, j, k0 * P:k1 * P], src_of(j)[:, k0 * P:k1 * P]).then_inc(signal, 16)
                        load_x(c + 1)
                    load(HEAD, src_of(HEAD))
                    start = RING
                steps = (slabs - start) // RING
                with sp.Fori(0, steps) as i:
                    for j in range(RING):
                        load(n + start + j, src_of(i * RING + start + j), i)
                for j in range(start + steps * RING, slabs):
                    load(n + j, src_of(j))

            for layer in range(DEPTH):
                for half in range(2):
                    f = 2 * layer + half
                    for g, ft in enumerate(FT_GROUPS):
                        load_run(FIRST["up", layer, half, g], 2 * ft,
                                 lambda j, b=f * 2 * FT + 16 * g: w_up[b + j])
                        if half == 1 and g == 0:
                            sp.wait_ge(x_lo_ready, DT * (X_OF[layer, 1] + 1))
                            sp.dma_start(p_raw, pT[layer]).then_inc(p_loaded, 16)
                        if g < 2:
                            load_run(FIRST["down", layer, half, g], DT,
                                     lambda j, b=(f * 2 + g) * DT: w_down8[b + j])
                        else:
                            load_run(FIRST["down", layer, half, g], DT,
                                     lambda j, b=f * DT: w_down6[b + j])
                    if half == 0:
                        w_mix = w_mix0 if layer == 0 else w_mix1
                        load_run(FIRST["mix", layer], w_mix.shape[0], lambda j, w=w_mix: w[j])
                load_run(FIRST["ple_proj", layer], 2 + DT, lambda j, b=layer * (2 + DT): w_ple[b + j])
            for d in range(DT):
                sp.wait_ge(mixed_in, DT + d + 1)
                sp.dma_start(outT[:, d, :], tile(xf, d)).then_inc(out_stored, 16)
            sp.wait_ge(out_stored, 16 * DT)

        @block.gpsimd
        def _(pool):
            nc.gpsimd.memset(mean_col[:, :], 1.0 / D).then_inc(const_ready, 1)
            nc.gpsimd.memset(ones[:, :], 1.0).then_inc(const_ready, 1)
            nc.gpsimd.memset(warm_rhs[:, :], 1.0).then_inc(const_ready, 1)
            nc.gpsimd.memset(eps[:, 0:1], LN_EPS).then_inc(const_ready, 1)
            nc.gpsimd.memset(eps[:, 1:2], 4 * LN_EPS).then_inc(const_ready, 1)

            def split_x(refresh, d, hi, lo, part=WHOLE):
                pool.wait_ge(x_hi_ready, DT * refresh + d + 1)
                if refresh == 0:
                    for c, (d0, _) in enumerate(X_CHUNKS):
                        if d == d0:
                            pool.wait_ge(x_loaded[c], 16)
                elif refresh != X_OF["ple"]:
                    pool.wait_ge(xf_ready, DT * NORM_OF[refresh] + d + 1)
                nc.gpsimd.tensor_tensor(tile_part(lo, d, part), tile_part(xf, d, part),
                                        tile_part(hi, d, part).bitcast(F32), ALU.subtract).then_inc(x_lo_ready, 1)

            for d in range(DT):
                split_x(0, d, a_hi, a_lo)

            nc.gpsimd.memset(kz, 0.0).then_inc(const_ready, 1)
            nc.gpsimd.memset(vz, 0.0).then_inc(const_ready, 1)
            nc.gpsimd.memset(mask, 0.0).then_inc(pool_chain, 1)
            pool.wait_ge(pool_chain, 1)
            nc.gpsimd.affine_select(out=mask[:, 0:P], in_=mask[:, 0:P], compare_op=ALU.is_gt, fill=MASKED,
                                    base=0, pattern=[[1, P]], channel_multiplier=-1).then_inc(const_ready, 1)
            nc.gpsimd.affine_select(out=mask[:, P:2 * P], in_=mask[:, P:2 * P], compare_op=ALU.is_ge,
                                    fill=MASKED, base=0, pattern=[[-1, P]],
                                    channel_multiplier=1).then_inc(const_ready, 1)
            pool.wait_ge(const_loaded, 16 * 8)
            spatial3 = spatial.rearrange("p (g t) -> p g t", g=8)
            nc.gpsimd.affine_select(out=spatial3, in_=spatial3, compare_op=ALU.is_ge, fill=0.0, base=0,
                                    pattern=[[0, 8], [1, P]], channel_multiplier=-1).then_inc(const_ready, 1)

            def beside_norm(layer, which, n7):
                m, norm, hn = n7 - 1 + RING, 3 * layer + which, halved(layer, which)
                pool.wait_ge(hi_ready, m + 1)
                pool.wait_ge(lo_ready, m)
                nc.gpsimd.tensor_tensor(w_lo[:, m % RING, :], raw[:, m % RING, :],
                                        w_hi[:, m % RING, :].bitcast(F32), ALU.subtract).then_inc(lo_ready, 1)
                pool.wait_ge(sums_ready, 12 * norm + 12)
                pool.wait_ge(second_read, hn + 1)
                nc.gpsimd.tensor_tensor(sum_z[:, TH:T], sum_z[:, TH:T], tile(xf, DT - 1)[:, TH:T],
                                        ALU.add).then_inc(second_sums, 1)
                pool.wait_ge(second_square, hn + 1)
                nc.gpsimd.tensor_tensor(sum_q[:, TH:T], sum_q[:, TH:T], square[:, 1, TH:T],
                                        ALU.add).then_inc(second_sums, 1)

            def norm_part(layer, which, hi, lo):
                if which < 2:
                    beside_norm(layer, which, FIRST["mix", layer] - 1 if which == 0 else FIRST["up", layer, 1, 0] - 1)
                    for d in range(DT):
                        done = DT * halved(layer, which) + d + 1
                        pool.wait_ge(first_hi, done)
                        pool.wait_ge(first_xf, done)
                        nc.gpsimd.tensor_tensor(tile_part(lo, d, FIRST_HALF), tile_part(xf, d, FIRST_HALF),
                                                tile_part(hi, d, FIRST_HALF).bitcast(F32),
                                                ALU.subtract).then_inc(first_lo, 1)
                for d in range(DT):
                    split_x(X_OF[layer, which], d, hi, lo, WHOLE if which == 2 else SECOND_HALF)

            def mixer_part():
                m0 = FIRST["mix", 0]
                pool.wait_ge(table_ready, 2)
                for r in (3, QT):
                    pool.wait_ge(bank_read[(m0 + r) % RING], uses(m0 + r) + 1)
                    nc.gpsimd.tensor_tensor(inner[:, r - 3, :], tile(q, r) if r < QT else square[:, 0, :], cos,
                                            ALU.mult).then_inc(in_phase_ready, 1)
                for tb in range(BLOCKS):
                    v = tile(v_act, tb)
                    pool.wait_ge(v_scaled, tb + 1)
                    nc.gpsimd.tensor_tensor(v, v, sgu_gain, ALU.mult).then_inc(pool_chain, 1)
                    pool.wait_ge(pool_chain, 2 + tb)
                    nc.gpsimd.tensor_tensor(v, v, sgu_bias, ALU.add).then_inc(v_normed, 1)

            for layer in range(DEPTH):
                x_hi, x_lo, o_hi, o_lo = (a_hi, a_lo, b_hi, b_lo) if layer == 0 else (b_hi, b_lo, a_hi, a_lo)
                norm_part(layer, 0, x_hi, x_lo)
                if layer == 0:
                    mixer_part()
                norm_part(layer, 1, x_hi, x_lo)
                norm_part(layer, 2, x_hi, x_lo)
                if layer == 0:
                    for d in range(DT):
                        split_x(X_OF["ple"], d, o_hi, o_lo)

        @block.scalar
        def _(act):
            def split_chunk(c):
                act.wait_ge(x_loaded[c], 16)
                for d in range(*X_CHUNKS[c]):
                    nc.scalar.activation(tile(a_hi, d), tile(xf, d), ACT.Copy).then_inc(x_hi_ready, 1)

            act.wait_ge(const_ready, 2)
            nc.scalar.activation(warm_tile[:, 0:1], mean_col[:, 0:1], ACT.Copy)
            split_chunk(0)
            for c, (k0, k1) in enumerate(PIECES):
                for j in range(HEAD):
                    act.wait_ge(head_loaded[c][j] if c < 2 else loaded[j], 16)
                    nc.scalar.activation(w_hi[:, j, k0 * P:k1 * P], raw[:, j, k0 * P:k1 * P],
                                         ACT.Copy).then_inc(head_hi if c < 2 else hi_ready, 1)
                split_chunk(c + 1)
            act.wait_ge(loaded[HEAD], 16)
            nc.scalar.activation(w_hi[:, HEAD, :], raw[:, HEAD, :], ACT.Copy).then_inc(hi_ready, 1)
            act.dma_start(ident_rot[:, :], consts).then_inc(const_loaded, 16)
            act.dma_start(gb[:, :], ln_gb).then_inc(const_loaded, 16)
            act.dma_start(spatial, sgu_wT).then_inc(const_loaded, 16)
            act.dma_start(spatial_bias, sgu_b).then_inc(const_loaded, 16)
            act.dma_start(scratch[:, 14080 - 2 * T:14080], sgu_gb.broadcast_to([P, 2 * T])).then_inc(const_loaded, 16)
            act.dma_start(nsink[:, :], sinks.broadcast_to([P, HEADS])).then_inc(const_loaded, 16)
            act.dma_start(conv_taps[:, :], conv_w).then_inc(const_loaded, 16)
            act.dma_start(q[:, 0:T].bitcast(I32), positions.broadcast_to([P, T])).then_inc(const_loaded, 16)

            def warm(func):
                nc.scalar.activation(warm_tile[:, 1:2], mean_col[:, 0:1], func)

            def refill(n, i=0):
                m = n + RING
                if m < N_SLABS:
                    act.wait_ge(loaded[m % RING], 16 * (m // RING + 1) + 16 * i)
                    nc.scalar.activation(w_hi[:, m % RING, :], raw[:, m % RING, :], ACT.Copy).then_inc(hi_ready, 1)

            act.wait_ge(const_ready, 5)
            warm(ACT.Silu)

            def up_pair(n, jj, h_tile, i=0):
                b = n % RING
                act.wait_ge(slab_done, n + 1 + RING * i)
                nc.scalar.activation(gate[:, jj, :], bank[b][:, :], ACT.Silu).then_inc(bank_read[b], 1)
                refill(n, i)
                act.wait_ge(slab_done, n + 2 + RING * i)
                refill(n + 1, i)
                act.wait_ge(bank_read[(n + 1) % RING], uses(n + 1) + 1 + i)
                nc.scalar.activation(h_tile, inner[:, jj, :], ACT.Copy).then_inc(h_hi_ready, 1)

            def ffn(layer, half, o_hi):
                for g, ft in enumerate(FT_GROUPS):
                    n = FIRST["up", layer, half, g]
                    with act.Fori(0, ft // 2) as i:
                        for jj in range(2):
                            up_pair(n + 2 * jj, jj, tile(o_hi, 2 * i + jj), i)
                    if g < 2:
                        n = FIRST["down", layer, half, g]
                        with act.Fori(0, DT // RING) as i:
                            for j in range(RING):
                                act.wait_ge(slab_done, n + j + 1 + RING * i)
                                refill(n + j, i)
                    if layer == 0 and half == 0 and g == 0:
                        act.wait_ge(angle_ready, 1)
                        nc.scalar.activation(sin, temp[:, 0, :], ACT.Sin).then_inc(table_ready, 1)
                        nc.scalar.activation(cos, temp[:, 1, :], ACT.Sin).then_inc(table_ready, 1)
                        warm(ACT.Silu)
                    if half == 1 and g == 0:
                        act.wait_ge(p_loaded, 16 * (layer + 1))
                        nc.scalar.activation(p_hi[:, :], p_raw, ACT.Copy).then_inc(p_hi_ready, 1)

            def final_products(norm, n0, part):
                warm(ACT.Sqrt)
                for d in range(DT):
                    cols = part_of(part if d == DT - 1 else WHOLE)
                    n = n0 + d
                    if d >= 2:
                        act.wait_ge(sums_ready, 12 * norm + 2 * max(1, d - 2))
                    act.wait_ge(bank_read[n % RING], uses(n) + 1)
                    nc.scalar.activation(square[:, d % 2, cols], tile(xf, d)[:, cols],
                                         ACT.Square).then_inc(square_ready, 1)
                    if d < DT - 1:
                        refill(n)

            def deviation(norm, part, scale):
                c = CHAIN[norm] + (part or 0)
                cols = part_of(part, BLOCKS)
                act.wait_ge(var_ready, c + 1)
                nc.scalar.activation(small[:, 8:12][:, cols], small[:, 4:8][:, cols], ACT.Sqrt,
                                     bias=eps[:, scale:scale + 1]).then_inc(std_ready, 1)

            def gain_and_bias(norm, d, hi, part, signals):
                c, g0 = norm * DT + d, 3 * DEPTH * DT
                for dst, signal in ((tile_part(hi, d, part), signals[0]), (tile_part(xf, d, part), signals[1])):
                    nc.scalar.activation(dst, temp[:, d % 2, part_of(part)], ACT.Identity, scale=gb[:, c:c + 1],
                                         bias=gb[:, g0 + c:g0 + c + 1]).then_inc(signal, 1)

            def normalise(layer, which, scale, hi, next_func, extra):
                norm = 3 * layer + which
                deviation(norm, WHOLE, scale)
                extra(-2)
                warm(next_func)
                extra(-1)
                for d in range(DT):
                    act.wait_ge(normed_ready, norm * DT + d + 1)
                    gain_and_bias(norm, d, hi, WHOLE, (x_hi_ready, xf_ready))
                    extra(d)

            def normalise_halves(layer, which, scale, hi, next_func, n7):
                norm, hn = 3 * layer + which, halved(layer, which)
                deviation(norm, FIRST_HALF, scale)
                act.wait_ge(slab_done, n7 + 1)
                refill(n7)
                act.wait_ge(second_read, hn + 1)
                nc.scalar.activation(square[:, 1, TH:T], tile(xf, DT - 1)[:, TH:T],
                                     ACT.Square).then_inc(second_square, 1)
                for d in range(DT):
                    act.wait_ge(first_normed, hn * DT + d + 1)
                    gain_and_bias(norm, d, hi, FIRST_HALF, (first_hi, first_xf))
                    if d == 3:
                        deviation(norm, SECOND_HALF, scale)
                for d in range(DT):
                    act.wait_ge(normed_ready, norm * DT + d + 1)
                    gain_and_bias(norm, d, hi, SECOND_HALF, (x_hi_ready, xf_ready))
                warm(next_func)

            def attention_mixer(o_hi):
                m0 = FIRST["mix", 0]

                def take(n, dst, func=ACT.Copy):
                    act.wait_ge(slab_done, n + 1)
                    nc.scalar.activation(dst, bank[n % RING][:, :], func).then_inc(bank_read[n % RING], 1)

                def exps(u):
                    lo = P if u < QT else 0
                    par = u % 2
                    act.wait_ge(max_ready, u + 1)
                    for g in range(2):
                        c = slice(g * 2 * P + lo, (g + 1) * 2 * P)
                        nc.scalar.activation(tile(probs, par)[:, c], inner[:, par, c], ACT.Exp, scale=-1.0,
                                             bias=sm[:, par, 2 + g:3 + g],
                                             accum_out=sm[:, par, 6 + g:7 + g]).then_inc(act_chain, 1)
                    nc.scalar.activation(sm[:, par, 8:10], sm[:, par, 4:6], ACT.Exp).then_inc(act_chain, 1)
                    act.wait_ge(act_chain, 3 * u + 3)
                    nc.scalar.activation(warm_tile[:, 2:3], mean_col[:, 0:1], ACT.Copy).then_inc(exp_ready, 1)

                def turned_out(u):
                    act.wait_ge(turned, u + 1)
                    if u >= 2:
                        act.wait_ge(pv_done, u - 1)
                    lo = P if u < QT else 0
                    src = bank[6][:, :].rearrange("p (g k) -> p g k", g=2)[:, :, lo:]
                    dst = tile(probsT, u % 2).rearrange("p (g k) -> p g k", g=2)[:, :, lo:]
                    nc.scalar.activation(dst, src, ACT.Copy).then_inc(probsT_ready, 1)

                def att_out(n):
                    act.wait_ge(pv_done, QT * (n + 1))
                    dst = o_hi[:, 0:QT * T].rearrange("p (j t) -> p j t", j=QT)[:, :, n * P:(n + 1) * P]
                    src = bank[7][:, :].rearrange("p (j t) -> p j t", j=QT)
                    nc.scalar.activation(dst, src, ACT.Copy).then_inc(h_hi_ready, 1)

                for j in range(QT):
                    take(m0 + j, tile(q, j))
                    refill(m0 + j)
                take(m0 + 4, square[:, 0, :])
                refill(m0 + 4)
                for w in range(STEPS):
                    n = m0 + 5 + w
                    if 1 <= w <= UNITS // 2:
                        turned_out(2 * w - 2)
                    if w == 0:
                        take(n, gate[:, 0, :])
                    if w == 4:
                        act.wait_ge(slab_done, n + 1)
                        b = (m0 + 6) % RING
                        nc.scalar.activation(tile(v_act, 0), bank[b][:, :], ACT.Copy).then_inc(bank_read[b], 1)
                    if 5 <= w < 9:
                        take(n, tile(u_act, w - 5))
                    if w < 9:
                        act.wait_ge(slab_done, n + 1)
                        refill(n)
                    if w == 0:
                        act.wait_ge(v_turned, 1)
                        act.wait_ge(const_ready, 7)
                        vz4 = vz.rearrange("p (g n c) -> p g n c", g=2, n=BLOCKS)
                        src = bank[6][:, :].rearrange("p (n c) -> p n c", n=BLOCKS)
                        for g in range(2):
                            c = slice(g * HEAD_DIM, (g + 1) * HEAD_DIM)
                            nc.scalar.activation(vz4[:, g, :, c], src[:, :, c], ACT.Copy).then_inc(vz_ready, 1)
                    for u in (2 * w, 2 * w + 1):
                        if u % 2 == 1 and 2 <= u < UNITS + 2:
                            turned_out(u - 2)
                        if u < UNITS:
                            exps(u)
                    if w == 4:
                        act.wait_ge(bank_read[(m0 + 6) % RING], uses(m0 + 6) + 1)
                        nc.scalar.activation(tile(v_act, 0), tile(v_act, 0), ACT.Gelu_apprx_tanh).then_inc(gelu_v, 1)
                        for tb in range(1, BLOCKS):
                            b = (m0 + 6 + tb) % RING
                            nc.scalar.activation(tile(v_act, tb), bank[b][:, :],
                                                 ACT.Gelu_apprx_tanh).then_inc(bank_read[b], 1)
                    if w >= 3 and w % 2 == 1:
                        att_out((w - 3) // 2)
                    if w == 5:
                        act.wait_ge(v_var, 1)
                        nc.scalar.activation(sgu_std[:, :], stats2[:, :, 1], ACT.Sqrt,
                                             bias=eps[:, 0:1]).then_inc(v_std, 1)
                    if w >= UNITS // 2:
                        for j in (0, 1) if w == UNITS // 2 else (2, 3):
                            act.wait_ge(bank_read[(m0 + 10 + j) % RING], uses(m0 + 10 + j) + 1)
                            nc.scalar.activation(tile(u_act, j), tile(u_act, j),
                                                 ACT.Gelu_apprx_tanh).then_inc(gelu_u, 1)
                for j in range(4):
                    act.wait_ge(sgu_ready, j + 1)
                    nc.scalar.activation(tile(o_hi, QT + j), inner[:, j % 2, :], ACT.Copy).then_inc(h_hi_ready, 1)

            def conv_mixer(o_hi):
                m0 = FIRST["mix", 1]

                def gate_and_z(n, i=0):
                    for jj in range(2):
                        g = n + 2 * jj
                        act.wait_ge(slab_done, g + 1 + RING * i)
                        act.wait_ge(bank_read[(g + 1) % RING], uses(g + 1) + i)
                        nc.scalar.activation(gate[:, jj, :], bank[g % RING][:, :],
                                             ACT.Copy).then_inc(bank_read[g % RING], 1)
                        refill(g, i)
                        act.wait_ge(slab_done, g + 2 + RING * i)
                        refill(g + 1, i)

                with act.Fori(0, DT // 2) as i:
                    gate_and_z(m0, i)
                n = m0 + 2 * DT
                with act.Fori(0, DT // RING) as i:
                    for j in range(RING):
                        act.wait_ge(slab_done, n + j + 1 + RING * i)
                        refill(n + j, i)
                        act.wait_ge(bank_read[(n + j) % RING], uses(n + j) + 1 + i)
                        nc.scalar.activation(tile(o_hi, RING * i + j), inner[:, j % 2, :],
                                             ACT.Copy).then_inc(h_hi_ready, 1)

            def ple_step(layer):
                pp0 = FIRST["ple_proj", layer]

                def take(p):
                    if p % 4 == 3:
                        act.wait_ge(slab_done, pp0 + p // 4 + 1)
                    else:
                        act.wait_ge(ple_done, 6 * layer + 3 * (p // 4) + p % 4 + 1)
                    nc.scalar.activation(tile(ple, p), bank[4 + p % 2][:, :], ACT.Copy).then_inc(ple_read, 1)

                def after_last():
                    take(0)

                def extra(d):
                    for p in {-2: (1,), -1: (2, 3), 0: (4,), 1: (5,), 2: (6,), 5: (7,)}.get(d, ()):
                        take(p)
                    if d == -1:
                        refill(pp0)
                    if d == 6:
                        refill(pp0 + 1)
                return after_last, extra

            def ple_gates(layer, o_hi):
                n0 = FIRST["ple_gate", layer]
                for d in range(DT):
                    n = n0 + d
                    act.wait_ge(slab_done, n + 1)
                    if d >= 2:
                        act.wait_ge(mixed_in, DT * layer + d - 1)
                    nc.scalar.activation(gate[:, d % 2, :], bank[n % RING][:, :],
                                         ACT.Sigmoid).then_inc(bank_read[n % RING], 1)
                    if d == DT - 1 and layer < DEPTH - 1:
                        warm(ACT.Silu)
                    refill(n)
                    if layer == 0:
                        act.wait_ge(mixed_in, DT * layer + d + 1)
                        nc.scalar.activation(tile(o_hi, d), tile(xf, d), ACT.Copy).then_inc(x_hi_ready, 1)

            for layer in range(DEPTH):
                x_hi, o_hi = (a_hi, b_hi) if layer == 0 else (b_hi, a_hi)
                ffn(layer, 0, o_hi)
                final_products(3 * layer, FIRST["down", layer, 0, 2], FIRST_HALF)
                normalise_halves(layer, 0, 1, x_hi, ACT.Exp if layer == 0 else ACT.Copy, FIRST["mix", layer] - 1)
                if layer == 0:
                    attention_mixer(o_hi)
                else:
                    conv_mixer(o_hi)
                final_products(3 * layer + 1, FIRST["mix_out", layer], FIRST_HALF)
                normalise_halves(layer, 1, 0, x_hi, ACT.Silu, FIRST["up", layer, 1, 0] - 1)
                ffn(layer, 1, o_hi)
                after_last, extra = ple_step(layer)
                final_products(3 * layer + 2, FIRST["down", layer, 1, 2], WHOLE)
                refill(FIRST["ple_proj", layer] - 1)
                after_last()
                normalise(layer, 2, 1, x_hi, ACT.Sigmoid, extra)
                ple_gates(layer, o_hi)

        @block.vector
        def _(dve):
            chain = [0]

            def link(ins):
                chain[0] += 1
                ins.then_inc(dve_chain, 1)
                dve.wait_ge(dve_chain, chain[0])

            def refill(n, i=0):
                m = n + RING
                if m < N_SLABS:
                    dve.wait_ge(hi_ready, m + 1 + RING * i)
                    nc.vector.tensor_tensor(w_lo[:, m % RING, :], raw[:, m % RING, :],
                                            w_hi[:, m % RING, :].bitcast(F32), ALU.subtract).then_inc(lo_ready, 1)

            for c, (k0, k1) in enumerate(PIECES):
                for j in range(HEAD):
                    if c < 2:
                        dve.wait_ge(head_hi, HEAD * c + j + 1)
                    else:
                        dve.wait_ge(hi_ready, j + 1)
                    part = slice(k0 * P, k1 * P)
                    nc.vector.tensor_tensor(w_lo[:, j, part], raw[:, j, part], w_hi[:, j, part].bitcast(F32),
                                            ALU.subtract).then_inc(head_lo if c < 2 else lo_ready, 1)
            refill(HEAD - RING)

            def up_pair(n, jj, split, o_hi, o_lo, k, i=0):
                refill(n, i)
                dve.wait_ge(bank_read[n % RING], uses(n) + 1 + i)
                dve.wait_ge(slab_done, n + 2 + RING * i)
                b = (n + 1) % RING
                nc.vector.tensor_tensor(inner[:, jj, :], gate[:, jj, :], bank[b][:, :],
                                        ALU.mult).then_inc(bank_read[b], 1)
                refill(n + 1, i)
                dve.wait_ge(h_hi_ready, split + 1 + 2 * i)
                nc.vector.tensor_tensor(tile(o_lo, k), inner[:, jj, :], tile(o_hi, k).bitcast(F32),
                                        ALU.subtract).then_inc(h_lo_ready, 1)

            def add_into(z, product, first, scale):
                if first:
                    return nc.vector.scalar_tensor_tensor(out=z, in0=z, scalar=scale, in1=product,
                                                          op0=ALU.mult, op1=ALU.add)
                return nc.vector.tensor_tensor(z, z, product, ALU.add)

            def add_product(n, z, first, scale, i=0):
                b = n % RING
                dve.wait_ge(slab_done, n + 1 + RING * i)
                add_into(z, bank[b][:, :], first, scale).then_inc(bank_read[b], 1)

            def angles():
                c1, c2, c3 = split_two_pi()
                dve.wait_ge(const_loaded, 16 * 8)
                ang, turns, high, low = temp[:, 0, :], temp[:, 1, :], square[:, 0, :], square[:, 1, :]
                link(nc.vector.tensor_copy(ang, q[:, 0:T].bitcast(I32)))
                link(nc.vector.tensor_scalar(ang, ang, inv_freq, None, ALU.mult))
                link(nc.vector.tensor_scalar(turns, ang, 1 / TWO_PI, None, ALU.mult))
                link(nc.vector.tensor_scalar(turns, turns, MAGIC, None, ALU.add))
                link(nc.vector.tensor_scalar(turns, turns, MAGIC, None, ALU.subtract))
                link(nc.vector.tensor_scalar(high, turns, MAGIC * 4096, None, ALU.add))
                link(nc.vector.tensor_scalar(high, high, MAGIC * 4096, None, ALU.subtract))
                link(nc.vector.tensor_tensor(low, turns, high, ALU.subtract))
                for part, c in ((high, c1), (low, c1), (high, c2), (low, c2), (turns, c3)):
                    link(nc.vector.scalar_tensor_tensor(out=ang, in0=part, scalar=-c, in1=ang,
                                                        op0=ALU.mult, op1=ALU.add))
                link(nc.vector.tensor_scalar(ang, ang, float(np.float32(3.1415925)), -float(np.float32(3.1415925)),
                                             ALU.min, ALU.max))
                link(nc.vector.scalar_tensor_tensor(out=turns, in0=ang, scalar=-1.0, in1=ang,
                                                    op0=ALU.mult, op1=ALU.max))
                nc.vector.tensor_scalar(turns, turns, -1.0, float(np.pi / 2), ALU.mult, ALU.add).then_inc(angle_ready, 1)

            def ffn(layer, half, o_hi, o_lo):
                for g, ft in enumerate(FT_GROUPS):
                    n, h = FIRST["up", layer, half, g], H_BEFORE[layer, half, g]
                    with dve.Fori(0, ft // 2) as i:
                        for jj in range(2):
                            up_pair(n + 2 * jj, jj, h + jj, o_hi, o_lo, 2 * i + jj, i)
                    if g < 2:
                        n = FIRST["down", layer, half, g]
                        with dve.Fori(0, DT // RING) as i:
                            for j in range(RING):
                                add_product(n + j, tile(xf, RING * i + j), g == 0, 2 * ALPHA, i)
                                refill(n + j, i)
                    if layer == 0 and half == 0 and g == 0:
                        angles()
                    if half == 1 and g == 0:
                        dve.wait_ge(p_hi_ready, layer + 1)
                        nc.vector.tensor_tensor(p_lo[:, :], p_raw, p_hi[:, :].bitcast(F32),
                                                ALU.subtract).then_inc(p_lo_ready, 1)

            def final_products(norm, n0, first, scale, part):
                for d in range(DT):
                    z = tile(xf, d)
                    if d == DT - 1 and part is FIRST_HALF:
                        dve.wait_ge(first_product, halved(norm // 3, norm % 3) + 1)
                        b = (n0 + d) % RING
                        add_into(z[:, 0:TH], bank[b][:, 0:TH], first, scale).then_inc(bank_read[b], 1)
                        dve.wait_ge(bank_read[b], uses(n0 + d) + 1)
                        dve.wait_ge(sums_ready, 12 * norm + 12)
                        nc.vector.tensor_tensor(sum_z[:, 0:TH], sum_z[:, 0:TH], z[:, 0:TH],
                                                ALU.add).then_inc(first_sums, 1)
                        dve.wait_ge(square_ready, DT * norm + d + 1)
                        nc.vector.tensor_tensor(sum_q[:, 0:TH], sum_q[:, 0:TH], square[:, 1, 0:TH],
                                                ALU.add).then_inc(first_sums, 1)
                        continue
                    add_product(n0 + d, z, first, scale)
                    if 1 <= d < DT - 1:
                        dve.wait_ge(bank_read[(n0 + d) % RING], uses(n0 + d) + 1)
                        nc.vector.tensor_tensor(sum_z[:, :], tile(xf, 0) if d == 1 else sum_z[:, :], z,
                                                ALU.add).then_inc(sums_ready, 1)
                        dve.wait_ge(square_ready, DT * norm + d + 1)
                        nc.vector.tensor_tensor(sum_q[:, :], square[:, 0, :] if d == 1 else sum_q[:, :],
                                                square[:, d % 2, :], ALU.add).then_inc(sums_ready, 1)
                    if d < (DT - 2 if part is FIRST_HALF else DT - 1):
                        refill(n0 + d)

            def columns_of(first_column, part):
                c = part_of(part, BLOCKS)
                return small[:, first_column + c.start:first_column + c.stop]

            def diagonal(which, col, part):
                dst = square[:, which, part_of(part)]
                blocks = BLOCKS if part is WHOLE else BLOCKS // 2
                nc.vector.tensor_tensor(
                    dst.rearrange("p (b t) -> p b t", b=blocks),
                    ident.unsqueeze(1).broadcast_to([P, blocks, P]),
                    col.unsqueeze(2).broadcast_to([P, blocks, P]),
                    ALU.mult).then_inc(diag_ready, 1)

            def variance(norm, part):
                c = CHAIN[norm] + (part or 0)
                mean, mean2, var = (columns_of(first, part) for first in (16, 0, 4))
                dve.wait_ge(mean_ready, c + 1)
                if part is SECOND_HALF:
                    dve.wait_ge(meansq_ready, c + 1)
                link(nc.vector.tensor_copy(mean, statistics_bank(0, part)))
                nc.vector.tensor_tensor(mean2, mean, mean, ALU.mult).then_inc(mean2_ready, 1)
                diagonal(0, mean, part)
                dve.wait_ge(mean2_ready, c + 1)
                dve.wait_ge(meansq_ready, c + 1)
                nc.vector.tensor_tensor(var, statistics_bank(1, part), mean2, ALU.subtract).then_inc(var_ready, 1)

            def inverse_deviation(norm, part):
                c = CHAIN[norm] + (part or 0)
                std, rstd = columns_of(8, part), columns_of(12, part)
                dve.wait_ge(std_ready, c + 1)
                link(nc.vector.reciprocal(rstd, std))
                diagonal(1, rstd, part)

            def norm_tile(norm, d, part, xf_signal, xf_count, signal):
                c = CHAIN[norm] + (part or 0)
                t = temp[:, d % 2, part_of(part)]
                if d == 0:
                    dve.wait_ge(spread_ready, 2 * c + 1)
                if d >= 2:
                    dve.wait_ge(xf_signal, xf_count + d - 1)
                link(nc.vector.tensor_tensor(t, tile_part(xf, d, part), spread_bank(0, part), ALU.subtract))
                if d == 0:
                    dve.wait_ge(spread_ready, 2 * c + 2)
                nc.vector.tensor_tensor(t, t, spread_bank(1, part), ALU.mult).then_inc(signal, 1)

            def normalise(layer, which, n7):
                norm = 3 * layer + which
                variance(norm, WHOLE)
                refill(n7)
                inverse_deviation(norm, WHOLE)
                for d in range(DT):
                    norm_tile(norm, d, WHOLE, xf_ready, norm * DT, normed_ready)
                    if d == 0:
                        refill(n7 + 1)
                refill(n7 + 2)

            def normalise_halves(layer, which, n7, first, scale):
                norm, hn = 3 * layer + which, halved(layer, which)
                variance(norm, FIRST_HALF)
                inverse_deviation(norm, FIRST_HALF)
                dve.wait_ge(slab_done, n7 + 1)
                add_into(tile(xf, DT - 1)[:, TH:T], bank[4][:, TH:T], first, scale).then_inc(second_read, 1)
                for d in range(DT):
                    norm_tile(norm, d, FIRST_HALF, first_xf, hn * DT, first_normed)
                    if d == 2:
                        variance(norm, SECOND_HALF)
                    if d == 4:
                        inverse_deviation(norm, SECOND_HALF)
                for d in range(DT):
                    norm_tile(norm, d, SECOND_HALF, xf_ready, norm * DT, normed_ready)
                dve.wait_ge(lo_ready, n7 + RING)
                refill(n7)

            def attention_mixer(o_hi, o_lo):
                m0, h0 = FIRST["mix", 0], H_BEFORE["mix", 0]

                def rotate(r, src):
                    b = bank[4 + r % 2]
                    if r < 3:
                        dve.wait_ge(bank_read[(m0 + r) % RING], uses(m0 + r) + 1)
                        in_phase = temp[:, 0, :]
                        link(nc.vector.tensor_tensor(in_phase, src, cos, ALU.mult))
                    else:
                        dve.wait_ge(in_phase_ready, r - 2)
                        in_phase = inner[:, r - 3, :]
                    dve.wait_ge(rot_done, r + 1)
                    link(nc.vector.tensor_tensor(temp[:, 1, :], b[:, :], sin, ALU.mult))
                    if r < QT:
                        nc.vector.tensor_tensor(src, in_phase, temp[:, 1, :], ALU.add).then_inc(rot_ready, 1)
                        dve.wait_ge(rot_ready, r + 1)
                    else:
                        for g in range(2):
                            rows = slice(g * HEAD_DIM, (g + 1) * HEAD_DIM)
                            nc.vector.tensor_tensor(kz[rows, g * T:(g + 1) * T], in_phase[rows, :],
                                                    temp[rows, 1, :], ALU.add).then_inc(rot_ready, 1)

                def mask_and_max(u):
                    par, j = u % 2, u % QT
                    lo = P if u < QT else 0
                    view = inner[:, par, :].rearrange("p (g k) -> p g k", g=2)[:, :, lo:]
                    src = bank[4 + par][:, :].rearrange("p (g k) -> p g k", g=2)[:, :, lo:]
                    dve.wait_ge(scores_done, u + 1)
                    nc.vector.scalar_tensor_tensor(
                        out=view, in0=src, scalar=-HEAD_DIM ** -0.5,
                        in1=mask[:, lo:2 * P].unsqueeze(1).broadcast_to([P, 2, 2 * P - lo]),
                        op0=ALU.mult, op1=ALU.add).then_inc(scores_read, 1)
                    dve.wait_ge(scores_read, u + 1)
                    link(nc.vector.tensor_reduce(sm[:, par, 0:2], view, AX.X, ALU.min))
                    ns = nsink[:, 2 * j:2 * j + 2]
                    link(nc.vector.tensor_tensor(sm[:, par, 2:4], sm[:, par, 0:2], ns, ALU.min))
                    nc.vector.tensor_tensor(sm[:, par, 4:6], sm[:, par, 2:4], ns, ALU.subtract).then_inc(max_ready, 1)

                def normalise_probs(u):
                    par = u % 2
                    lo = P if u < QT else 0
                    dve.wait_ge(exp_ready, u + 1)
                    link(nc.vector.tensor_tensor(sm[:, par, 10:12], sm[:, par, 6:8], sm[:, par, 8:10], ALU.add))
                    link(nc.vector.reciprocal(sm[:, par, 10:12], sm[:, par, 10:12]))
                    for g in range(2):
                        c = slice(g * 2 * P + lo, (g + 1) * 2 * P)
                        e = tile(probs, par)[:, c]
                        ins = nc.vector.tensor_scalar(e, e, sm[:, par, 10 + g:11 + g], None, ALU.mult)
                        if g == 0:
                            link(ins)
                    ins.then_inc(probs_ready, 1)

                def att_out(n):
                    dve.wait_ge(h_hi_ready, h0 + n + 1)
                    c = slice(n * P, (n + 1) * P)
                    hi = o_hi[:, 0:QT * T].rearrange("p (j t) -> p j t", j=QT)[:, :, c]
                    lo = o_lo[:, 0:QT * T].rearrange("p (j t) -> p j t", j=QT)[:, :, c]
                    nc.vector.tensor_tensor(lo, bank[7][:, :].rearrange("p (j t) -> p j t", j=QT),
                                            hi.bitcast(F32), ALU.subtract).then_inc(h_lo_ready, 1)

                link(nc.vector.tensor_scalar(nsink[:, :], nsink[:, :], -1.0, None, ALU.mult))
                dve.wait_ge(const_ready, 10)
                dve.wait_ge(table_ready, 2)
                for j in range(3):
                    refill(m0 + j)
                rotate(0, tile(q, 0))
                refill(m0 + 3)
                rotate(1, tile(q, 1))
                rotate(2, tile(q, 2))
                refill(m0 + 4)
                rotate(3, tile(q, 3))
                rotate(4, square[:, 0, :])

                def spatial(j):
                    for cp in range(2):
                        dve.wait_ge(spatial_done, 2 * j + cp + 1)
                        for g in range(2):
                            rows = slice(g * HEAD_DIM, (g + 1) * HEAD_DIM)
                            src = bank[4 + cp][rows, :].rearrange("p (c k) -> p c k", c=2)[:, :, g * P:(g + 1) * P]
                            dst = temp[rows, j % 2, cp * 2 * P:(cp + 1) * 2 * P].rearrange("p (c k) -> p c k", c=2)
                            bias = spatial_bias[rows, j * P:(j + 1) * P].unsqueeze(1).broadcast_to([HEAD_DIM, 2, P])
                            nc.vector.tensor_tensor(dst, src, bias, ALU.add).then_inc(spatial_read, 1)
                    dve.wait_ge(spatial_read, 4 * j + 4)
                    dve.wait_ge(gelu_u, j + 1)
                    nc.vector.tensor_tensor(inner[:, j % 2, :], temp[:, j % 2, :], tile(u_act, j),
                                            ALU.mult).then_inc(sgu_ready, 1)

                def spatial_low(j):
                    dve.wait_ge(h_hi_ready, h0 + BLOCKS + j + 1)
                    nc.vector.tensor_tensor(tile(o_lo, QT + j), inner[:, j % 2, :], tile(o_hi, QT + j).bitcast(F32),
                                            ALU.subtract).then_inc(h_lo_ready, 1)

                for w in range(STEPS):
                    if w == 5:
                        dve.wait_ge(gelu_v, 1)
                        for tb in range(BLOCKS):
                            if tb > 0:
                                b = (m0 + 6 + tb) % RING
                                dve.wait_ge(bank_read[b], uses(m0 + 6 + tb) + 1)
                            link(nc.vector.bn_stats(stats6[:, tb, :], tile(v_act, tb)))
                            ins = nc.vector.bn_aggr(stats2[:, tb, :], stats6[:, tb, :])
                            if tb < BLOCKS - 1:
                                link(ins)
                        ins.then_inc(v_var, 1)
                    if w == 6:
                        dve.wait_ge(v_std, 1)
                        link(nc.vector.reciprocal(sgu_rstd[:, :], sgu_std[:, :]))
                        for tb in range(BLOCKS):
                            v = tile(v_act, tb)
                            nc.vector.tensor_scalar(v, v, stats2[:, tb, 0:1], sgu_rstd[:, tb:tb + 1],
                                                    ALU.subtract, ALU.mult).then_inc(v_scaled, 1)
                    if w < UNITS // 2:
                        mask_and_max(2 * w)
                        mask_and_max(2 * w + 1)
                        normalise_probs(2 * w)
                        normalise_probs(2 * w + 1)
                    if w >= 3 and w % 2 == 1:
                        att_out((w - 3) // 2)
                    if w < 9:
                        refill(m0 + 5 + w)
                    if w == UNITS // 2:
                        spatial(0)
                spatial(1)
                for j in range(4):
                    spatial_low(j)
                    if j + 2 < 4:
                        spatial(j + 2)

            def conv_mixer(o_hi, o_lo):
                m0, h0 = FIRST["mix", 1], H_BEFORE["mix", 1]
                for s in range(2):
                    link(nc.vector.memset(zpad[:, s * (T + 2):s * (T + 2) + 2], 0.0))
                base = chain[0]
                with dve.Fori(0, DT // 2) as i:
                    for jj in range(2):
                        n = m0 + 2 * jj
                        b = (n + 1) % RING
                        refill(n, i)
                        dve.wait_ge(bank_read[n % RING], uses(n) + 1 + i)
                        dve.wait_ge(slab_done, n + 2 + RING * i)
                        z0 = jj * (T + 2)
                        nc.vector.tensor_tensor(zpad[:, z0 + 2:z0 + 2 + T], gate[:, jj, :], bank[b][:, :],
                                                ALU.mult).then_inc(bank_read[b], 1)
                        refill(n + 1, i)
                        dve.wait_ge(bank_read[b], uses(n + 1) + 1 + i)
                        k = 2 * i + jj
                        y = tile(conv_y, k)
                        done = base + 4 * jj + 1 + 8 * i
                        nc.vector.tensor_copy(taps[:, jj, :], conv_taps[:, bass.ds(k * 3, 3)]).then_inc(dve_chain, 1)
                        dve.wait_ge(dve_chain, done)
                        for tap in range(3):
                            z = zpad[:, z0 + tap:z0 + tap + T]
                            wt = taps[:, jj, tap:tap + 1]
                            if tap == 0:
                                ins = nc.vector.tensor_scalar(y, z, wt, None, ALU.mult)
                            else:
                                ins = nc.vector.scalar_tensor_tensor(out=y, in0=z, scalar=wt, in1=y,
                                                                     op0=ALU.mult, op1=ALU.add)
                            ins.then_inc(dve_chain, 1)
                            dve.wait_ge(dve_chain, done + tap + 1)
                chain[0] += 4 * DT
                n = m0 + 2 * DT
                with dve.Fori(0, DT // RING) as i:
                    for j in range(RING):
                        b = (n + j) % RING
                        k = RING * i + j
                        dve.wait_ge(slab_done, n + j + 1 + RING * i)
                        nc.vector.tensor_tensor(inner[:, j % 2, :], tile(conv_y, k), bank[b][:, :],
                                                ALU.mult).then_inc(bank_read[b], 1)
                        refill(n + j, i)
                        dve.wait_ge(h_hi_ready, h0 + j + 1 + RING * i)
                        nc.vector.tensor_tensor(tile(o_lo, k), inner[:, j % 2, :], tile(o_hi, k).bitcast(F32),
                                                ALU.subtract).then_inc(h_lo_ready, 1)

            def ple_gates(layer):
                n0 = FIRST["ple_gate", layer]
                for d in range(DT):
                    n = n0 + d
                    dve.wait_ge(bank_read[n % RING], uses(n) + 1)
                    if d == 0:
                        dve.wait_ge(ple_read, DT * (layer + 1))
                    link(nc.vector.tensor_tensor(temp[:, d % 2, :], tile(ple, d), gate[:, d % 2, :], ALU.mult))
                    nc.vector.tensor_tensor(tile(xf, d), tile(xf, d), temp[:, d % 2, :],
                                            ALU.add).then_inc(mixed_in, 1)
                    refill(n)

            for layer in range(DEPTH):
                o_hi, o_lo = (b_hi, b_lo) if layer == 0 else (a_hi, a_lo)
                ffn(layer, 0, o_hi, o_lo)
                final_products(3 * layer, FIRST["down", layer, 0, 2], False, None, FIRST_HALF)
                normalise_halves(layer, 0, FIRST["mix", layer] - 1, False, None)
                if layer == 0:
                    attention_mixer(o_hi, o_lo)
                else:
                    conv_mixer(o_hi, o_lo)
                final_products(3 * layer + 1, FIRST["mix_out", layer], True, ALPHA, FIRST_HALF)
                normalise_halves(layer, 1, FIRST["up", layer, 1, 0] - 1, True, ALPHA)
                ffn(layer, 1, o_hi, o_lo)
                final_products(3 * layer + 2, FIRST["down", layer, 1, 2], False, None, WHOLE)
                normalise(layer, 2, FIRST["ple_proj", layer] - 1)
                ple_gates(layer)

        @block.tensor
        def _(pe):
            X_SPLIT, H_SPLIT = (x_hi_ready, x_lo_ready), (h_hi_ready, h_lo_ready)

            def three_passes(out, slot, c, x_hi, x_lo, start, stop):
                nc.tensor.matmul(out, w_hi[:, slot, c], x_hi, start=start, stop=False)
                nc.tensor.matmul(out, w_hi[:, slot, c], x_lo, start=False, stop=False)
                return nc.tensor.matmul(out, w_lo[:, slot, c], x_hi, start=False, stop=stop)

            def wait_slab(n, i=0):
                pe.wait_ge(lo_ready, n + 1 + RING * i)
                if uses(n) > 0:
                    pe.wait_ge(bank_read[n % RING], uses(n) + i)

            def slab(n, hi, lo, tiles=DT, i=0, ready=None, midway=None):
                wait_slab(n, i)
                for k in range(tiles):
                    if midway is not None and k == tiles - 2:
                        midway()
                    if ready is not None:
                        pe.wait_ge(h_lo_ready, ready(k))
                    last = three_passes(bank[n % RING][:, :], n % RING, slice(k * P, (k + 1) * P),
                                        tile(hi, k), tile(lo, k), k == 0, k == tiles - 1)
                last.then_inc(slab_done, 1)

            def slabs_by_tile(n, signals, ready, hi, lo, hooks={}, part=WHOLE):
                cols = part_of(part)
                for k in range(DT + 1):
                    if n == 0 and k == PIECES[1][0]:
                        pe.wait_ge(head_lo, 2 * HEAD)
                    if n == 0 and k == PIECES[2][0]:
                        pe.wait_ge(lo_ready, HEAD)
                    if k in hooks:
                        hooks[k]()
                    if k < DT:
                        pe.wait_ge(signals[0], ready(k))
                        for m in range(n, n + HEAD):
                            if n == 0 and k == 0:
                                pe.wait_ge(head_lo, m + 1)
                            if n > 0 and k == 0 and part is not SECOND_HALF:
                                wait_slab(m)
                            s, c = m % RING, slice(k * P, (k + 1) * P)
                            out, x_hi = bank[s][:, cols], tile_part(hi, k, part)
                            nc.tensor.matmul(out, w_hi[:, s, c], x_hi, start=(k == 0), stop=False)
                            nc.tensor.matmul(out, w_lo[:, s, c], x_hi, start=False, stop=False)
                    if k > 0:
                        pe.wait_ge(signals[1], ready(k - 1))
                        for m in range(n, n + HEAD):
                            s, c = m % RING, slice((k - 1) * P, k * P)
                            last = nc.tensor.matmul(bank[s][:, cols], w_hi[:, s, c], tile_part(lo, k - 1, part),
                                                    start=False, stop=(k == DT))
                            if k == DT and part is not FIRST_HALF:
                                last.then_inc(slab_done, 1)

            def slabs_by_half(layer, which, n, hi, lo):
                norm, refresh = 3 * layer + which, X_OF[layer, which]
                m = n + HEAD

                def filler(weights, x_part, part, k, start=False, stop=False):
                    return nc.tensor.matmul(bank[m % RING][:, part_of(part)], weights[:, m % RING, k * P:(k + 1) * P],
                                            tile_part(x_part, k, part), start=start, stop=stop)

                def step(k):
                    if k == 1:
                        half_sums(norm, 1, SECOND_HALF)
                    if k == 4:
                        spread(norm, 0, SECOND_HALF)
                    if k == 6:
                        spread(norm, 1, SECOND_HALF)
                    if k == 1:
                        pe.wait_ge(hi_ready, m + 1)
                        pe.wait_ge(bank_read[m % RING], uses(m))
                    if k > 0:
                        filler(w_hi, hi, FIRST_HALF, k - 1, start=(k == 1))
                    if k > 1:
                        filler(w_hi, lo, FIRST_HALF, k - 2)

                slabs_by_tile(n, (first_hi, first_lo), lambda k: DT * halved(layer, which) + k + 1, hi, lo,
                              {k: (lambda k=k: step(k)) for k in range(1, DT + 1)}, FIRST_HALF)
                filler(w_hi, lo, FIRST_HALF, DT - 1)
                slabs_by_tile(n, X_SPLIT, lambda k: DT * refresh + k + 1, hi, lo, {}, SECOND_HALF)
                pe.wait_ge(lo_ready, m + 1)
                for k in range(DT):
                    filler(w_lo, hi, FIRST_HALF, k, stop=(k == DT - 1))
                for k in range(DT):
                    filler(w_hi, hi, SECOND_HALF, k, start=(k == 0))
                    filler(w_hi, lo, SECOND_HALF, k)
                    last = filler(w_lo, hi, SECOND_HALF, k, stop=(k == DT - 1))
                last.then_inc(slab_done, 1)

            def ffn(layer, half, refresh, x, o):
                for g, ft in enumerate(FT_GROUPS):
                    n, h = FIRST["up", layer, half, g], H_BEFORE[layer, half, g]
                    steps = ft // 2
                    if g == 0:
                        if half == 0:
                            slabs_by_tile(n, X_SPLIT, lambda k: DT * refresh + k + 1, *x)
                            slab(n + HEAD, *x)
                        else:
                            slabs_by_half(layer, 1, n, *x)
                        n += RING
                        steps -= 1
                    with pe.Fori(0, steps) as i:
                        for j in range(RING):
                            slab(n + j, *x, i=i)
                    n = FIRST["down", layer, half, g]
                    if g == len(FT_GROUPS) - 1:
                        final_slabs(3 * layer + 2 * half, n, *o, ft, lambda k: h + k + 1,
                                    FIRST_HALF if half == 0 else WHOLE)
                        continue
                    with pe.Fori(0, DT // RING) as i:
                        for j in range(RING):
                            slab(n + j, *o, tiles=ft, i=i, ready=(lambda k: h + k + 1) if j == 0 else None)

            def add_statistics(src, which, part, start, stop):
                cols = part_of(part)
                for tb in range((cols.stop - cols.start) // P):
                    c = cols.start + tb * P
                    last = nc.tensor.matmul(statistics_bank(which, part)[:, tb:tb + 1], src[:, c:c + P],
                                            mean_col[:, 0:1], start=start and tb == 0, stop=stop,
                                            skip_group_check=True)
                return last

            def add_sums(norm):
                pe.wait_ge(const_ready, 5)
                pe.wait_ge(sums_ready, 12 * norm + 12)
                add_statistics(sum_z[:, :], 0, WHOLE, True, False)
                add_statistics(sum_q[:, :], 1, WHOLE, True, False)

            def finish_sums(norm, n7):
                pe.wait_ge(bank_read[n7 % RING], uses(n7) + 1)
                add_statistics(tile(xf, DT - 1), 0, WHOLE, False, True).then_inc(mean_ready, 1)
                pe.wait_ge(square_ready, DT * (norm + 1))
                add_statistics(square[:, 1, :], 1, WHOLE, False, True).then_inc(meansq_ready, 1)

            def half_sums(norm, which, part):
                pe.wait_ge(const_ready, 5)
                pe.wait_ge(first_sums if part == FIRST_HALF else second_sums,
                           2 * halved(norm // 3, norm % 3) + which + 1)
                add_statistics((sum_z, sum_q)[which][:, :], which, part, True,
                               True).then_inc((mean_ready, meansq_ready)[which], 1)

            def spread(norm, which, part=WHOLE):
                pe.wait_ge(diag_ready, 2 * (CHAIN[norm] + (part or 0)) + which + 1)
                nc.tensor.matmul(spread_bank(which, part), ones[:, :], square[:, which, part_of(part)],
                                 start=True, stop=True).then_inc(spread_ready, 1)

            def keep_warm(count, n):
                pe.wait_ge(bank_read[n % RING], uses(n) + 1)
                for _ in range(count):
                    nc.tensor.matmul(bank[n % RING][:, :], warm_rhs[:, 0:P], warm_rhs[:, :], start=True, stop=True)

            def last_slab(norm, n7, hi, lo, tiles=DT):
                slab(n7, hi, lo, tiles=tiles, midway=lambda: add_sums(norm))

            def last_slab_halves(norm, n7, hi, lo, tiles=DT):
                wait_slab(n7)
                hooks = {(1, 4): lambda: half_sums(norm, 0, FIRST_HALF),
                         (1, 5): lambda: half_sums(norm, 1, FIRST_HALF)}
                if tiles == DT:
                    hooks[1, tiles - 1] = lambda: spread(norm, 0, FIRST_HALF)
                for part, b in ((FIRST_HALF, n7 % RING), (SECOND_HALF, 4)):
                    for k in range(tiles):
                        if (part, k) in hooks:
                            hooks[part, k]()
                        last = three_passes(bank[b][:, part_of(part)], n7 % RING, slice(k * P, (k + 1) * P),
                                            tile_part(hi, k, part), tile_part(lo, k, part), k == 0, k == tiles - 1)
                    last.then_inc(first_product if part == FIRST_HALF else slab_done, 1)
                if tiles < DT:
                    spread(norm, 0, FIRST_HALF)
                keep_warm(1, n7 - 1)
                spread(norm, 1, FIRST_HALF)
                keep_warm(1, n7 - 1)
                half_sums(norm, 0, SECOND_HALF)

            def final_slabs(norm, n, hi, lo, tiles, ready, part):
                for j in range(DT - 1):
                    slab(n + j, hi, lo, tiles=tiles, ready=ready if j == 0 else None)
                (last_slab if part is WHOLE else last_slab_halves)(norm, n + DT - 1, hi, lo, tiles)

            def attention_mixer(x, o):
                m0, h0 = FIRST["mix", 0], H_BEFORE["mix", 0]
                vz4 = vz.rearrange("p (g n c) -> p g n c", g=2, n=BLOCKS)

                def rotate(r):
                    n = m0 + r
                    pe.wait_ge(bank_read[n % RING], uses(n) + 1)
                    if r >= 2:
                        pe.wait_ge(rot_ready, r - 1)
                    src = tile(q, r) if r < QT else square[:, 0, :]
                    nc.tensor.matmul(bank[4 + r % 2][:, :], rotT, src, start=True, stop=True).then_inc(rot_done, 1)

                def turn_v():
                    pe.wait_ge(bank_read[(m0 + 5) % RING], uses(m0 + 5) + 1)
                    for n in range(BLOCKS):
                        last = nc.tensor.transpose(bank[6][:, n * P:(n + 1) * P], gate[:, 0, n * P:(n + 1) * P], ident)
                    last.then_inc(v_turned, 1)

                def sgu_v_slab(r):
                    n = m0 + 6 + r
                    if r == 0:
                        for tb in range(BLOCKS):
                            pe.wait_ge(bank_read[(n + tb) % RING], uses(n + tb))
                    pe.wait_ge(lo_ready, n + 1)
                    for kk in range(2):
                        k = 2 * r + kk
                        whi = w_hi[:, n % RING, kk * T:(kk + 1) * T]
                        wlo = w_lo[:, n % RING, kk * T:(kk + 1) * T]
                        for tb in range(BLOCKS):
                            out = bank[(m0 + 6 + tb) % RING][:, :]
                            c = slice(k * T + tb * P, k * T + (tb + 1) * P)
                            nc.tensor.matmul(out, x[0][:, c], whi, start=(k == 0), stop=False)
                            nc.tensor.matmul(out, x[0][:, c], wlo, start=False, stop=False)
                            last = nc.tensor.matmul(out, x[1][:, c], whi, start=False, stop=(k == DT - 1))
                    last.then_inc(slab_done, 1)

                def scores(u):
                    n, j = u // QT, u % QT
                    if u == 0:
                        pe.wait_ge(rot_ready, QT + 2)
                    if u >= 2:
                        pe.wait_ge(scores_read, u - 1)
                    for g in range(2):
                        k0, k1 = max(n - 1, 0) * P, (n + 1) * P
                        out = bank[4 + u % 2][:, (g + 1) * 2 * P - (k1 - k0):(g + 1) * 2 * P]
                        last = nc.tensor.matmul(out, q[:, j * T + n * P:j * T + (n + 1) * P],
                                                kz[:, g * T + k0:g * T + k1], start=True, stop=True)
                    last.then_inc(scores_done, 1)

                def turn_probs(u):
                    pe.wait_ge(probs_ready, u + 1)
                    if u > 0:
                        pe.wait_ge(probsT_ready, u)
                    else:
                        pe.wait_ge(vz_ready, 2)
                    e = tile(probs, u % 2)
                    for g in range(2):
                        for kb in range(1 if u < QT else 0, 2):
                            c = slice((2 * g + kb) * P, (2 * g + kb + 1) * P)
                            last = nc.tensor.transpose(bank[6][:, c], e[:, c], ident)
                    last.then_inc(turned, 1)

                def weighted_values(u):
                    n, j = u // QT, u % QT
                    pe.wait_ge(probsT_ready, u + 1)
                    if j == 0 and n > 0:
                        pe.wait_ge(h_lo_ready, h0 + n)
                    parts = [(g, kb) for g in range(2) for kb in range(1 if n == 0 else 0, 2)]
                    for g, kb in parts:
                        c = slice((2 * g + kb) * P, (2 * g + kb + 1) * P)
                        last = nc.tensor.matmul(bank[7][:, j * P:(j + 1) * P], vz4[:, g, n - 1 + kb, :],
                                                tile(probsT, u % 2)[:, c], start=(g, kb) == parts[0],
                                                stop=(g, kb) == parts[-1])
                    last.then_inc(pv_done, 1)

                slabs_by_half(0, 0, m0, *x)
                rotate(0)
                rotate(1)
                slab(m0 + 4, *x)
                rotate(2)
                rotate(3)

                def spatial_product(j):
                    for cp in range(2):
                        if j > 0:
                            pe.wait_ge(spatial_read, 4 * (j - 1) + 2 * cp + 2)
                        for cc in range(2):
                            c = 2 * cp + cc
                            last = nc.tensor.matmul(bank[4 + cp][:, cc * 2 * P:(cc + 1) * 2 * P],
                                                    v_act[:, c * T + j * P:c * T + (j + 1) * P],
                                                    spatial[:, 2 * j * P:(2 * j + 2) * P], start=True, stop=True)
                        last.then_inc(spatial_done, 1)

                for w in range(STEPS):
                    if 1 <= w < 5:
                        sgu_v_slab(w - 1)
                    elif w < 9:
                        slab(m0 + 5 + w, *x, midway=(lambda: rotate(QT)) if w == 0 else None)
                    if w == 0:
                        turn_v()
                    for u in (2 * w, 2 * w + 1):
                        if u < UNITS:
                            scores(u)
                        if 2 <= u < UNITS + 2:
                            turn_probs(u - 2)
                        if u >= 4:
                            weighted_values(u - 4)
                    if w == UNITS // 2:
                        pe.wait_ge(v_normed, BLOCKS)
                        pe.wait_ge(scores_read, UNITS)
                        spatial_product(0)
                spatial_product(1)
                n = FIRST["mix_out", 0]
                slabs_by_tile(n, H_SPLIT, lambda k: h0 + BLOCKS + max(0, k - QT + 1), *o,
                              {2: lambda: spatial_product(2), QT: lambda: spatial_product(3)})
                for d in range(3, DT - 1):
                    slab(n + d, *o)
                last_slab_halves(1, n + DT - 1, *o)

            def conv_mixer(x, o):
                n, h0 = FIRST["mix", 1], H_BEFORE["mix", 1]
                slabs_by_half(1, 0, n, *x)
                with pe.Fori(0, (3 * DT - RING) // RING) as i:
                    for j in range(RING):
                        slab(n + RING + j, *x, i=i)
                n = FIRST["mix_out", 1]
                final_slabs(4, n, *o, DT, lambda k: h0 + k + 1, FIRST_HALF)

            def ple_products(layer, half_slab, p):
                n = FIRST["ple_proj", layer] + half_slab
                c = 4 * half_slab + p
                if p == 0:
                    pe.wait_ge(lo_ready, n + 1)
                    pe.wait_ge(p_lo_ready, layer + 1)
                done = DT * layer + c
                if done >= 2:
                    pe.wait_ge(ple_read, done - 1)
                for k in range(PLE_T):
                    last = three_passes(bank[4 + c % 2][:, :], n % RING,
                                        slice((2 * p + k) * P, (2 * p + k + 1) * P), tile(p_hi, k), tile(p_lo, k), k == 0, k == PLE_T - 1)
                last.then_inc(slab_done if p == 3 else ple_done, 1)

            for layer in range(DEPTH):
                a, b = ((a_hi, a_lo), (b_hi, b_lo)) if layer == 0 else ((b_hi, b_lo), (a_hi, a_lo))
                ffn(layer, 0, 0 if layer == 0 else X_OF["ple"], a, b)
                (attention_mixer if layer == 0 else conv_mixer)(a, b)
                ffn(layer, 1, None, a, b)
                norm = 3 * layer + 2
                ple_products(layer, 0, 0)
                finish_sums(norm, FIRST["ple_proj", layer] - 1)
                ple_products(layer, 0, 1)
                spread(norm, 0)
                ple_products(layer, 0, 2)
                spread(norm, 1)
                ple_products(layer, 0, 3)
                ple_products(layer, 1, 0)
                ple_products(layer, 1, 1)
                n = FIRST["ple_gate", layer]
                slabs_by_tile(n, X_SPLIT, lambda k: DT * X_OF[layer, 2] + k + 1, *a,
                              {1: lambda: ple_products(layer, 1, 2), 4: lambda: ple_products(layer, 1, 3)})
                for d in range(3, DT):
                    slab(n + d, *a)


def constants():
    c = np.zeros((P, 2 * P + 2), np.float32)
    c[:, 0:P] = np.eye(P)
    inv = np.power(np.float32(ROPE_THETA), -np.arange(ROT_HALF, dtype=np.float32) * np.float32(2.0 / (2 * ROT_HALF)))
    for base in (0, HEAD_DIM):
        for d in range(ROT_HALF):
            c[base + d + ROT_HALF, P + base + d] = -1.0
            c[base + d, P + base + d + ROT_HALF] = 1.0
            c[base + d, 2 * P] = c[base + d + ROT_HALF, 2 * P] = inv[d]
    return c


def kernel(x, p, positions, ln_g, ln_b, ffn_w_gate, ffn_w_up, ffn_w_down, ab_w_in, ab_sinks, sgu_ln_g,
           sgu_ln_b, sgu_w_s, sgu_b_s, ab_w_out, sc_w_in, sc_conv_w, sc_w_out, ple_w_proj, ple_w_gate):
    import concourse.bacc as bacc
    from concourse.bass_utils import run_bass_kernel_spmd

    def slabs(w):
        w = np.asarray(w)
        k, m = w.shape
        return w.reshape(k // P, P, m // P, P).transpose(2, 1, 0, 3).reshape(m // P, P, k)

    def feature_major(a):
        a = np.asarray(a)
        return np.ascontiguousarray(a.T.reshape(-1, P, a.shape[0]).transpose(1, 0, 2))

    wg, wu, wd = np.asarray(ffn_w_gate), np.asarray(ffn_w_up), np.asarray(ffn_w_down)
    w_up, w_down8, w_down6 = [], [], []
    for layer in range(DEPTH):
        for half in range(2):
            w_up.append(np.stack([slabs(wg[layer, half]), slabs(wu[layer, half])], 1).reshape(2 * FT, P, D))
            rows = wd[layer, half]
            w_down8 += [slabs(rows[0:8 * P]), slabs(rows[8 * P:16 * P])]
            w_down6.append(slabs(rows[16 * P:]))

    w_in = np.asarray(ab_w_in)[0]
    q_cols = w_in[:, 0:512].reshape(D, 2, QT, HEAD_DIM).transpose(0, 2, 1, 3).reshape(D, 512)
    k_cols, v_cols, su, sv = w_in[:, 512:640], w_in[:, 640:768], w_in[:, 768:1280], w_in[:, 1280:1792]
    sv_slabs = sv.reshape(4, 2, P, 512).transpose(0, 2, 1, 3).reshape(4, P, D)
    w_out = np.asarray(ab_w_out)[0]
    att_rows = w_out[0:512].reshape(2, QT, HEAD_DIM, D).transpose(1, 0, 2, 3).reshape(512, D)
    w_mix0 = np.concatenate([slabs(q_cols), slabs(k_cols), slabs(v_cols), sv_slabs, slabs(su),
                             slabs(np.concatenate([att_rows, w_out[512:]], 0))], 0)
    sc = np.asarray(sc_w_in)[0]
    w_mix1 = np.concatenate([
        np.stack([slabs(sc[:, D:2 * D]), slabs(sc[:, 2 * D:])], 1).reshape(2 * DT, P, D),
        slabs(sc[:, 0:D]), slabs(np.asarray(sc_w_out)[0])], 0)
    w_ple = np.concatenate([np.concatenate([
        slabs(np.asarray(ple_w_proj)[i]).reshape(2, 4, P, 256).transpose(0, 2, 1, 3).reshape(2, P, D),
        slabs(np.asarray(ple_w_gate)[i])], 0) for i in range(DEPTH)], 0)

    def columns(a):
        return np.asarray(a).reshape(3 * DEPTH, DT, P).transpose(2, 0, 1).reshape(P, 3 * DEPTH * DT)

    arrays = {
        "xT": feature_major(np.asarray(x)[0]),
        "pT": np.stack([feature_major(np.asarray(p)[i, 0]).reshape(P, PLE_T * T) for i in range(DEPTH)]),
        "positions": np.asarray(positions).reshape(1, T),
        "ln_gb": np.concatenate([columns(ln_g), columns(ln_b)], 1),
        "w_up": np.concatenate(w_up, 0),
        "w_down8": np.concatenate(w_down8, 0),
        "w_down6": np.concatenate(w_down6, 0),
        "w_mix0": w_mix0,
        "w_mix1": w_mix1,
        "w_ple": w_ple,
        "sinks": np.asarray(ab_sinks)[0].reshape(2, QT).T.reshape(1, HEADS),
        "sgu_gb": np.concatenate([np.asarray(sgu_ln_g)[0], np.asarray(sgu_ln_b)[0]]).reshape(1, 2 * T),
        "sgu_wT": np.asarray(sgu_w_s)[0].transpose(2, 0, 1).reshape(P, 8 * P),
        "sgu_b": np.repeat(np.asarray(sgu_b_s)[0].reshape(4, 2, 1, P), HEAD_DIM, 2).reshape(4, P, P)
                   .transpose(1, 0, 2).reshape(P, 4 * P),
        "conv_w": np.asarray(sc_conv_w)[0].reshape(3, DT, P).transpose(2, 1, 0).reshape(P, 3 * DT),
        "consts": constants(),
    }
    nc = bacc.Bacc("TRN2", target_bir_lowering=False, num_devices=1, dynamic_dma_scratch_size=1024)
    args, feed = [], {}
    for name, a in arrays.items():
        a = np.ascontiguousarray(a)
        feed[name] = a
        args.append(nc.dram_tensor(name, a.shape, mybir.dt.from_np(a.dtype), kind="ExternalInput").ap())
    args.append(nc.dram_tensor("outT", (P, DT, T), F32, kind="ExternalOutput").ap())
    build_program(nc, *args)
    got = run_bass_kernel_spmd(nc, [feed], core_ids=[0]).results[0]["outT"]
    return got.transpose(1, 0, 2).reshape(D, T).T.reshape(1, T, D)
```
